# Optimizing a Trainium2 kernel written in Bass

```python
import numpy as np
import jax
import jax.numpy as jnp
from jax import lax

D_MODEL = 1024
BATCH = 1
SEQ = 256
DEPTH = 2

PLE_DIM = 256
HEAD_DIM = 64
N_HEADS_A = 8
N_HEADS_B = 8
N_KV_B = 2
GQA_REP = N_HEADS_B // N_KV_B
N_HEADS_TOTAL = N_HEADS_A + N_HEADS_B
D_MIX = N_HEADS_TOTAL * HEAD_DIM
DILATED_PATTERNS = ((128, 1), (512, 4), (2048, 16))
Q_BLOCK_A = 128
CMP_BLOCK = 32
CMP_STRIDE = 16
CMP_HIDDEN = 256
SEL_BLOCK = 64
SEL_TOP = 16
N_LOCAL_BLOCKS = 2
WINDOW = 512
Q_BLOCK_B = 64
N_GROUPS = 4
EXPERTS_PER_GROUP = 4
N_EXPERTS = N_GROUPS * EXPERTS_PER_GROUP
D_EXPERT = 512
TOP_K_IN_GROUP = 2
RMS_EPS = 1e-6
NEG = -1e30
FORCE_BONUS = 1e4
A_W = N_HEADS_A * HEAD_DIM
B_Q = N_HEADS_B * HEAD_DIM
B_KV = N_KV_B * HEAD_DIM
B_GATE = N_HEADS_B * 3
SPLITS = (A_W, A_W, A_W, B_Q, B_KV, B_KV, B_KV, B_KV, B_KV, B_KV, B_GATE)
N_IN = sum(SPLITS)

kernel_name = "hybrid_dilated_nsa_hmoe_block"

def rms_norm(x, g):
    xf = x.astype(jnp.float32)
    y = xf * lax.rsqrt(jnp.mean(xf * xf, axis=-1, keepdims=True) + RMS_EPS)
    return (y * g.astype(jnp.float32)).astype(x.dtype)

def alibi_slopes():
    s = 2.0 ** (-8.0 * np.arange(1, N_HEADS_TOTAL + 1) / N_HEADS_TOTAL)
    return jnp.asarray(s[0::2], jnp.float32), jnp.asarray(s[1::2].reshape(N_KV_B, GQA_REP), jnp.float32)

def dilated_attention(q, k, v, slopes):
    B, H, S, dh = q.shape
    scale = dh ** -0.5
    m = slopes[None, :, None, None]

    def block(t0):
        qb = lax.dynamic_slice_in_dim(q, t0, Q_BLOCK_A, axis=2)
        t = t0 + jnp.arange(Q_BLOCK_A)
        nums, dens, maxs = [], [], []
        for window, dil in DILATED_PATTERNS:
            dist = jnp.arange(window // dil + 1) * dil
            pos = t[:, None] - dist[None, :]
            valid = pos >= 0
            posc = jnp.maximum(pos, 0)
            kg = k[:, :, posc]
            vg = v[:, :, posc]
            s = jnp.einsum('bhqd,bhqjd->bhqj', qb, kg).astype(jnp.float32) * scale - m * dist.astype(jnp.float32)
            s = jnp.where(valid, s, NEG)
            mx = jnp.max(s, axis=-1, keepdims=True)
            e = jnp.exp(s - mx)
            dens.append(jnp.sum(e, axis=-1, keepdims=True))
            nums.append(jnp.einsum('bhqj,bhqjd->bhqd', e.astype(v.dtype), vg).astype(jnp.float32))
            maxs.append(mx)
        M = maxs[0]
        for mx in maxs[1:]:
            M = jnp.maximum(M, mx)
        ws = [jnp.exp(mx - M) for mx in maxs]
        num = sum(w * n for w, n in zip(ws, nums))
        den = sum(w * d for w, d in zip(ws, dens))
        return (num / den).astype(q.dtype)

    outs = lax.map(block, jnp.arange(S // Q_BLOCK_A) * Q_BLOCK_A)
    return jnp.moveaxis(outs, 0, 2).reshape(B, H, S, dh)

def nsa_attention(q, k_c, v_c, k_s, v_s, k_w, v_w, gates, m, w_ck1, w_ck2, w_cv1, w_cv2, cmp_pos):
    B, G, R, S, dh = q.shape
    scale = dh ** -0.5
    t = jnp.arange(S)
    n_cmp = (S - CMP_BLOCK) // CMP_STRIDE + 1
    cidx = np.arange(n_cmp)[:, None] * CMP_STRIDE + np.arange(CMP_BLOCK)[None, :]

    def compress(kv, pos, w1, w2):
        blk = (kv[:, :, cidx] + pos).reshape(B, G, n_cmp, CMP_BLOCK * dh)
        return jax.nn.gelu(blk @ w1) @ w2

    k_cmp = compress(k_c, cmp_pos[0], w_ck1, w_ck2)
    v_cmp = compress(v_c, cmp_pos[1], w_cv1, w_cv2)
    cmp_end = jnp.asarray(cidx[:, -1])
    dist_c = (t[:, None] - cmp_end[None, :]).astype(jnp.float32)
    valid_c = dist_c >= 0
    s = jnp.einsum('bgrqd,bgcd->bgrqc', q, k_cmp).astype(jnp.float32) * scale - m * dist_c
    p_cmp = jax.nn.softmax(jnp.where(valid_c, s, NEG), axis=-1) * valid_c
    o_cmp = jnp.einsum('bgrqc,bgcd->bgrqd', p_cmp.astype(v_cmp.dtype), v_cmp)

    nb = S // SEL_BLOCK
    cs = cidx[:, 0]
    bs = np.arange(nb) * SEL_BLOCK
    ov = np.clip(np.minimum(cs[:, None] + CMP_BLOCK, bs[None, :] + SEL_BLOCK) - np.maximum(cs[:, None], bs[None, :]), 0, None) / CMP_BLOCK
    ov = jnp.asarray(ov, jnp.float32)
    imp = jnp.einsum('bgrqc,cn->bgqn', p_cmp, ov)
    back = (t // SEL_BLOCK)[:, None] - jnp.arange(nb)[None, :]
    valid_s = back >= 0
    forced = (jnp.arange(nb)[None, :] == 0) | (valid_s & (back < N_LOCAL_BLOCKS))
    score = jnp.where(valid_s, imp + jnp.where(forced, FORCE_BONUS, 0.0), NEG)
    n_top = min(SEL_TOP, nb)
    top_val, top_idx = lax.top_k(score, n_top)
    top_ok = top_val > 0.5 * NEG

    kb = k_s.reshape(B, G, nb, SEL_BLOCK, dh)
    vb = v_s.reshape(B, G, nb, SEL_BLOCK, dh)
    kw_pad = jnp.pad(k_w, ((0, 0), (0, 0), (WINDOW, 0), (0, 0)))
    vw_pad = jnp.pad(v_w, ((0, 0), (0, 0), (WINDOW, 0), (0, 0)))
    bi = jnp.arange(B)[:, None, None, None]
    gi = jnp.arange(G)[None, :, None, None]
    n_keys = n_top * SEL_BLOCK

    def block(t0):
        qb = lax.dynamic_slice_in_dim(q, t0, Q_BLOCK_B, axis=3)
        tq = t0 + jnp.arange(Q_BLOCK_B)
        idx = lax.dynamic_slice_in_dim(top_idx, t0, Q_BLOCK_B, axis=2)
        ok = lax.dynamic_slice_in_dim(top_ok, t0, Q_BLOCK_B, axis=2)
        ks = kb[bi, gi, idx].reshape(B, G, Q_BLOCK_B, n_keys, dh)
        vs = vb[bi, gi, idx].reshape(B, G, Q_BLOCK_B, n_keys, dh)
        spos = (idx[..., None] * SEL_BLOCK + jnp.arange(SEL_BLOCK)).reshape(B, G, Q_BLOCK_B, n_keys)
        dist = (tq[:, None] - spos).astype(jnp.float32)
        okk = jnp.broadcast_to(ok[..., None], ok.shape + (SEL_BLOCK,)).reshape(B, G, Q_BLOCK_B, n_keys) & (dist >= 0)
        s = jnp.einsum('bgrqd,bgqkd->bgrqk', qb, ks).astype(jnp.float32) * scale - m * dist[:, :, None]
        p = jax.nn.softmax(jnp.where(okk[:, :, None], s, NEG), axis=-1)
        o_s = jnp.einsum('bgrqk,bgqkd->bgrqd', p.astype(vs.dtype), vs)
        kw = lax.dynamic_slice_in_dim(kw_pad, t0, WINDOW + Q_BLOCK_B, axis=2)
        vw = lax.dynamic_slice_in_dim(vw_pad, t0, WINDOW + Q_BLOCK_B, axis=2)
        wpos = t0 - WINDOW + jnp.arange(WINDOW + Q_BLOCK_B)
        wdist = tq[:, None] - wpos[None, :]
        wok = (wdist >= 0) & (wdist < WINDOW) & (wpos[None, :] >= 0)
        s = jnp.einsum('bgrqd,bgkd->bgrqk', qb, kw).astype(jnp.float32) * scale - m * wdist.astype(jnp.float32)
        p = jax.nn.softmax(jnp.where(wok, s, NEG), axis=-1)
        o_w = jnp.einsum('bgrqk,bgkd->bgrqd', p.astype(vw.dtype), vw)
        return o_s, o_w

    o_s, o_w = lax.map(block, jnp.arange(S // Q_BLOCK_B) * Q_BLOCK_B)
    unblock = lambda o: jnp.moveaxis(o, 0, 3).reshape(B, G, R, S, dh)
    g = gates.astype(q.dtype)
    return g[..., 0:1] * o_cmp + g[..., 1:2] * unblock(o_s) + g[..., 2:3] * unblock(o_w)

def mixing_layer(h, w_in, w_out, w_ck1, w_ck2, w_cv1, w_cv2, cmp_pos):
    B, S, _ = h.shape
    proj = h @ w_in
    qa, ka, va, qb, kc, vc, ks, vs, kw, vw, gl = jnp.split(proj, list(np.cumsum(SPLITS)[:-1]), axis=-1)
    heads = lambda z, n: z.reshape(B, S, n, HEAD_DIM).transpose(0, 2, 1, 3)
    slopes_a, slopes_b = alibi_slopes()
    oa = dilated_attention(heads(qa, N_HEADS_A), heads(ka, N_HEADS_A), heads(va, N_HEADS_A), slopes_a)
    qB = heads(qb, N_HEADS_B).reshape(B, N_KV_B, GQA_REP, S, HEAD_DIM)
    gates = jax.nn.sigmoid(gl.astype(jnp.float32)).reshape(B, S, N_KV_B, GQA_REP, 3).transpose(0, 2, 3, 1, 4)
    ob = nsa_attention(qB, heads(kc, N_KV_B), heads(vc, N_KV_B), heads(ks, N_KV_B), heads(vs, N_KV_B),
                       heads(kw, N_KV_B), heads(vw, N_KV_B), gates, slopes_b[None, :, :, None, None],
                       w_ck1, w_ck2, w_cv1, w_cv2, cmp_pos)
    ob = ob.reshape(B, N_HEADS_B, S, HEAD_DIM)
    o = jnp.concatenate([oa, ob], axis=1).transpose(0, 2, 1, 3).reshape(B, S, D_MIX)
    return o @ w_out

def hierarchical_moe(h, w_rg, b_rg, w_re, b_re, w_gate, w_up, w_down):
    B, S, D = h.shape
    tok = h.reshape(-1, D)
    glog = (tok @ w_rg).astype(jnp.float32) + b_rg.astype(jnp.float32)
    gprob = jax.nn.softmax(glog, axis=-1)
    gsel = jnp.argmax(glog, axis=-1)
    gw = jnp.take_along_axis(gprob, gsel[:, None], axis=-1)
    elog = ((tok @ w_re).astype(jnp.float32) + b_re.astype(jnp.float32)).reshape(-1, N_GROUPS, EXPERTS_PER_GROUP)
    within = jnp.take_along_axis(elog, gsel[:, None, None], axis=1)[:, 0]
    tv, ti = lax.top_k(within, TOP_K_IN_GROUP)
    ew = jax.nn.softmax(tv, axis=-1) * gw
    local = jnp.sum(jax.nn.one_hot(ti, EXPERTS_PER_GROUP, dtype=jnp.float32) * ew[..., None], axis=1)
    y = jnp.zeros_like(tok)
    for g in range(N_GROUPS):
        gate_g = jnp.where((gsel == g)[:, None], local, 0.0).astype(tok.dtype)
        sl = slice(g * EXPERTS_PER_GROUP, (g + 1) * EXPERTS_PER_GROUP)
        a = jax.nn.silu(jnp.einsum('td,edh->teh', tok, w_gate[sl])) * jnp.einsum('td,edh->teh', tok, w_up[sl])
        y = y + jnp.einsum('teh,ehd->td', a * gate_g[..., None], w_down[sl])
    return y.reshape(B, S, D)

def setup_inputs(seed: int = 0) -> dict:
    key = jax.random.key(seed)
    ks = jax.random.split(key, 22)
    f32 = jnp.float32
    nrm = lambda k, shape, fan_in: jax.random.normal(k, shape, f32) * fan_in ** -0.5
    gain = lambda k, shape: 1.0 + 0.02 * jax.random.normal(k, shape, f32)
    return {
        "x": jax.random.normal(ks[0], (BATCH, SEQ, D_MODEL), f32),
        "p": jax.random.normal(ks[1], (DEPTH, BATCH, SEQ, PLE_DIM), f32),
        "attn_norm": gain(ks[2], (DEPTH, D_MODEL)),
        "w_in": nrm(ks[3], (DEPTH, D_MODEL, N_IN), D_MODEL),
        "w_out": nrm(ks[4], (DEPTH, D_MIX, D_MODEL), D_MIX),
        "w_cmp_k1": nrm(ks[5], (DEPTH, CMP_BLOCK * HEAD_DIM, CMP_HIDDEN), CMP_BLOCK * HEAD_DIM),
        "w_cmp_k2": nrm(ks[6], (DEPTH, CMP_HIDDEN, HEAD_DIM), CMP_HIDDEN),
        "w_cmp_v1": nrm(ks[7], (DEPTH, CMP_BLOCK * HEAD_DIM, CMP_HIDDEN), CMP_BLOCK * HEAD_DIM),
        "w_cmp_v2": nrm(ks[8], (DEPTH, CMP_HIDDEN, HEAD_DIM), CMP_HIDDEN),
        "cmp_pos": 0.02 * jax.random.normal(ks[9], (DEPTH, 2, CMP_BLOCK, HEAD_DIM), f32),
        "ffn_norm": gain(ks[10], (DEPTH, D_MODEL)),
        "w_route_group": nrm(ks[11], (DEPTH, D_MODEL, N_GROUPS), D_MODEL),
        "b_route_group": 0.01 * jax.random.normal(ks[12], (DEPTH, N_GROUPS), f32),
        "w_route_expert": nrm(ks[13], (DEPTH, D_MODEL, N_EXPERTS), D_MODEL),
        "b_route_expert": 0.01 * jax.random.normal(ks[14], (DEPTH, N_EXPERTS), f32),
        "w_expert_gate": nrm(ks[15], (DEPTH, N_EXPERTS, D_MODEL, D_EXPERT), D_MODEL),
        "w_expert_up": nrm(ks[16], (DEPTH, N_EXPERTS, D_MODEL, D_EXPERT), D_MODEL),
        "w_expert_down": nrm(ks[17], (DEPTH, N_EXPERTS, D_EXPERT, D_MODEL), D_EXPERT),
        "ple_norm": gain(ks[18], (DEPTH, D_MODEL)),
        "w_ple_gate": nrm(ks[19], (DEPTH, D_MODEL, D_MODEL), D_MODEL),
        "w_ple_proj": nrm(ks[20], (DEPTH, PLE_DIM, D_MODEL), PLE_DIM),
        "final_norm": gain(ks[21], (D_MODEL,)),
    }

def reference(x, p, attn_norm, w_in, w_out, w_cmp_k1, w_cmp_k2, w_cmp_v1, w_cmp_v2, cmp_pos,
              ffn_norm, w_route_group, b_route_group, w_route_expert, b_route_expert,
              w_expert_gate, w_expert_up, w_expert_down, ple_norm, w_ple_gate, w_ple_proj, final_norm):
    for i in range(DEPTH):
        h = rms_norm(x, attn_norm[i])
        x = x + mixing_layer(h, w_in[i], w_out[i], w_cmp_k1[i], w_cmp_k2[i], w_cmp_v1[i], w_cmp_v2[i], cmp_pos[i])
        h = rms_norm(x, ffn_norm[i])
        x = x + hierarchical_moe(h, w_route_group[i], b_route_group[i], w_route_expert[i], b_route_expert[i],
                                 w_expert_gate[i], w_expert_up[i], w_expert_down[i])
        gate = jax.nn.sigmoid(rms_norm(x, ple_norm[i]) @ w_ple_gate[i])
        x = x + gate * (p[i] @ w_ple_proj[i])
    return rms_norm(x, final_norm)


_drawn_inputs = setup_inputs


def setup_inputs(seed=0):
    import zlib

    import numpy as np

    out = dict(_drawn_inputs(seed))
    spreads = {}
    factors = {'cmp_pos': 4.191,
     'b_route_group': 4.126,
     'b_route_expert': 5.626,
     'ple_norm': 23.866,
     'final_norm': 7.496}
    for name, (base, spread) in spreads.items():
        noise = np.random.default_rng([zlib.crc32(name.encode()), seed]).standard_normal(out[name].shape)
        drawn = base * np.exp(spread * noise) if base else spread * noise
        out[name] = jnp.asarray(drawn.astype(out[name].dtype))
    for name, factor in factors.items():
        out[name] = (out[name] * factor).astype(out[name].dtype)
    return out
```

```python
import math
from contextlib import ExitStack

import numpy as np

import concourse.bass as bass
from concourse import mybir

F32 = mybir.dt.float32
I32 = mybir.dt.int32
ALU = mybir.AluOpType
ACT = mybir.ActivationFunctionType
AX = mybir.AxisListType

P = 128
DEPTH, SEQ, D = 2, 256, 1024
TT = SEQ // P
KT = D // P
HD = 64
HA, HB, KVB = 8, 8, 2
REP = HB // KVB
PLE = 256
NG, EPG, DE = 4, 4, 512
FT = DE // P
NR = NG + NG * EPG
CBLK, CSTR, CHID = 32, 16, 256
NC = (SEQ - CBLK) // CSTR + 1
CPAD = 32
CAP = 96
EPS = 1e-6
HUGE = 1e30
GELU_C = math.sqrt(2.0 / math.pi)

QA, KA, VA, QB = 0, 512, 1024, 1536
KC = 2048
KW = KC + 512
N_IN = KW + 2 * P + 3 * HB

HEADS_TURN = 1

RING = 6
SLOT = 4096
ATT_PIECES = 10
GROUP_PIECES = 3 * EPG
PIECES = ATT_PIECES + NG * GROUP_PIECES + 2
ROUNDS = PIECES // RING
assert PIECES % RING == 0 and GROUP_PIECES % RING == 0
P_KCV, P_QB, P_KVW, P_CK1, P_CV1, P_KA, P_QA, P_VA, P_WO0, P_WO1 = range(ATT_PIECES)
G_ORDER = [("gate", 0), ("up", 0), ("gate", 1), ("up", 1), ("down", 0), ("gate", 2), ("up", 2),
           ("down", 1), ("gate", 3), ("up", 3), ("down", 2), ("down", 3)]
P_PG = PIECES - 2

SM_GAIN = 0
SM_POS = SM_GAIN + 3 * KT
SM_W2 = SM_POS + 2 * (CBLK // 2)
SM_ROUT = SM_W2 + 2 * 2 * HD
SM_RB = SM_ROUT + KT * NR
SM_PT = SM_RB + NR
SM = SM_PT + 2 * SEQ
C_DIST = 0
C_MA = C_DIST + SEQ
C_MB = C_MA + SEQ
C_CC = C_MB + SEQ
C_CV = C_CC + TT * HB * NC
C_ID = C_CV + TT * NC
C_LT = C_ID + P
C_ONE = C_LT + P
C_IOTA = C_ONE + P
C_TIE = C_IOTA + CAP
C_POW = C_TIE + 4
CN = C_POW + TT


def slopes():
    n = HA + HB
    s = [2.0 ** (-8.0 * (i + 1) / n) for i in range(n)]
    return s[0::2], s[1::2]


def tables():
    c = np.zeros((P, CN), np.float64)
    q = np.arange(P)[:, None]
    dist = P + q - np.arange(SEQ)[None, :]
    past = dist >= 0
    count = ((dist <= 128).astype(int) + (dist % 4 == 0) + (dist % 16 == 0)) * past
    c[:, C_DIST:C_DIST + SEQ] = np.where(past, dist, 0)
    c[:, C_MA:C_MA + SEQ] = np.where(count > 0, -np.log(np.maximum(count, 1)), HUGE)
    c[:, C_MB:C_MB + SEQ] = np.where(past, 0.0, HUGE)
    end = np.arange(NC) * CSTR + CBLK - 1
    _, mb = slopes()
    for t in range(TT):
        dc = (t * P + q) - end[None, :]
        for h in range(HB):
            at = C_CC + (((h % 2) * TT + t) * (HB // 2) + h // 2) * NC
            c[:, at:at + NC] = np.where(dc >= 0, mb[h] * dc, HUGE)
        c[:, C_CV + t * NC:C_CV + (t + 1) * NC] = dc >= 0
    c[:, C_ID:C_ID + P] = np.eye(P)
    c[:, C_LT:C_LT + P] = q < np.arange(P)[None, :]
    c[:, C_ONE:C_ONE + P] = 1.0
    c[:, C_IOTA:C_IOTA + CAP] = np.arange(CAP)
    c[:, C_TIE:C_TIE + 4] = [4, 3, 2, 1]
    c[:, C_POW:C_POW + TT] = -0.5
    return c.astype(np.float32)


class Chain:

    def __init__(self, eng, sem, n=0, base=0):
        self.eng, self.sem, self.n, self.base = eng, sem, n, base

    def add(self, ins):
        self.n += 1
        ins.then_inc(self.sem, 1)

    def wait(self):
        self.eng.wait_ge(self.sem, self.base + self.n)


def build_trunk(nc, x_in, small_in, table_in, fgain_in, w_in, w_out, w_ck1, w_cv1,
                w_eg, w_eu, w_ed, w_pg, w_pp, out):
    ctx = ExitStack()
    with ctx:
        def sb(name, shape, dt=F32):
            return ctx.enter_context(nc.sbuf_tensor(name, shape, dt))

        ring = sb("ring", [P, RING, SLOT])
        x = sb("x", [P, TT, D])
        xn = sb("xn", [P, TT, D])
        hT = sb("hT", [P, KT, SEQ])
        tab = sb("tab", [P, CN])
        small = sb("small", [P, SM])
        fgain = sb("fgain", [P, D])
        cost_a = sb("cost_a", [P, HA, SEQ])
        cost_b = sb("cost_b", [P, HB, SEQ])
        pc = sb("pc", [P, TT, HB, CPAD])
        vbd = sb("vbd", [P, KVB, REP * HD])
        sq = sb("sq", [P, TT])
        xn_flat = xn[:].rearrange("p t d -> p (t d)")
        rstd = sb("rstd", [P, TT])
        work = sb("work", [P, 13700])

        ps = ctx.enter_context(nc.psum_tensor("ps", [P, 8, 512], F32))

        cut = [0]

        def take(n):
            cut[0] += n
            assert cut[0] <= 13700, cut[0]
            return work[:, cut[0] - n:cut[0]]

        qbT = take(4 * SEQ).rearrange("p (i n) -> p i n", i=4)
        qaT = take(4 * SEQ).rearrange("p (i n) -> p i n", i=4)
        kaT = take(4 * SEQ).rearrange("p (i n) -> p i n", i=4)
        kbT = take(KVB * 2 * SEQ).rearrange("p (g w n) -> p g w n", g=KVB, w=2)
        va = take(TT * 512).rearrange("p (t n) -> p t n", t=TT)
        vb = take(TT * 2 * P).rearrange("p (w t n) -> p w t n", w=2, t=TT)
        gate = take(TT * 3 * HB).rearrange("p (t n) -> p t n", t=TT)
        cost = take(2 * 3 * P).rearrange("p (b n) -> p b n", b=2)
        pr = take(3 * 3 * P).rearrange("p (b n) -> p b n", b=3)
        prT = take(3 * 3 * P).rearrange("p (b n) -> p b n", b=3)
        low = take(24 * TT).rearrange("p (j t) -> p j t", t=TT)
        den = take(24 * TT).rearrange("p (j t) -> p j t", t=TT)
        wgt = take(24 * TT).rearrange("p (j t) -> p j t", t=TT)
        part = take(2 * 512).rearrange("p (b n) -> p b n", b=2)
        NJ = CBLK // 2
        blk = take(2 * NJ * KVB * NC).rearrange("p (w j g c) -> p w j g c", w=2, j=NJ, g=KVB)
        NH = 2 * 2 * KVB * NC
        hid = take(NH)
        hid_u = take(NH)
        hid_g = take(NH).rearrange("p (w m n) -> p w m n", w=2, m=2)
        kcT = take(KVB * NC).rearrange("p (g c) -> p g c", g=KVB)
        cs = take(TT * HB * NC).rearrange("p (n c) -> p n c", c=NC)
        cz = take(TT * HB * NC).rearrange("p (n c) -> p n c", c=NC)
        clow = take(TT * HB)
        cden = take(TT * HB)
        cw = take(TT * HB)
        pcT = take(TT * KVB * P).rearrange("p (n q) -> p n q", q=P)

        cut[0] = 0
        lg = take(TT * NR).rearrange("p (t n) -> p t n", t=TT)
        r_m = take(TT)
        r_e = take(TT * 4).rearrange("p (t n) -> p t n", t=TT)
        r_w = take(TT * 4).rearrange("p (t n) -> p t n", t=TT)
        r_wm = take(TT)
        onehot = take(TT * NG).rearrange("p (t n) -> p t n", t=TT)
        r_x = take(TT * 4).rearrange("p (t n) -> p t n", t=TT)
        gsum = take(TT)
        gw = take(TT)
        r_big = take(TT * NG * EPG)
        within = take(TT * EPG).rearrange("p (t n) -> p t n", t=TT)
        sel1 = take(TT * EPG).rearrange("p (t n) -> p t n", t=TT)
        sel2 = take(TT * EPG).rearrange("p (t n) -> p t n", t=TT)
        top1 = take(TT)
        top2 = take(TT)
        e2 = take(TT)
        w1 = take(TT)
        w2 = take(TT)
        local = take(TT * EPG).rearrange("p (t n) -> p t n", t=TT)
        local2 = take(TT * EPG).rearrange("p (t n) -> p t n", t=TT)
        slot_of = take(TT * (NG + 1)).rearrange("p (t n) -> p t n", t=TT)
        most = take(1)
        over_w = take(TT * NG * EPG).rearrange("p (t g e) -> p t g e", t=TT, g=NG)
        late = take(TT * NG).rearrange("p (t n) -> p t n", t=TT)
        pick = take(TT * CAP).rearrange("p (t n) -> p t n", t=TT)
        pickT = take(TT * P).rearrange("p (t n) -> p t n", t=TT)
        xg = take(KT * CAP).rearrange("p (k n) -> p k n", k=KT)
        gb = take(EPG * CAP).rearrange("p (e n) -> p e n", e=EPG)
        FN = FT * CAP
        over_from = cut[0]
        th = take(2 * FN).rearrange("p (b n) -> p b n", b=2)
        a1 = take(2 * FN).rearrange("p (b n) -> p b n", b=2)
        a2 = take(2 * FN).rearrange("p (b n) -> p b n", b=2)
        act_in = take(2 * FN).rearrange("p (b n) -> p b n", b=2)
        y = take(D)
        cut[0] = max(cut[0], over_from + 3 * D)
        over_wf = over_w.rearrange("p t g e -> p t (g e)")
        at = over_from
        ow_gate = work[:, at:at + KT * P].rearrange("p (k n) -> p k n", k=KT)
        ow_up = work[:, at + KT * P:at + 2 * KT * P].rearrange("p (k n) -> p k n", k=KT)
        ow_down = work[:, at + 2 * KT * P:at + 2 * KT * P + D]
        o_th, o_a1, o_a2 = (xn_flat[:, i * SEQ:(i + 1) * SEQ] for i in range(3))
        ple_w = take(2 * D).rearrange("p (k n) -> p k n", k=2)
        pth = take(2 * 512).rearrange("p (b n) -> p b n", b=2)
        pv = take(2 * 512).rearrange("p (b n) -> p b n", b=2)
        most_i = sb("most_i", [P, 1], I32)

        ident = tab[:, C_ID:C_ID + P]
        ones = tab[:, C_ONE:C_ONE + P]

        def gain(s, k0, n=1):
            return small[:, SM_GAIN + s * KT + k0:SM_GAIN + s * KT + k0 + n]

        pos2 = small[:, SM_POS:SM_POS + 2 * NJ].rearrange("p (w j) -> p w j", w=2)
        cw2 = small[:, SM_W2:SM_W2 + 4 * HD].rearrange("p (w m n) -> p w m n", w=2, m=2)
        rout = small[:, SM_ROUT:SM_ROUT + KT * NR].rearrange("p (k n) -> p k n", k=KT)
        pT = small[:, SM_PT:SM_PT + 2 * SEQ].rearrange("p (k n) -> p k n", k=2)

        def sem(name):
            return ctx.enter_context(nc.semaphore(name))

        slot_in = [sem(f"slot_in{i}") for i in range(RING)]
        piece_used = sem("piece_used")
        x_in_sem, table_sem, fgain_sem, out_sem = sem("x_in"), sem("table"), sem("fgain"), sem("out_s")
        setup_done = sem("setup_done")
        names = """small_in ple_in sq_act sq_dve ms_ready rstd_ready chain_dve xn_dve xn_act turned hT_act hT_dve kcv_out qb_out kb_out qa_out ka_out cmp_out va_out
            blk_ready kb_act vs_ready vw_ready gate_act gate_dve qb_dve qb_act gelu_x gelu_t gelu_done
            qk_act qk_dve kc_ready vc_ready va_act va_dve cscore cexp_in cexp cprob cturn cturned cout
            ocmp score costed expd turnedP prT_dve prT_act summed out_even part_added wo_out x_added
            routed rank_in ranked rexp_in rexp route_done picked misc6 misc7 free6 free7
            th_ready bank_free act_ready y_act y_dve
            ple_q ple_z ple_th ple_x over_ld over_g over_t over_a over_y over_x over_l""".split()
        s = {n: sem("l_" + n) for n in names}
        nums = [v.num for v in s.values()]
        assert nums == list(range(nums[0], nums[0] + len(nums)))

        def piece_src(l, i):
            cols = {P_KCV: (KC, 512), P_QB: (QB, 512), P_KVW: (KW, N_IN - KW), P_QA: (QA, 512),
                    P_KA: (KA, 512), P_VA: (VA, 512)}
            if i in cols:
                c, n = cols[i]
                return w_in[l, :, c:c + n].rearrange("(k p) n -> p k n", p=P), n
            if i in (P_CK1, P_CV1):
                return (w_ck1 if i == P_CK1 else w_cv1)[l].rearrange("(k p) n -> p k n", p=P), CHID
            if i in (P_WO0, P_WO1):
                h = i - P_WO0
                return w_out[l, :, h * 512:(h + 1) * 512].rearrange("(k p) n -> p k n", p=P), 512
            h = i - P_PG
            return w_pg[l, :, h * 512:(h + 1) * 512].rearrange("(k p) n -> p k n", p=P), 512

        def slot(i, n):
            k = SLOT // n
            return ring[:, i % RING, 0:k * n].rearrange("p (k n) -> p k n", n=n)

        def slot8(i, n=512):
            return ring[:, i % RING, 0:KT * n].rearrange("p (k n) -> p k n", n=n)

        def load_piece(sp, l, i):
            src, n = piece_src(l, i)
            dst = ring[:, i % RING, 0:src.shape[1] * n].rearrange("p (k n) -> p k n", n=n)
            sp.dma_start(dst, src).then_inc(slot_in[i % RING], 16)

        sa, sbb = slopes()

        with nc.Block() as block:
            @block.sync
            def _(sp):
                sp.dma_start(x[:], x_in.rearrange("(t p) d -> p t d", p=P)).then_inc(x_in_sem, 16)
                for i in range(RING):
                    load_piece(sp, 0, i)

            @block.scalar
            def _(act):
                act.dma_start(tab[:], table_in).then_inc(table_sem, 16)
                act.dma_start(fgain[:], fgain_in).then_inc(fgain_sem, 16)
                act.wait_ge(fgain_sem, 16)

            @block.vector
            def _(dve):
                nc.vector.memset(pc[:], 0.0)
                nc.vector.memset(vbd[:], 0.0)
                dve.wait_ge(table_sem, 16)
                dist = tab[:, C_DIST:C_DIST + SEQ]
                for h in range(HA):
                    nc.vector.scalar_tensor_tensor(out=cost_a[:, h, :], in0=dist, scalar=sa[h],
                                                   in1=tab[:, C_MA:C_MA + SEQ], op0=ALU.mult, op1=ALU.add)
                for h in range(HB):
                    nc.vector.scalar_tensor_tensor(out=cost_b[:, h, :], in0=dist, scalar=sbb[h],
                                                   in1=tab[:, C_MB:C_MB + SEQ], op0=ALU.mult, op1=ALU.add)
                dve.wait_ge(x_in_sem, 16)

        HEADS = [("a", h) for h in range(HA)] + [("s", h) for h in range(HB)] + [("w", h) for h in range(HB)]
        NHD = len(HEADS)
        TRI = [(0, 0, 0), (1, 0, P), (1, 1, 2 * P)]

        def head_qk(j):
            kind, h = HEADS[j]
            lo = HD * (h % 2)
            if kind == "a":
                return qaT[lo:lo + HD, h // 2, :], kaT[lo:lo + HD, h // 2, :]
            return qbT[lo:lo + HD, h // 2, :], kbT[lo:lo + HD, h // REP, 0 if kind == "s" else 1, :]

        def head_v(j, t):
            kind, h = HEADS[j]
            if kind == "a":
                return va[:, t, h * HD:(h + 1) * HD]
            return vb[:, 0 if kind == "s" else 1, t, (h // REP) * HD:(h // REP + 1) * HD]

        with nc.Fori(0, DEPTH) as l:
            with nc.Block() as block:

                def used(eng, i, g=0):
                    eng.wait_ge(piece_used, PIECES * l + GROUP_PIECES * g + i + 1)

                @block.sync
                def _(sp):
                    def room(n):
                        sp.wait_ge(piece_used, PIECES * l + n + 1 - RING)

                    for i in range(RING, ATT_PIECES):
                        room(i)
                        load_piece(sp, l, i)
                    with sp.Fori(0, NG) as g:
                        for k, (kind, e) in enumerate(G_ORDER):
                            i = ATT_PIECES + k
                            sp.wait_ge(piece_used, PIECES * l + GROUP_PIECES * g + i + 1 - RING)
                            w = {"gate": w_eg, "up": w_eu, "down": w_ed}[kind]
                            n = D if kind == "down" else DE
                            sp.dma_start(slot(i, n), w[l, EPG * g + e].rearrange("(k p) n -> p k n", p=P)
                                         ).then_inc(slot_in[i % RING], 16)
                    for i in (P_PG, P_PG + 1):
                        room(i)
                        load_piece(sp, l, i)
                    with sp.If(l < DEPTH - 1):
                        for i in range(RING):
                            sp.wait_ge(piece_used, PIECES * l + PIECES + i + 1 - RING)
                            load_piece(sp, (l + 1) % DEPTH, i)

                @block.tensor
                def _(pe):
                    mm = nc.tensor.matmul

                    def arrived(i):
                        pe.wait_ge(slot_in[i % RING], 16 * ROUNDS * l + 16 * (i // RING + 1))

                    def turn(event, src):
                        for t in range(TT):
                            if event != HEADS_TURN:
                                pe.wait_ge(s["xn_act" if t else "xn_dve"], 1 if event == 0 else event)
                            for k in range(KT):
                                at = (k % 2) * SEQ + t * P
                                m = nc.tensor.transpose(ps[:, k // 2, at:at + P], src[:, t, k * P:(k + 1) * P], ident)
                                if t == TT - 1 and k % 2 == 1:
                                    m.then_inc(s["turned"], 1)

                    def turned_in(event):
                        pe.wait_ge(s["hT_act"], KT // 2 * (event + 1))
                        pe.wait_ge(s["hT_dve"], KT // 2 * (event + 1))

                    pe.wait_ge(s["small_in"], 16)
                    turn(0, xn)
                    turned_in(0)

                    def features(bank, c, w, col):
                        for k in range(KT):
                            m = mm(ps[:, bank, c:c + SEQ], w[:, k, col:col + P], hT[:, k, :],
                                   start=(k == 0), stop=(k == KT - 1))
                        return m

                    def tokens(bank, c, w, col, n, t):
                        for k in range(KT):
                            m = mm(ps[:, bank, c:c + n], hT[:, k, t * P:(t + 1) * P], w[:, k, col:col + n],
                                   start=(k == 0), stop=(k == KT - 1))
                        return m

                    arrived(P_KCV)
                    w = slot8(P_KCV)
                    features(4, 0, w, 0)
                    features(4, SEQ, w, P).then_inc(s["kcv_out"], 1)
                    features(5, 0, w, 2 * P)
                    tokens(6, 0, w, 3 * P, P, 0)
                    tokens(6, P, w, 3 * P, P, 1).then_inc(piece_used, 1)
                    arrived(P_QB)
                    w = slot8(P_QB)
                    for i in range(4):
                        m = features(i // 2, (i % 2) * SEQ, w, i * P)
                        if i == 1:
                            m.then_inc(s["qb_out"], 1)
                    m.then_inc(piece_used, 1)
                    arrived(P_KVW)
                    w = slot8(P_KVW, N_IN - KW)
                    features(5, SEQ, w, 0).then_inc(s["kb_out"], 1)
                    NV = P + 3 * HB
                    tokens(7, 0, w, P, NV, 0)
                    tokens(7, NV, w, P, NV, 1).then_inc(piece_used, 1)
                    pe.wait_ge(s["blk_ready"], 4)
                    for w_i, i in ((0, P_CK1), (1, P_CV1)):
                        arrived(i)
                        w = slot(i, CHID)
                        for mt in range(2):
                            c = (w_i * 2 + mt) * KVB * NC
                            for j in range(NJ):
                                m = mm(ps[:, 2, c:c + KVB * NC], w[:, j, mt * P:(mt + 1) * P],
                                       blk[:, w_i, j, :, :].rearrange("p g c -> p (g c)"),
                                       start=(j == 0), stop=(j == NJ - 1))
                        m.then_inc(piece_used, 1)
                    arrived(P_KA)
                    w = slot8(P_KA)
                    for i in range(4):
                        if i == 2:
                            pe.wait_ge(s["kb_act"], 4)
                        m = features(4 + i // 2, (i % 2) * SEQ, w, i * P)
                        if i == 1:
                            m.then_inc(s["ka_out"], 1)
                    m.then_inc(piece_used, 1)
                    arrived(P_QA)
                    w = slot8(P_QA)
                    for i in range(4):
                        if i == 0:
                            pe.wait_ge(s["vs_ready"], 1)
                        if i == 2:
                            pe.wait_ge(s["vw_ready"], 1)
                            pe.wait_ge(s["gate_act"], 1)
                        m = features(6 + i // 2, (i % 2) * SEQ, w, i * P)
                        if i == 1:
                            m.then_inc(s["qa_out"], 1)
                    m.then_inc(piece_used, 1)
                    pe.wait_ge(s["gelu_done"], 1)
                    for mt in range(2):
                        mm(ps[0:HD, 3, 0:KVB * NC], cw2[:, 0, mt, :], hid_g[:, 0, mt, :],
                           start=(mt == 0), stop=(mt == 1))
                    for g in range(KVB):
                        for mt in range(2):
                            m = mm(ps[0:NC, 3, HD + g * HD:2 * HD + g * HD], hid_g[:, 1, mt, g * NC:(g + 1) * NC],
                                   cw2[:, 1, mt, :], start=(mt == 0), stop=(mt == 1))
                    m.then_inc(s["cmp_out"], 1)
                    arrived(P_VA)
                    w = slot8(P_VA)
                    pe.wait_ge(s["qb_dve"], 1)
                    pe.wait_ge(s["qb_act"], 1)
                    tokens(0, 0, w, 0, 512, 0).then_inc(s["va_out"], 1)
                    tokens(1, 0, w, 0, 512, 1).then_inc(piece_used, 1)

                    pe.wait_ge(s["qk_act"], 2)
                    pe.wait_ge(s["qk_dve"], 2)
                    pe.wait_ge(s["kc_ready"], 2)
                    for t in range(TT):
                        for h in range(HB):
                            lo = HD * (h % 2)
                            at = (t * (HB // 2) + h // 2) * CPAD
                            m = mm(ps[:, 6 + h % 2, at:at + NC],
                                   qbT[lo:lo + HD, h // 2, t * P:(t + 1) * P], kcT[lo:lo + HD, h // REP, :],
                                   start=True, stop=True)
                    m.then_inc(s["cscore"], 1)

                    def scores(j):
                        q, k = head_qk(j)
                        if j >= 2:
                            pe.wait_ge(s["costed"], 2 * (j - 1))
                        b = 4 + j % 2
                        mm(ps[:, b, 0:P], q[:, 0:P], k[:, 0:P], start=True, stop=True)
                        mm(ps[:, b, P:3 * P], q[:, P:SEQ], k[:, :], start=True, stop=True).then_inc(s["score"], 1)

                    def turn_weights(j):
                        pe.wait_ge(s["expd"], 2 * (j + 1))
                        if j == 0:
                            pe.wait_ge(s["gelu_x"], 1)
                        if j == 1:
                            pe.wait_ge(s["vc_ready"], 8)
                        if j >= 2:
                            pe.wait_ge(s["prT_act" if j % 2 else "prT_dve"], j // 2)
                        for _, _, c in TRI:
                            m = nc.tensor.transpose(ps[:, 2 + j % 2, c:c + P], pr[:, j % 3, c:c + P], ident)
                        m.then_inc(s["turnedP"], 1)

                    def weigh(j):
                        pe.wait_ge(s["prT_act" if j % 2 else "prT_dve"], j // 2 + 1)
                        if j == 0:
                            pe.wait_ge(s["va_act"], 1)
                            pe.wait_ge(s["va_dve"], 1)
                        if j >= 8 and j % 4 == 0:
                            pe.wait_ge(s["out_even"], j // 4 - 1)
                        b = (j // 4) % 2
                        c = (j % 4) * TT * HD
                        mm(ps[:, b, c:c + HD], prT[:, j % 3, 0:P], head_v(j, 0), start=True, stop=True)
                        mm(ps[:, b, c + HD:c + 2 * HD], prT[:, j % 3, P:2 * P], head_v(j, 0), start=True, stop=False)
                        mm(ps[:, b, c + HD:c + 2 * HD], prT[:, j % 3, 2 * P:3 * P], head_v(j, 1),
                           start=False, stop=True).then_inc(s["summed"], 1)

                    for step in range(NHD + 2):
                        if step < NHD:
                            scores(step)
                        if 1 <= step <= NHD:
                            turn_weights(step - 1)
                        if step >= 2:
                            weigh(step - 2)
                        if step == 5:
                            pe.wait_ge(s["cprob"], 1)
                            for n in range(TT * KVB):
                                m = nc.tensor.transpose(ps[:, 7, n * P:(n + 1) * P],
                                                        pc[:, n // KVB, (n % KVB) * REP:(n % KVB + 1) * REP, :]
                                                        .rearrange("p h c -> p (h c)"), ident)
                            m.then_inc(s["cturn"], 1)
                        if step == 8:
                            pe.wait_ge(s["cturned"], 1)
                            for t in range(TT):
                                for g in range(KVB):
                                    m = mm(ps[:, 6 + t, g * REP * HD:(g + 1) * REP * HD], pcT[:, t * KVB + g, :],
                                           vbd[:, g, :], start=True, stop=True)
                            m.then_inc(s["cout"], 1)

                    pe.wait_ge(s["out_even"], NHD // 4)
                    pe.wait_ge(s["part_added"], 4)
                    turn(HEADS_TURN, xn)
                    turned_in(HEADS_TURN)
                    for half in range(2):
                        arrived(P_WO0 + half)
                        for t in range(TT):
                            tokens(4 + 2 * half + t, 0, slot8(P_WO0 + half), 0, 512, t
                                   ).then_inc(piece_used if t else s["wo_out"], 1)

                    turn(2, xn)
                    turned_in(2)
                    pe.wait_ge(s["x_added"], 4)
                    for t in range(TT):
                        for k in range(KT):
                            mm(ps[:, 4, t * NR:(t + 1) * NR], hT[:, k, t * P:(t + 1) * P], rout[:, k, :],
                               start=(k == 0), stop=False)
                        m = mm(ps[:, 4, t * NR:(t + 1) * NR], tab[0:1, C_ONE:C_ONE + P],
                               small[0:1, SM_RB:SM_RB + NR], start=False, stop=True)
                    m.then_inc(s["routed"], 1)
                    pe.wait_ge(s["rank_in"], 1)
                    lt = tab[:, C_LT:C_LT + P]
                    mm(ps[:, 5, 0:NG], lt, onehot[:, 0, :], start=True, stop=True)
                    mm(ps[:, 5, NG:2 * NG], ones, onehot[:, 0, :], start=True, stop=False)
                    mm(ps[:, 5, NG:2 * NG], lt, onehot[:, 1, :], start=False, stop=True)
                    mm(ps[:, 5, 2 * NG:3 * NG], ones, onehot[:, 0, :], start=True, stop=False)
                    mm(ps[:, 5, 2 * NG:3 * NG], ones, onehot[:, 1, :], start=False, stop=True).then_inc(s["ranked"], 1)

                    def gather(n6, n7):
                        for b in range(2):
                            pe.wait_ge(s["free6" if b == 0 else "free7"], n6 if b == 0 else n7)
                            for kk in range(4):
                                k = b * 4 + kk
                                for t in range(TT):
                                    m = mm(ps[:, 6 + b, kk * CAP:(kk + 1) * CAP], xn[:, t, k * P:(k + 1) * P],
                                           pick[:, t, :], start=(t == 0), stop=(t == 1))
                            m.then_inc(s["misc6" if b == 0 else "misc7"], 1)

                    def spread_gates(n6):
                        pe.wait_ge(s["free6"], n6)
                        for e in range(EPG):
                            for t in range(TT):
                                m = mm(ps[:, 6, e * CAP:(e + 1) * CAP],
                                       local2[:, t, e:e + 1].to_broadcast([P, P]),
                                       pick[:, t, :], start=(t == 0), stop=(t == 1))
                        m.then_inc(s["misc6"], 1)

                    def turn_pick(n7):
                        pe.wait_ge(s["free7"], n7)
                        for t in range(TT):
                            m = nc.tensor.transpose(ps[0:CAP, 7, t * P:(t + 1) * P], pick[:, t, :], ident)
                        m.then_inc(s["misc7"], 1)

                    pe.wait_ge(s["picked"], 1)
                    for b in range(2):
                        for kk in range(4):
                            k = b * 4 + kk
                            for t in range(TT):
                                m = mm(ps[:, 6 + b, kk * CAP:(kk + 1) * CAP], xn[:, t, k * P:(k + 1) * P],
                                       pick[:, t, :], start=(t == 0), stop=(t == 1))
                        m.then_inc(s["misc6" if b == 0 else "misc7"], 1)
                    spread_gates(1)
                    turn_pick(1)

                    with pe.Fori(0, NG) as g:
                        def got(k):
                            i = ATT_PIECES + k
                            pe.wait_ge(slot_in[i % RING], 16 * ROUNDS * l + 16 * (GROUP_PIECES // RING) * g
                                       + 16 * (i // RING + 1))
                            return i

                        def gate_up(e):
                            pe.wait_ge(s["bank_free"], EPG * g + e + 1)
                            for kind, b in (("gate", e % 2), ("up", 2 + e % 2)):
                                w = slot(got(G_ORDER.index((kind, e))), DE)
                                for f in range(FT):
                                    for k in range(KT):
                                        m = mm(ps[:, b, f * CAP:(f + 1) * CAP], w[:, k, f * P:(f + 1) * P],
                                               xg[:, k, :], start=(k == 0), stop=(k == KT - 1))
                                m.then_inc(piece_used, 1)

                        def down(e):
                            w = slot(got(G_ORDER.index(("down", e))), D)
                            pe.wait_ge(s["act_ready"], EPG * g + e + 1)
                            for f in range(FT):
                                for half in range(2):
                                    m = mm(ps[0:CAP, 4 + half, :], act_in[:, e % 2, f * CAP:(f + 1) * CAP],
                                           w[:, f, half * 512:(half + 1) * 512],
                                           start=(e == 0 and f == 0), stop=(e == EPG - 1 and f == FT - 1),
                                           skip_group_check=True)
                            m.then_inc(piece_used, 1)

                        pe.wait_ge(s["free6"], 4 * g + 1)
                        pe.wait_ge(s["free7"], 4 * g + 1)
                        gate_up(0)
                        gate_up(1)
                        down(0)
                        gate_up(2)
                        down(1)
                        gate_up(3)
                        down(2)
                        pe.wait_ge(s["picked"], g + 2)
                        gather(4 * g + 2, 4 * g + 2)
                        down(3)
                        spread_gates(4 * g + 3)
                        pe.wait_ge(s["y_act"], g + 1)
                        pe.wait_ge(s["y_dve"], g + 1)
                        for n in range(4):
                            t, half = n % 2, n // 2
                            b = 7 - n % 2
                            pe.wait_ge(s["free7" if b == 7 else "free6"], 4 * g + 3 + (n // 2) + (b == 6))
                            mm(ps[:, b, :], pickT[0:CAP, t, :], y[0:CAP, half * 512:(half + 1) * 512],
                               start=True, stop=True).then_inc(s["misc7" if b == 7 else "misc6"], 1)
                        turn_pick(4 * g + 5)

                    pe.wait_ge(s["route_done"], 1)
                    with pe.If(pe.value_load(most_i[0:1, 0:1], min_val=0, max_val=SEQ) > CAP):
                        with pe.Fori(0, NG * EPG) as e:
                            for f in range(FT):
                                pe.wait_ge(s["over_ld"], 48 * FT * e + 48 * (f + 1))
                                for b, w in ((0, ow_gate), (1, ow_up)):
                                    features(b, 0, w, 0).then_inc(s["over_g"], 1)
                                pe.wait_ge(s["over_a"], FT * e + f + 1)
                                for t in range(TT):
                                    for half in range(2):
                                        m = mm(ps[:, 2 + 2 * t + half, :], o_a2[:, t * P:(t + 1) * P],
                                               ow_down[:, half * 512:(half + 1) * 512], start=True, stop=True)
                                m.then_inc(s["over_y"], 1)
                        pe.wait_ge(s["over_x"], NG * EPG * FT + 1)
                    pe.wait_ge(s["ple_in"], 16)
                    pe.wait_ge(s["free6"], 4 * NG + 2)
                    pe.wait_ge(s["free7"], 4 * NG + 2)
                    for half in range(2):
                        for t in range(TT):
                            for k in range(2):
                                m = mm(ps[:, 4 + 2 * half + t, :], pT[:, k, t * P:(t + 1) * P],
                                       ple_w[:, k, half * 512:(half + 1) * 512], start=(k == 0), stop=(k == 1))
                            m.then_inc(s["ple_q"], 1)
                    turn(3, xn)
                    turned_in(3)
                    for half in range(2):
                        arrived(P_PG + half)
                        for t in range(TT):
                            tokens(2 * half + t, 0, slot8(P_PG + half), 0, 512, t
                                   ).then_inc(piece_used if t else s["ple_z"], 1)

                @block.scalar
                def _(act):
                    A = nc.scalar.activation

                    act.dma_start(small[:], small_in[l]).then_inc(s["small_in"], 16)
                    act.wait_ge(s["small_in"], 16)

                    def norm(n):
                        A(xn[:, 1, :], x[:, 1, :], ACT.Square, accum_out=sq[:, 1:2]).then_inc(s["sq_act"], 1)
                        act.wait_ge(s["rstd_ready"], n + 1)
                        A(xn[:, 1, :], x[:, 1, :], ACT.Copy, scale=rstd[:, 1:2]).then_inc(s["xn_act"], 1)

                    def evac_turned(event, g):
                        for b in (0, 2):
                            act.wait_ge(s["turned"], 4 * event + b + 1)
                            for k in (2 * b, 2 * b + 1):
                                A(hT[:, k, :], ps[:, b, (k % 2) * SEQ:(k % 2 + 1) * SEQ], ACT.Copy,
                                  scale=1.0 if g is None else gain(g, k)).then_inc(s["hT_act"], 1)

                    norm(0)
                    evac_turned(0, 0)
                    used(act, P_KCV)
                    A(vb[:, 0, :, :], ps[:, 6, 0:SEQ].rearrange("p (t n) -> p t n", t=TT), ACT.Copy
                      ).then_inc(s["vs_ready"], 1)
                    used(act, P_QB)
                    A(qbT[:, 2:4, :], ps[:, 1, :].rearrange("p (i n) -> p i n", i=2), ACT.Copy,
                      scale=-(HD ** -0.5)).then_inc(s["qb_act"], 1)
                    act.wait_ge(s["kb_out"], 1)
                    for g in range(KVB):
                        for lo in (0, HD):
                            A(kbT[lo:lo + HD, g, :, :],
                              ps[g * HD:(g + 1) * HD, 5, :].rearrange("p (w n) -> p w n", w=2),
                              ACT.Copy).then_inc(s["kb_act"], 1)
                    used(act, P_KVW)
                    NV = P + 3 * HB
                    A(gate[:], ps[:, 7, 0:2 * NV].rearrange("p (t n) -> p t n", t=TT)[:, :, P:NV], ACT.Tanh,
                      scale=0.5).then_inc(s["gate_act"], 1)
                    act.wait_ge(s["gelu_t"], 1)
                    A(hid_u, hid_u, ACT.Tanh, scale=GELU_C).then_inc(s["gelu_t"], 1)
                    act.wait_ge(s["ka_out"], 1)
                    A(kaT[:, 0:2, :], ps[:, 4, :].rearrange("p (i n) -> p i n", i=2), ACT.Copy
                      ).then_inc(s["qk_act"], 1)
                    act.wait_ge(s["qa_out"], 1)
                    A(qaT[:, 0:2, :], ps[:, 6, :].rearrange("p (i n) -> p i n", i=2), ACT.Copy,
                      scale=-(HD ** -0.5)).then_inc(s["qk_act"], 1)
                    act.wait_ge(s["cmp_out"], 1)
                    for lo in (0, HD):
                        A(kcT[lo:lo + HD, :, :], ps[0:HD, 3, 0:KVB * NC].rearrange("p (g c) -> p g c", g=KVB),
                          ACT.Copy).then_inc(s["kc_ready"], 1)
                    act.wait_ge(s["va_out"], 1)
                    A(va[:, 0, :], ps[:, 0, :], ACT.Copy).then_inc(s["va_act"], 1)

                    def weights(j):
                        for t in range(TT):
                            act.wait_ge(s["costed"], 2 * j + t + 1)
                            if j >= 3 and t == 0:
                                act.wait_ge(s["turnedP"], j - 2)
                            c, n = (0, P) if t == 0 else (P, SEQ)
                            A(pr[:, j % 3, c:c + n], cost[:, j % 2, c:c + n], ACT.Exp, scale=-1.0,
                              bias=low[:, j, t:t + 1], accum_out=den[:, j, t:t + 1]).then_inc(s["expd"], 1)

                    def evac_weights(j):
                        act.wait_ge(s["turnedP"], j + 1)
                        if j >= 3:
                            act.wait_ge(s["summed"], j - 2)
                        A(prT[:, j % 3, :], ps[:, 2 + j % 2, 0:3 * P], ACT.Copy).then_inc(s["prT_act"], 1)

                    for step in range(NHD + 1):
                        if step >= 1 and (step - 1) % 2 == 1:
                            evac_weights(step - 1)
                        if step < NHD:
                            weights(step)
                        if step == 2:
                            act.wait_ge(s["cexp_in"], 1)
                            A(cs[:], cs[:], ACT.Exp, scale=-1.0).then_inc(s["cexp"], 1)
                        if step == 6:
                            act.wait_ge(s["cturn"], 1)
                            A(pcT[:], ps[:, 7, :].rearrange("p (n q) -> p n q", q=P), ACT.Copy
                              ).then_inc(s["cturned"], 1)
                    evac_turned(HEADS_TURN, None)
                    act.wait_ge(s["wo_out"], 1)
                    act.dma_start(ple_w[:], w_pp[l].rearrange("(k p) n -> p k n", p=P)).then_inc(s["ple_in"], 16)

                    act.wait_ge(s["x_added"], 4)
                    norm(1)
                    evac_turned(2, 1)
                    act.wait_ge(s["rexp_in"], 1)
                    A(r_x[:], r_x[:], ACT.Exp)
                    A(e2, e2, ACT.Exp).then_inc(s["rexp"], 1)

                    act.wait_ge(s["misc6"], 2)
                    A(gb[:], ps[:, 6, 0:EPG * CAP].rearrange("p (e n) -> p e n", e=EPG), ACT.Copy
                      ).then_inc(s["free6"], 1)
                    act.wait_ge(s["misc7"], 2)
                    A(pickT[0:CAP, :, :], ps[0:CAP, 7, 0:TT * P].rearrange("p (t n) -> p t n", t=TT), ACT.Copy
                      ).then_inc(s["free7"], 1)
                    with act.Fori(0, NG) as g:
                        for e in range(EPG):
                            used(act, ATT_PIECES + G_ORDER.index(("gate", e)), g)
                            A(th[:, e % 2, :], ps[:, e % 2, 0:FN], ACT.Tanh, scale=0.5).then_inc(s["th_ready"], 1)
                        used(act, ATT_PIECES + GROUP_PIECES - 1, g)
                        A(y[0:CAP, 0:512], ps[0:CAP, 4, :], ACT.Copy).then_inc(s["y_act"], 1)
                        act.wait_ge(s["misc6"], 4 * g + 4)
                        A(gb[:], ps[:, 6, 0:EPG * CAP].rearrange("p (e n) -> p e n", e=EPG), ACT.Copy
                          ).then_inc(s["free6"], 1)
                        act.wait_ge(s["misc7"], 4 * g + 6)
                        A(pickT[0:CAP, :, :], ps[0:CAP, 7, 0:TT * P].rearrange("p (t n) -> p t n", t=TT), ACT.Copy
                          ).then_inc(s["free7"], 1)

                    act.wait_ge(s["route_done"], 1)
                    with act.If(act.value_load(most_i[0:1, 0:1], min_val=0, max_val=SEQ) > CAP):
                        with act.Fori(0, NG * EPG) as e:
                            for f in range(FT):
                                act.wait_ge(s["over_x"], FT * e + f + 1)
                                for dst, w in ((ow_gate, w_eg), (ow_up, w_eu)):
                                    act.dma_start(dst, w[l, e, :, f * P:(f + 1) * P].rearrange("(k p) n -> p k n", p=P)
                                                  ).then_inc(s["over_ld"], 16)
                                act.dma_start(ow_down, w_ed[l, e, f * P:(f + 1) * P, :]).then_inc(s["over_ld"], 16)
                                act.wait_ge(s["over_g"], 2 * FT * e + 2 * f + 1)
                                A(o_th, ps[:, 0, 0:SEQ], ACT.Tanh, scale=0.5).then_inc(s["over_t"], 1)
                        act.wait_ge(s["over_x"], NG * EPG * FT + 1)
                    act.wait_ge(s["free6"], 4 * NG + 2)
                    act.wait_ge(s["free7"], 4 * NG + 2)
                    norm(2)
                    evac_turned(3, 2)
                    for n in range(4):
                        if n % 2:
                            used(act, P_PG + n // 2)
                        else:
                            act.wait_ge(s["ple_z"], n // 2 + 1)
                        if n >= 2:
                            act.wait_ge(s["ple_x"], n - 1)
                        A(pth[:, n % 2, :], ps[:, n, :], ACT.Tanh, scale=0.5).then_inc(s["ple_th"], 1)

                @block.gpsimd
                def _(pool):
                    def inverse_rms(n):
                        pool.wait_ge(s["ms_ready"], n + 1)
                        nc.gpsimd.tensor_tensor(rstd[:], sq[:], tab[:, C_POW:C_POW + TT], ALU.pow
                                                ).then_inc(s["rstd_ready"], 1)

                    inverse_rms(0)
                    for m in range(4):
                        pool.wait_ge(s["out_even"], m + 3)
                        if m == 0:
                            pool.wait_ge(s["ocmp"], 2)
                        if m >= 1:
                            pool.wait_ge(s["part_added"], m)
                        o = xn[:, :, 512 + (m % 2) * 256:768 + (m % 2) * 256]
                        nc.gpsimd.tensor_tensor(
                            o, o, part[:, m % 2, :].rearrange("p (t n) -> p t n", t=TT), ALU.add
                        ).then_inc(s["part_added"], 1)
                    inverse_rms(1)
                    inverse_rms(2)

                @block.vector
                def _(dve):
                    V = nc.vector
                    c = Chain(dve, s["chain_dve"])

                    def norm(n):
                        V.tensor_tensor_reduce(xn[:, 0, :], x[:, 0, :], x[:, 0, :], 1.0, 0.0, ALU.mult, ALU.add,
                                               sq[:, 0:1]).then_inc(s["sq_dve"], 1)
                        dve.wait_ge(s["sq_dve"], n + 1)
                        dve.wait_ge(s["sq_act"], n + 1)
                        V.tensor_scalar(sq[:], sq[:], 1.0 / D, EPS, ALU.mult, ALU.add).then_inc(s["ms_ready"], 1)
                        dve.wait_ge(s["rstd_ready"], n + 1)
                        V.tensor_scalar(xn[:, 0, :], x[:, 0, :], rstd[:, 0:1], None, ALU.mult).then_inc(s["xn_dve"], 1)

                    def evac_turned(event, g):
                        for b in (1, 3):
                            dve.wait_ge(s["turned"], 4 * event + b + 1)
                            for k in (2 * b, 2 * b + 1):
                                src = ps[:, b, (k % 2) * SEQ:(k % 2 + 1) * SEQ]
                                ins = (V.tensor_copy(hT[:, k, :], src) if g is None else
                                       V.tensor_scalar(hT[:, k, :], src, gain(g, k), None, ALU.mult))
                                ins.then_inc(s["hT_dve"], 1)

                    dve.wait_ge(s["small_in"], 16)
                    norm(0)
                    evac_turned(0, 0)
                    dve.wait_ge(s["kcv_out"], 1)
                    for g in range(KVB):
                        for half in range(2):
                            lo = half * HD
                            kv = ps[g * HD:(g + 1) * HD, 4, :].rearrange("p (w n) -> p w n", w=2)
                            for w_i in range(2):
                                src = bass.AP(kv.tensor, kv.offset + w_i * SEQ + half,
                                              [list(kv.ap[0]), [2, NJ], [CSTR, NC]])
                                add = pos2[lo:lo + HD, w_i, :].unsqueeze(2).to_broadcast([HD, NJ, NC])
                                ins = V.tensor_tensor(blk[lo:lo + HD, w_i, :, g, :], src, add, ALU.add)
                            ins.then_inc(s["blk_ready"], 1)
                    dve.wait_ge(s["qb_out"], 1)
                    V.tensor_scalar(qbT[:, 0:2, :], ps[:, 0, :].rearrange("p (i n) -> p i n", i=2), -(HD ** -0.5),
                                    None, ALU.mult).then_inc(s["qb_dve"], 1)
                    used(dve, P_KVW)
                    NV = P + 3 * HB
                    dve.wait_ge(s["gate_act"], 1)
                    V.tensor_copy(vb[:, 1, :, :], ps[:, 7, 0:2 * NV].rearrange("p (t n) -> p t n", t=TT)[:, :, 0:P]
                                  ).then_inc(s["vw_ready"], 1)
                    V.tensor_scalar(gate[:], gate[:], 0.5, 0.5, ALU.mult, ALU.add).then_inc(s["gate_dve"], 1)
                    used(dve, P_CV1)
                    V.tensor_copy(hid, ps[:, 2, 0:NH]).then_inc(s["gelu_x"], 1)
                    dve.wait_ge(s["gelu_x"], 1)
                    c.add(V.tensor_tensor(hid_u, hid, hid, ALU.mult))
                    c.wait()
                    c.add(V.tensor_scalar(hid_u, hid_u, 0.044715, 1.0, ALU.mult, ALU.add))
                    c.wait()
                    V.tensor_tensor(hid_u, hid_u, hid, ALU.mult).then_inc(s["gelu_t"], 1)
                    dve.wait_ge(s["gelu_t"], 2)
                    c.add(V.scalar_tensor_tensor(out=hid_u, in0=hid_u, scalar=1.0, in1=hid, op0=ALU.add, op1=ALU.mult))
                    c.wait()
                    V.tensor_scalar(hid_g.rearrange("p w m n -> p (w m n)"), hid_u, 0.5, None,
                                    ALU.mult).then_inc(s["gelu_done"], 1)
                    used(dve, P_KA)
                    V.tensor_copy(kaT[:, 2:4, :], ps[:, 5, :].rearrange("p (i n) -> p i n", i=2)
                                  ).then_inc(s["qk_dve"], 1)
                    used(dve, P_QA)
                    V.tensor_scalar(qaT[:, 2:4, :], ps[:, 7, :].rearrange("p (i n) -> p i n", i=2), -(HD ** -0.5),
                                    None, ALU.mult).then_inc(s["qk_dve"], 1)
                    dve.wait_ge(s["kc_ready"], 2)
                    for g in range(KVB):
                        for h in range(REP):
                            V.tensor_copy(vbd[h * CPAD:h * CPAD + NC, g, h * HD:(h + 1) * HD],
                                          ps[0:NC, 3, HD + g * HD:2 * HD + g * HD]).then_inc(s["vc_ready"], 1)
                    used(dve, P_VA)
                    V.tensor_copy(va[:, 1, :], ps[:, 1, :]).then_inc(s["va_dve"], 1)

                    def add_cost(j):
                        kind, h = HEADS[j]
                        tb = cost_a if kind == "a" else cost_b
                        dve.wait_ge(s["score"], j + 1)
                        if j >= 2:
                            dve.wait_ge(s["expd"], 2 * (j - 1))
                        for t in range(TT):
                            lo, n = (0, P) if t == 0 else (P, SEQ)
                            V.tensor_tensor_reduce(cost[:, j % 2, lo:lo + n], ps[:, 4 + j % 2, lo:lo + n],
                                                   tb[:, h, SEQ - n:SEQ], 1.0, 3.0e38, ALU.add, ALU.min,
                                                   low[:, j, t:t + 1]).then_inc(s["costed"], 1)

                    def evac_weights(j):
                        dve.wait_ge(s["turnedP"], j + 1)
                        if j >= 3:
                            dve.wait_ge(s["summed"], j - 2)
                        V.tensor_copy(prT[:, j % 3, :], ps[:, 2 + j % 2, 0:3 * P]).then_inc(s["prT_dve"], 1)

                    def finish_heads(m):
                        j0 = 4 * m
                        dve.wait_ge(s["expd"], 2 * (j0 + 4))
                        c.add(V.reciprocal(wgt[:, j0:j0 + 4, :], den[:, j0:j0 + 4, :]))
                        c.wait()
                        kind, h0 = HEADS[j0]
                        if kind != "a":
                            br = 1 if kind == "s" else 2
                            gt = gate[:].rearrange("p t (h b) -> p h b t", b=3)[:, h0:h0 + 4, br, :]
                            c.add(V.tensor_tensor(wgt[:, j0:j0 + 4, :], wgt[:, j0:j0 + 4, :], gt, ALU.mult))
                            c.wait()
                        dve.wait_ge(s["summed"], j0 + 4)
                        if m >= 4:
                            dve.wait_ge(s["part_added"], m - 3)
                        if kind == "a":
                            dst = xn[:, :, h0 * HD:(h0 + 4) * HD].rearrange("p t (i d) -> p i t d", i=4)
                        else:
                            dst = part[:, m % 2, :].rearrange("p (t i d) -> p i t d", t=TT, i=4)
                        V.tensor_tensor(dst, ps[:, m % 2, :].rearrange("p (i t d) -> p i t d", i=4, t=TT),
                                        wgt[:, j0:j0 + 4, :].unsqueeze(3).to_broadcast([P, 4, TT, HD]),
                                        ALU.mult).then_inc(s["out_even"], 1)

                    cost_c = tab[:, C_CC:C_CC + TT * HB * NC].rearrange("p (b n c) -> p b n c", b=2, c=NC)
                    valid_c = tab[:, C_CV:C_CV + TT * NC].rearrange("p (t c) -> p t c", t=TT)
                    for step in range(NHD + 3):
                        if step < NHD:
                            add_cost(step)
                        if 1 <= step <= NHD and (step - 1) % 2 == 0:
                            evac_weights(step - 1)
                        if step >= 3 and (step - 3) % 4 == 3:
                            finish_heads((step - 3) // 4)
                        if step == 1:
                            dve.wait_ge(s["cscore"], 1)
                            c.add(V.tensor_tensor(cz[:].rearrange("p (b n) c -> p b n c", b=2), ps[:, 6:8, 0:TT * REP * CPAD].rearrange("p b (n c) -> p b n c", c=CPAD)[:, :, :, 0:NC],
                                                  cost_c, ALU.add))
                            c.wait()
                            c.add(V.tensor_reduce(clow, cz[:], AX.X, ALU.min))
                            c.wait()
                            V.tensor_tensor(cs[:], cz[:], clow.unsqueeze(2).to_broadcast([P, TT * HB, NC]),
                                            ALU.subtract).then_inc(s["cexp_in"], 1)
                        if step == 3:
                            dve.wait_ge(s["cexp"], 1)
                            c.add(V.tensor_reduce(cden, cs[:], AX.X, ALU.add))
                            for t in range(TT):
                                ins = V.tensor_tensor(pc[:, t, :, 0:NC].rearrange("p (i b) c -> p b i c", b=2),
                                                      cs[:].rearrange("p (b t i) c -> p b t i c", b=2, t=TT)[:, :, t, :, :],
                                                      valid_c[:, t, :].unsqueeze(1).unsqueeze(1)
                                                      .to_broadcast([P, 2, HB // 2, NC]), ALU.mult)
                            ins.then_inc(s["cprob"], 1)
                            c.wait()
                            c.add(V.reciprocal(cw, cden))
                            c.wait()
                            dve.wait_ge(s["gate_dve"], 1)
                            gt = gate[:].rearrange("p t (i q b) -> p q t i b", q=2, b=3)[:, :, :, :, 0]
                            cwv = cw.rearrange("p (q t i) -> p q t i", q=2, t=TT)
                            c.add(V.tensor_tensor(cwv, cwv, gt, ALU.mult))
                        if step == 10:
                            dve.wait_ge(s["cout"], 1)
                            c.wait()
                            for t in range(TT):
                                cwt = cw.rearrange("p (q t i) -> p i q t", q=2, t=TT)[:, :, :, t]
                                V.tensor_tensor(xn[:, t, 512:1024].rearrange("p (i q d) -> p i q d", q=2, d=HD),
                                                ps[:, 6 + t, :].rearrange("p (i q d) -> p i q d", q=2, d=HD),
                                                cwt.unsqueeze(3).to_broadcast([P, HB // 2, 2, HD]),
                                                ALU.mult).then_inc(s["ocmp"], 1)
                    evac_turned(HEADS_TURN, None)
                    for n in range(4):
                        half, t = n // 2, n % 2
                        if t:
                            used(dve, P_WO0 + half)
                        else:
                            dve.wait_ge(s["wo_out"], half + 1)
                        xs = x[:, t, half * 512:(half + 1) * 512]
                        V.tensor_tensor(xs, xs, ps[:, 4 + n, :], ALU.add).then_inc(s["x_added"], 1)

                    dve.wait_ge(s["x_added"], 4)
                    norm(1)
                    evac_turned(2, 1)
                    tie = tab[:, C_TIE:C_TIE + 4].unsqueeze(1).to_broadcast([P, TT, 4])

                    def wide(v):
                        return v.unsqueeze(2).to_broadcast([P, TT, 4])

                    def do(ins):
                        c.add(ins)
                        c.wait()

                    def first_max(dst, val, m):
                        do(V.tensor_reduce(m, val, AX.X, ALU.max))
                        do(V.tensor_tensor(r_e[:], val, wide(m), ALU.is_equal))
                        do(V.tensor_tensor(r_w[:], r_e[:], tie, ALU.mult))
                        do(V.tensor_reduce(r_wm, r_w[:], AX.X, ALU.max))
                        do(V.tensor_tensor(dst, r_w[:], wide(r_wm), ALU.is_equal))

                    dve.wait_ge(s["routed"], 1)
                    do(V.tensor_copy(lg[:], ps[:, 4, 0:TT * NR].rearrange("p (t n) -> p t n", t=TT)))
                    glog = lg[:, :, 0:NG]
                    do(V.tensor_reduce(r_m, glog, AX.X, ALU.max))
                    do(V.tensor_tensor(r_e[:], glog, wide(r_m), ALU.is_equal))
                    do(V.tensor_tensor(r_w[:], r_e[:], tie, ALU.mult))
                    do(V.tensor_reduce(r_wm, r_w[:], AX.X, ALU.max))
                    V.tensor_tensor(onehot[:], r_w[:], wide(r_wm), ALU.is_equal).then_inc(s["rank_in"], 1)
                    do(V.tensor_tensor(r_x[:], glog, wide(r_m), ALU.subtract))
                    dve.wait_ge(s["rank_in"], 1)
                    big = r_big.rearrange("p (t e g) -> p t e g", t=TT, e=EPG)
                    for t in range(TT):
                        ins = V.tensor_tensor(big[:, t, :, :],
                                              lg[:, t, NG:NR].rearrange("p (g e) -> p e g", g=NG),
                                              onehot[:, t, :].unsqueeze(1).to_broadcast([P, EPG, NG]), ALU.mult)
                    do(ins)
                    do(V.tensor_reduce(within[:], big, AX.X, ALU.add))
                    first_max(sel1[:], within[:], top1)
                    do(V.scalar_tensor_tensor(out=within[:], in0=sel1[:], scalar=-HUGE, in1=within[:],
                                              op0=ALU.mult, op1=ALU.add))
                    first_max(sel2[:], within[:], top2)
                    V.tensor_tensor(e2, top2, top1, ALU.subtract).then_inc(s["rexp_in"], 1)
                    dve.wait_ge(s["ranked"], 1)
                    do(V.scalar_tensor_tensor(out=slot_of[:, :, 0:NG],
                                              in0=ps[:, 5, 0:2 * NG].rearrange("p (t n) -> p t n", t=TT),
                                              scalar=1.0, in1=onehot[:], op0=ALU.add, op1=ALU.mult))
                    V.memset(slot_of[:, :, NG:NG + 1], -1.0)
                    do(V.tensor_scalar(slot_of[:, :, 0:NG], slot_of[:, :, 0:NG], -1.0, None, ALU.add))
                    do(V.tensor_reduce(most, ps[:, 5, 2 * NG:3 * NG], AX.X, ALU.max))
                    V.tensor_copy(most_i[:], most).then_inc(s["route_done"], 1)
                    dve.wait_ge(s["rexp"], 1)
                    do(V.tensor_reduce(gsum, r_x[:], AX.X, ALU.add))
                    do(V.reciprocal(gw, gsum))
                    do(V.tensor_scalar(w1, e2, 1.0, None, ALU.add))
                    do(V.reciprocal(w1, w1))
                    do(V.tensor_tensor(w1, w1, gw, ALU.mult))
                    do(V.tensor_tensor(w2, w1, e2, ALU.mult))
                    do(V.tensor_tensor(sel1[:], sel1[:], wide(w1), ALU.mult))
                    do(V.tensor_tensor(sel2[:], sel2[:], wide(w2), ALU.mult))
                    do(V.tensor_tensor(local[:], sel1[:], sel2[:], ALU.add))
                    do(V.tensor_scalar(local2[:], local[:], 0.5, None, ALU.mult))

                    def make_pick(col):
                        for t in range(TT):
                            ins = V.tensor_scalar(pick[:, t, :], tab[:, C_IOTA:C_IOTA + CAP], slot_of[:, t, col:col + 1]
                                                  if isinstance(col, int) else slot_of[:, t, bass.ds(col, 1)],
                                                  None, ALU.is_equal)
                        ins.then_inc(s["picked"], 1)

                    def evac_gathered(n6, n7):
                        for b in range(2):
                            dve.wait_ge(s["misc6" if b == 0 else "misc7"], n6 if b == 0 else n7)
                            V.tensor_tensor(xg[:, b * 4:b * 4 + 4, :],
                                            ps[:, 6 + b, 0:4 * CAP].rearrange("p (k n) -> p k n", k=4),
                                            gain(1, b * 4, 4).unsqueeze(2).to_broadcast([P, 4, CAP]),
                                            ALU.mult).then_inc(s["free6" if b == 0 else "free7"], 1)

                    make_pick(0)
                    dve.wait_ge(s["hT_act"], 3 * KT // 2)
                    dve.wait_ge(s["hT_dve"], 3 * KT // 2)
                    dve.sem_inc(s["bank_free"], 2)
                    evac_gathered(1, 1)
                    base = c.n
                    with dve.Fori(0, NG) as g:
                        cg = Chain(dve, s["chain_dve"], 0, base + 2 * EPG * g)
                        dve.wait_ge(s["misc7"], 4 * g + 2)
                        make_pick(g + 1)
                        for e in range(EPG):
                            b = e % 2
                            dve.wait_ge(s["th_ready"], EPG * g + e + 1)
                            cg.add(V.scalar_tensor_tensor(out=a1[:, b, :], in0=th[:, b, :], scalar=1.0,
                                                          in1=ps[:, b, 0:FN], op0=ALU.add, op1=ALU.mult))
                            used(dve, ATT_PIECES + G_ORDER.index(("up", e)), g)
                            cg.wait()
                            cg.add(V.tensor_tensor(a2[:, b, :], a1[:, b, :], ps[:, 2 + b, 0:FN], ALU.mult))
                            cg.wait()
                            dve.sem_inc(s["bank_free"], 1)
                            if e == 0:
                                dve.wait_ge(s["free6"], 4 * g + 2)
                            V.tensor_tensor(act_in[:, b, :].rearrange("p (f n) -> p f n", f=FT),
                                            a2[:, b, :].rearrange("p (f n) -> p f n", f=FT),
                                            gb[:, e, :].unsqueeze(1).to_broadcast([P, FT, CAP]),
                                            ALU.mult).then_inc(s["act_ready"], 1)
                        assert cg.n == 2 * EPG
                        evac_gathered(4 * g + 3, 4 * g + 3)
                        used(dve, ATT_PIECES + GROUP_PIECES - 1, g)
                        V.tensor_copy(y[0:CAP, 512:1024], ps[0:CAP, 5, :]).then_inc(s["y_dve"], 1)
                        for n in range(4):
                            t, half = n % 2, n // 2
                            b = 7 - n % 2
                            dve.wait_ge(s["misc7" if b == 7 else "misc6"], 4 * g + 4 + (n // 2) + (b == 6))
                            xs = x[:, t, half * 512:(half + 1) * 512]
                            V.tensor_tensor(xs, xs, ps[:, b, :], ALU.add).then_inc(s["free7" if b == 7 else "free6"], 1)
                    c.n += 2 * EPG * NG

                    dve.wait_ge(s["free6"], 4 * NG + 2)
                    dve.wait_ge(s["free7"], 4 * NG + 2)
                    with dve.If(dve.value_load(most_i[0:1, 0:1], min_val=0, max_val=SEQ) > CAP):
                        co = Chain(dve, s["over_l"])
                        co.add(V.tensor_scalar(late[:], slot_of[:, :, 0:NG], float(CAP), None, ALU.is_ge))
                        co.wait()
                        for t in range(TT):
                            ins = V.tensor_tensor(over_w[:, t, :, :], late[:, t, :].unsqueeze(2).to_broadcast([P, NG, EPG]),
                                                  local2[:, t, :].unsqueeze(1).to_broadcast([P, NG, EPG]), ALU.mult)
                        ins.then_inc(s["over_x"], 1)
                        dve.wait_ge(s["over_x"], 1)
                        with dve.Fori(0, NG * EPG) as e:
                            ce = Chain(dve, s["over_l"], 0, co.n + FT * e)
                            for f in range(FT):
                                dve.wait_ge(s["over_t"], FT * e + f + 1)
                                ce.add(V.scalar_tensor_tensor(out=o_a1, in0=o_th, scalar=1.0, in1=ps[:, 0, 0:SEQ],
                                                              op0=ALU.add, op1=ALU.mult))
                                ce.wait()
                                dve.wait_ge(s["over_g"], 2 * FT * e + 2 * f + 2)
                                V.tensor_tensor(o_a2, o_a1, ps[:, 1, 0:SEQ], ALU.mult).then_inc(s["over_a"], 1)
                                dve.wait_ge(s["over_y"], FT * e + f + 1)
                                for t in range(TT):
                                    for half in range(2):
                                        xs = x[:, t, half * 512:(half + 1) * 512]
                                        ins = V.scalar_tensor_tensor(
                                            out=xs, in0=ps[:, 2 + 2 * t + half, :],
                                            scalar=over_wf[:, t, bass.ds(e, 1)], in1=xs, op0=ALU.mult, op1=ALU.add)
                                ins.then_inc(s["over_x"], 1)
                        dve.wait_ge(s["over_x"], NG * EPG * FT + 1)
                    norm(2)
                    evac_turned(3, 2)
                    for n in range(4):
                        half, t = n // 2, n % 2
                        dve.wait_ge(s["ple_th"], n + 1)
                        dve.wait_ge(s["ple_q"], 4)
                        do(V.scalar_tensor_tensor(out=pv[:, n % 2, :], in0=pth[:, n % 2, :], scalar=1.0,
                                                  in1=ps[:, 4 + n, :], op0=ALU.add, op1=ALU.mult))
                        xs = x[:, t, half * 512:(half + 1) * 512]
                        V.scalar_tensor_tensor(out=xs, in0=pv[:, n % 2, :], scalar=0.5, in1=xs, op0=ALU.mult,
                                               op1=ALU.add).then_inc(s["ple_x"], 1)

            nc.sync.sem_clear(range(nums[0], nums[-1] + 1))
            nc.all_engine_barrier()

        with nc.Block() as block:
            @block.gpsimd
            def _(pool):
                pool.wait_ge(s["ms_ready"], 1)
                nc.gpsimd.tensor_tensor(rstd[:], sq[:], tab[:, C_POW:C_POW + TT], ALU.pow
                                        ).then_inc(s["rstd_ready"], 1)

            @block.scalar
            def _(act):
                nc.scalar.activation(xn[:, 1, :], x[:, 1, :], ACT.Square, accum_out=sq[:, 1:2]
                                     ).then_inc(s["sq_act"], 1)

            @block.vector
            def _(dve):
                V = nc.vector
                c = Chain(dve, s["chain_dve"])
                c.add(V.tensor_tensor_reduce(xn[:, 0, :], x[:, 0, :], x[:, 0, :], 1.0, 0.0, ALU.mult, ALU.add,
                                             sq[:, 0:1]))
                c.wait()
                dve.wait_ge(s["sq_act"], 1)
                V.tensor_scalar(sq[:], sq[:], 1.0 / D, EPS, ALU.mult, ALU.add).then_inc(s["ms_ready"], 1)
                dve.wait_ge(s["rstd_ready"], 1)
                for t in range(TT):
                    V.scalar_tensor_tensor(out=xn[:, t, :], in0=x[:, t, :], scalar=rstd[:, t:t + 1], in1=fgain[:],
                                           op0=ALU.mult, op1=ALU.mult).then_inc(s["xn_dve"], 1)

            @block.sync
            def _(sp):
                o = out.rearrange("(t p) d -> p t d", p=P)
                for t in range(TT):
                    sp.wait_ge(s["xn_dve"], t + 1)
                    sp.dma_start(o[:, t, :], xn[:, t, :]).then_inc(out_sem, 16)
                sp.wait_ge(out_sem, 16 * TT)


def kernel(x, p, attn_norm, w_in, w_out, w_cmp_k1, w_cmp_k2, w_cmp_v1, w_cmp_v2, cmp_pos,
           ffn_norm, w_route_group, b_route_group, w_route_expert, b_route_expert,
           w_expert_gate, w_expert_up, w_expert_down, ple_norm, w_ple_gate, w_ple_proj, final_norm):
    import numpy as _np
    import concourse.bacc as _bacc
    from concourse import mybir as _mybir
    from concourse.bass_utils import run_bass_kernel_spmd as _run

    A = _np.asarray

    def columns(a):
        a = A(a)
        d, r, n = a.shape
        return a.reshape(d, r // P, P, n).transpose(0, 2, 1, 3).reshape(d, P, -1)

    bias = _np.zeros((DEPTH, P, NR), _np.float32)
    bias[:, 0, :NG] = A(b_route_group)
    bias[:, 0, NG:] = A(b_route_expert)
    pos = A(cmp_pos).reshape(DEPTH, 2, CBLK // 2, 2, HD).transpose(0, 3, 4, 1, 2).reshape(DEPTH, P, -1)
    router = _np.concatenate([A(w_route_group), A(w_route_expert)], axis=2)
    small = _np.concatenate(
        [columns(A(g)[:, :, None]) for g in (attn_norm, ffn_norm, ple_norm)]
        + [pos, columns(w_cmp_k2), columns(w_cmp_v2), columns(router), bias,
           columns(A(p)[:, 0].transpose(0, 2, 1))], axis=2)
    arrays = {
        "x_rows": A(x)[0], "small": small, "tables": tables(),
        "final_rows": _np.broadcast_to(A(final_norm)[None, :], (P, D)),
        "w_in": A(w_in), "w_out": A(w_out), "w_cmp_k1": A(w_cmp_k1), "w_cmp_v1": A(w_cmp_v1),
        "w_expert_gate": A(w_expert_gate), "w_expert_up": A(w_expert_up), "w_expert_down": A(w_expert_down),
        "w_ple_gate": A(w_ple_gate), "w_ple_proj": A(w_ple_proj),
    }
    arrays = {k: _np.ascontiguousarray(v) for k, v in arrays.items()}
    nc = _bacc.Bacc("TRN2", target_bir_lowering=False, num_devices=1)
    args = [nc.dram_tensor(k + "_dram", v.shape, _mybir.dt.from_np(v.dtype), kind="ExternalInput").ap()
            for k, v in arrays.items()]
    args.append(nc.dram_tensor("out_dram", (SEQ, D), _mybir.dt.float32, kind="ExternalOutput").ap())
    build_trunk(nc, *args)
    r = _run(nc, [{k + "_dram": v for k, v in arrays.items()}], core_ids=[0])
    return r.results[0]["out_dram"].reshape(1, SEQ, D)
```

```python
import math
from contextlib import ExitStack

import numpy as np

import concourse.bass as bass
from concourse import mybir

F32 = mybir.dt.float32
I32 = mybir.dt.int32
ALU = mybir.AluOpType
ACT = mybir.ActivationFunctionType
AX = mybir.AxisListType

P = 128
DEPTH, SEQ, D = 2, 256, 1024
TT = SEQ // P
KT = D // P
HD = 64
HA, HB, KVB = 8, 8, 2
REP = HB // KVB
PLE = 256
NG, EPG, DE = 4, 4, 512
FT = DE // P
NR = NG + NG * EPG
CBLK, CSTR, CHID = 32, 16, 256
NC = (SEQ - CBLK) // CSTR + 1
CPAD = 32
CAP = 64
NE = NG * EPG
PAIRS = NE // 2
EPS = 1e-6
HUGE = 1e30
GELU_C = math.sqrt(2.0 / math.pi)

QA, KA, VA, QB = 0, 512, 1024, 1536
KC = 2048
KW = KC + 512
N_IN = KW + 2 * P + 3 * HB

HEADS_TURN = 1

RING = 6
SLOT = 4096
ATT_PIECES = 10
PAIR_PIECES = 6
PIECES = ATT_PIECES + PAIRS * PAIR_PIECES + 2
ROUNDS = PIECES // RING
assert PIECES % RING == 0 and PAIR_PIECES % RING == 0
P_KCV, P_QB, P_KVW, P_CK1, P_CV1, P_KA, P_QA, P_VA, P_WO0, P_WO1 = range(ATT_PIECES)
E_GATE, E_UP, E_DOWN = 0, 2, 4
P_PG = PIECES - 2

SM_GAIN = 0
SM_POS = SM_GAIN + 3 * KT
SM_W2 = SM_POS + 2 * (CBLK // 2)
SM_ROUT = SM_W2 + 2 * 2 * HD
SM_RB = SM_ROUT + KT * NR
SM_PT = SM_RB + NR
SM = SM_PT + 2 * SEQ
C_DIST = 0
C_MA = C_DIST + SEQ
C_MB = C_MA + SEQ
C_CC = C_MB + SEQ
C_CV = C_CC + TT * HB * NC
C_ID = C_CV + TT * NC
C_LT = C_ID + P
C_ONE = C_LT + P
C_IOTA = C_ONE + P
C_TIE = C_IOTA + CAP
C_POW = C_TIE + 4
C_TRI = C_POW + TT
CN = C_TRI + 16


def slopes():
    n = HA + HB
    s = [2.0 ** (-8.0 * (i + 1) / n) for i in range(n)]
    return s[0::2], s[1::2]


def tables():
    c = np.zeros((P, CN), np.float64)
    q = np.arange(P)[:, None]
    dist = P + q - np.arange(SEQ)[None, :]
    past = dist >= 0
    count = ((dist <= 128).astype(int) + (dist % 4 == 0) + (dist % 16 == 0)) * past
    c[:, C_DIST:C_DIST + SEQ] = np.where(past, dist, 0)
    c[:, C_MA:C_MA + SEQ] = np.where(count > 0, -np.log(np.maximum(count, 1)), HUGE)
    c[:, C_MB:C_MB + SEQ] = np.where(past, 0.0, HUGE)
    end = np.arange(NC) * CSTR + CBLK - 1
    _, mb = slopes()
    for t in range(TT):
        dc = (t * P + q) - end[None, :]
        for h in range(HB):
            at = C_CC + (((h % 2) * TT + t) * (HB // 2) + h // 2) * NC
            c[:, at:at + NC] = np.where(dc >= 0, mb[h] * dc, HUGE)
        c[:, C_CV + t * NC:C_CV + (t + 1) * NC] = dc >= 0
    c[:, C_ID:C_ID + P] = np.eye(P)
    c[:, C_LT:C_LT + P] = q < np.arange(P)[None, :]
    c[:, C_ONE:C_ONE + P] = 1.0
    c[:, C_IOTA:C_IOTA + CAP] = np.arange(CAP)
    c[:, C_TIE:C_TIE + 4] = [4, 3, 2, 1]
    c[:, C_POW:C_POW + TT] = -0.5
    c[:, C_TRI:C_TRI + 16] = np.tril(np.ones((4, 4)), -1).ravel()
    return c.astype(np.float32)


class Chain:

    def __init__(self, eng, sem, n=0, base=0):
        self.eng, self.sem, self.n, self.base = eng, sem, n, base

    def add(self, ins):
        self.n += 1
        ins.then_inc(self.sem, 1)

    def wait(self):
        self.eng.wait_ge(self.sem, self.base + self.n)


def build_trunk(nc, x_in, small_in, table_in, fgain_in, w_in, w_out, w_ck1, w_cv1,
                w_eg, w_eu, w_ed, w_pg, w_pp, out):
    ctx = ExitStack()
    with ctx:
        def sb(name, shape, dt=F32):
            return ctx.enter_context(nc.sbuf_tensor(name, shape, dt))

        ring = sb("ring", [P, RING, SLOT])
        x = sb("x", [P, TT, D])
        xn = sb("xn", [P, TT, D])
        hT = sb("hT", [P, KT, SEQ])
        tab = sb("tab", [P, CN])
        small = sb("small", [P, SM])
        fgain = sb("fgain", [P, D])
        cost_a = sb("cost_a", [P, HA, SEQ])
        cost_b = sb("cost_b", [P, HB, SEQ])
        pc = sb("pc", [P, TT, HB, CPAD])
        vbd = sb("vbd", [P, KVB, REP * HD])
        sq = sb("sq", [P, TT])
        xn_flat = xn[:].rearrange("p t d -> p (t d)")
        rstd = sb("rstd", [P, TT])
        work = sb("work", [P, 13700])

        ps = ctx.enter_context(nc.psum_tensor("ps", [P, 8, 512], F32))

        cut = [0]

        def take(n):
            cut[0] += n
            assert cut[0] <= 13700, cut[0]
            return work[:, cut[0] - n:cut[0]]

        qbT = take(4 * SEQ).rearrange("p (i n) -> p i n", i=4)
        qaT = take(4 * SEQ).rearrange("p (i n) -> p i n", i=4)
        kaT = take(4 * SEQ).rearrange("p (i n) -> p i n", i=4)
        kbT = take(KVB * 2 * SEQ).rearrange("p (g w n) -> p g w n", g=KVB, w=2)
        va = take(TT * 512).rearrange("p (t n) -> p t n", t=TT)
        vb = take(TT * 2 * P).rearrange("p (w t n) -> p w t n", w=2, t=TT)
        gate = take(TT * 3 * HB).rearrange("p (t n) -> p t n", t=TT)
        cost = take(2 * 3 * P).rearrange("p (b n) -> p b n", b=2)
        pr = take(3 * 3 * P).rearrange("p (b n) -> p b n", b=3)
        prT = take(3 * 3 * P).rearrange("p (b n) -> p b n", b=3)
        low = take(24 * TT).rearrange("p (j t) -> p j t", t=TT)
        den = take(24 * TT).rearrange("p (j t) -> p j t", t=TT)
        wgt = take(24 * TT).rearrange("p (j t) -> p j t", t=TT)
        part = take(2 * 512).rearrange("p (b n) -> p b n", b=2)
        NJ = CBLK // 2
        blk = take(2 * NJ * KVB * NC).rearrange("p (w j g c) -> p w j g c", w=2, j=NJ, g=KVB)
        NH = 2 * 2 * KVB * NC
        hid = take(NH)
        hid_u = take(NH)
        hid_g = take(NH).rearrange("p (w m n) -> p w m n", w=2, m=2)
        kcT = take(KVB * NC).rearrange("p (g c) -> p g c", g=KVB)
        cs = take(TT * HB * NC).rearrange("p (n c) -> p n c", c=NC)
        cz = take(TT * HB * NC).rearrange("p (n c) -> p n c", c=NC)
        clow = take(TT * HB)
        cden = take(TT * HB)
        cw = take(TT * HB)
        pcT = take(TT * KVB * P).rearrange("p (n q) -> p n q", q=P)

        cut[0] = 0
        lg = take(TT * NR).rearrange("p (t n) -> p t n", t=TT)
        r_m = take(TT)
        r_e = take(TT * 4).rearrange("p (t n) -> p t n", t=TT)
        r_w = take(TT * 4).rearrange("p (t n) -> p t n", t=TT)
        r_wm = take(TT)
        onehot = take(TT * NG).rearrange("p (t n) -> p t n", t=TT)
        r_x = take(TT * 4).rearrange("p (t n) -> p t n", t=TT)
        gsum = take(TT)
        gw = take(TT)
        r_big = take(TT * NE)
        r_gt = take(TT * NE)
        within = take(TT * EPG).rearrange("p (t n) -> p t n", t=TT)
        above = take(TT * EPG).rearrange("p (t n) -> p t n", t=TT)
        chosen = take(TT * EPG).rearrange("p (t n) -> p t n", t=TT)
        top = take(TT)
        ex = take(TT * EPG).rearrange("p (t n) -> p t n", t=TT)
        esum = take(TT)
        member = take(TT * NE).rearrange("p (t n) -> p t n", t=TT)
        weight = take(TT * (NE + 2)).rearrange("p (t n) -> p t n", t=TT)
        slot_of = take(TT * (NE + 2)).rearrange("p (t n) -> p t n", t=TT)
        most = take(1)
        over_w = take(TT * NE).rearrange("p (t n) -> p t n", t=TT)
        pick = take(TT * P).rearrange("p (t n) -> p t n", t=TT)
        pickw = take(TT * P).rearrange("p (t n) -> p t n", t=TT)
        pickT = take(TT * P).rearrange("p (t n) -> p t n", t=TT)
        xg = take(KT * P).rearrange("p (k n) -> p k n", k=KT)
        over_from = cut[0]
        th = take(DE)
        a1 = take(DE)
        act_in = take(DE)
        actT = take(FT * P).rearrange("p (f n) -> p f n", f=FT)
        y = take(D)
        ow_gate = work[:, over_from:over_from + KT * P].rearrange("p (k n) -> p k n", k=KT)
        ow_up = work[:, over_from + KT * P:over_from + 2 * KT * P].rearrange("p (k n) -> p k n", k=KT)
        ow_down = work[:, over_from + 2 * KT * P:over_from + 2 * KT * P + D]
        o_th, o_a1, o_a2 = (xn_flat[:, i * SEQ:(i + 1) * SEQ] for i in range(3))
        assert cut[0] >= over_from + 3 * D
        ple_w = take(2 * D).rearrange("p (k n) -> p k n", k=2)
        pth = take(2 * 512).rearrange("p (b n) -> p b n", b=2)
        pv = take(2 * 512).rearrange("p (b n) -> p b n", b=2)
        most_i = sb("most_i", [P, 1], I32)

        ident = tab[:, C_ID:C_ID + P]
        ones = tab[:, C_ONE:C_ONE + P]

        def gain(s, k0, n=1):
            return small[:, SM_GAIN + s * KT + k0:SM_GAIN + s * KT + k0 + n]

        pos2 = small[:, SM_POS:SM_POS + 2 * NJ].rearrange("p (w j) -> p w j", w=2)
        cw2 = small[:, SM_W2:SM_W2 + 4 * HD].rearrange("p (w m n) -> p w m n", w=2, m=2)
        rout = small[:, SM_ROUT:SM_ROUT + KT * NR].rearrange("p (k n) -> p k n", k=KT)
        pT = small[:, SM_PT:SM_PT + 2 * SEQ].rearrange("p (k n) -> p k n", k=2)

        def sem(name):
            return ctx.enter_context(nc.semaphore(name))

        slot_in = [sem(f"slot_in{i}") for i in range(RING)]
        piece_used = sem("piece_used")
        x_in_sem, table_sem, fgain_sem, out_sem = sem("x_in"), sem("table"), sem("fgain"), sem("out_s")
        small_sem = sem("small_in")
        names = """ple_in sq_act sq_dve ms_ready rstd_ready chain_dve xn_dve xn_act turned hT_act hT_dve kcv_out qb_out kb_out qa_out ka_out cmp_out va_out
            blk_ready kb_act vs_ready vw_ready gate_act gate_dve qb_dve qb_act gelu_x gelu_t gelu_done
            qk_act qk_dve kc_ready vc_ready va_act va_dve cscore cexp_in cexp cprob cturn cturned cout
            ocmp score costed expd turnedP prT_dve prT_act summed out_even part_added wo_out x_added
            routed rank_in ranked gexp_in gexp eexp_in eexp route_done picked pickw_ready gathered
            xg_ready th_ready act_ready act_turned actT_ready pick_turned pickT_ready y_act y_dve
            scattered added
            ple_q ple_z ple_th ple_x over_ld over_g over_t over_a over_y over_x over_l""".split()
        s = {n: sem("l_" + n) for n in names}
        nums = [v.num for v in s.values()]
        assert nums == list(range(nums[0], nums[0] + len(nums)))

        def piece_src(l, i):
            cols = {P_KCV: (KC, 512), P_QB: (QB, 512), P_KVW: (KW, N_IN - KW), P_QA: (QA, 512),
                    P_KA: (KA, 512), P_VA: (VA, 512)}
            if i in cols:
                c, n = cols[i]
                return w_in[l, :, c:c + n].rearrange("(k p) n -> p k n", p=P), n
            if i in (P_CK1, P_CV1):
                return (w_ck1 if i == P_CK1 else w_cv1)[l].rearrange("(k p) n -> p k n", p=P), CHID
            if i in (P_WO0, P_WO1):
                h = i - P_WO0
                return w_out[l, :, h * 512:(h + 1) * 512].rearrange("(k p) n -> p k n", p=P), 512
            h = i - P_PG
            return w_pg[l, :, h * 512:(h + 1) * 512].rearrange("(k p) n -> p k n", p=P), 512

        def slot(i, n):
            k = SLOT // n
            return ring[:, i % RING, 0:k * n].rearrange("p (k n) -> p k n", n=n)

        def slot8(i, n=512):
            return ring[:, i % RING, 0:KT * n].rearrange("p (k n) -> p k n", n=n)

        def load_piece(sp, l, i):
            src, n = piece_src(l, i)
            dst = ring[:, i % RING, 0:src.shape[1] * n].rearrange("p (k n) -> p k n", n=n)
            sp.dma_start(dst, src).then_inc(slot_in[i % RING], 16)

        sa, sbb = slopes()

        with nc.Block() as block:
            @block.sync
            def _(sp):
                sp.dma_start(x[:], x_in.rearrange("(t p) d -> p t d", p=P)).then_inc(x_in_sem, 16)
                sp.dma_start(tab[:], table_in).then_inc(table_sem, 16)
                sp.dma_start(small[:], small_in[0]).then_inc(small_sem, 16)
                for i in range(RING):
                    load_piece(sp, 0, i)

            @block.vector
            def _(dve):
                nc.vector.memset(pc[:], 0.0)
                nc.vector.memset(vbd[:], 0.0)
                dve.wait_ge(table_sem, 16)
                dist = tab[:, C_DIST:C_DIST + SEQ]
                for h in range(HA):
                    nc.vector.scalar_tensor_tensor(out=cost_a[:, h, :], in0=dist, scalar=sa[h],
                                                   in1=tab[:, C_MA:C_MA + SEQ], op0=ALU.mult, op1=ALU.add)
                for h in range(HB):
                    nc.vector.scalar_tensor_tensor(out=cost_b[:, h, :], in0=dist, scalar=sbb[h],
                                                   in1=tab[:, C_MB:C_MB + SEQ], op0=ALU.mult, op1=ALU.add)
                dve.wait_ge(x_in_sem, 16)

        HEADS = [("a", h) for h in range(HA)] + [("s", h) for h in range(HB)] + [("w", h) for h in range(HB)]
        NHD = len(HEADS)
        TRI = [(0, 0, 0), (1, 0, P), (1, 1, 2 * P)]

        def head_qk(j):
            kind, h = HEADS[j]
            lo = HD * (h % 2)
            if kind == "a":
                return qaT[lo:lo + HD, h // 2, :], kaT[lo:lo + HD, h // 2, :]
            return qbT[lo:lo + HD, h // 2, :], kbT[lo:lo + HD, h // REP, 0 if kind == "s" else 1, :]

        def head_v(j, t):
            kind, h = HEADS[j]
            if kind == "a":
                return va[:, t, h * HD:(h + 1) * HD]
            return vb[:, 0 if kind == "s" else 1, t, (h // REP) * HD:(h // REP + 1) * HD]

        with nc.Fori(0, DEPTH) as l:
            with nc.Block() as block:

                def used(eng, i, j=0):
                    eng.wait_ge(piece_used, PIECES * l + PAIR_PIECES * j + i + 1)

                @block.sync
                def _(sp):
                    def room(n):
                        sp.wait_ge(piece_used, PIECES * l + n + 1 - RING)

                    for i in range(RING, ATT_PIECES):
                        room(i)
                        load_piece(sp, l, i)
                    with sp.Fori(0, PAIRS) as j:
                        for k in range(PAIR_PIECES):
                            i = ATT_PIECES + k
                            sp.wait_ge(piece_used, PIECES * l + PAIR_PIECES * j + i + 1 - RING)
                            w = (w_eg, w_eu, w_ed)[k // 2]
                            sp.dma_start(slot(i, D if k >= E_DOWN else DE),
                                         w[l, 2 * j + k % 2].rearrange("(k p) n -> p k n", p=P)
                                         ).then_inc(slot_in[i % RING], 16)
                    for i in (P_PG, P_PG + 1):
                        room(i)
                        load_piece(sp, l, i)
                    with sp.If(l < DEPTH - 1):
                        for i in range(RING):
                            if i == RING - 2:
                                sp.wait_ge(s["hT_act"], 2 * KT)
                                sp.wait_ge(s["hT_dve"], 2 * KT)
                                sp.wait_ge(s["ple_q"], 4)
                                sp.dma_start(small[:], small_in[(l + 1) % DEPTH]).then_inc(small_sem, 16)
                            sp.wait_ge(piece_used, PIECES * l + PIECES + i + 1 - RING)
                            load_piece(sp, (l + 1) % DEPTH, i)
                    with sp.If(l > DEPTH - 2):
                        sp.dma_start(fgain[:], fgain_in).then_inc(fgain_sem, 16)

                @block.tensor
                def _(pe):
                    mm = nc.tensor.matmul

                    def arrived(i):
                        pe.wait_ge(slot_in[i % RING], 16 * ROUNDS * l + 16 * (i // RING + 1))

                    def turn(event, src):
                        for t in range(TT):
                            if event != HEADS_TURN:
                                pe.wait_ge(s["xn_act" if t else "xn_dve"], 1 if event == 0 else event)
                            for k in range(KT):
                                at = (k % 2) * SEQ + t * P
                                m = nc.tensor.transpose(ps[:, k // 2, at:at + P], src[:, t, k * P:(k + 1) * P], ident)
                                if t == TT - 1 and k % 2 == 1:
                                    m.then_inc(s["turned"], 1)

                    def turned_in(event):
                        pe.wait_ge(s["hT_act"], KT // 2 * (event + 1))
                        pe.wait_ge(s["hT_dve"], KT // 2 * (event + 1))

                    pe.wait_ge(small_sem, 16 * l + 16)
                    turn(0, xn)
                    turned_in(0)

                    def features(bank, c, w, col):
                        for k in range(KT):
                            m = mm(ps[:, bank, c:c + SEQ], w[:, k, col:col + P], hT[:, k, :],
                                   start=(k == 0), stop=(k == KT - 1))
                        return m

                    def tokens(bank, c, w, col, n, t):
                        for k in range(KT):
                            m = mm(ps[:, bank, c:c + n], hT[:, k, t * P:(t + 1) * P], w[:, k, col:col + n],
                                   start=(k == 0), stop=(k == KT - 1))
                        return m

                    arrived(P_KCV)
                    w = slot8(P_KCV)
                    features(4, 0, w, 0)
                    features(4, SEQ, w, P).then_inc(s["kcv_out"], 1)
                    features(5, 0, w, 2 * P)
                    tokens(6, 0, w, 3 * P, P, 0)
                    tokens(6, P, w, 3 * P, P, 1).then_inc(piece_used, 1)
                    arrived(P_QB)
                    w = slot8(P_QB)
                    for i in range(4):
                        m = features(i // 2, (i % 2) * SEQ, w, i * P)
                        if i == 1:
                            m.then_inc(s["qb_out"], 1)
                    m.then_inc(piece_used, 1)
                    arrived(P_KVW)
                    w = slot8(P_KVW, N_IN - KW)
                    features(5, SEQ, w, 0).then_inc(s["kb_out"], 1)
                    NV = P + 3 * HB
                    tokens(7, 0, w, P, NV, 0)
                    tokens(7, NV, w, P, NV, 1).then_inc(piece_used, 1)
                    pe.wait_ge(s["blk_ready"], 4)
                    for w_i, i in ((0, P_CK1), (1, P_CV1)):
                        arrived(i)
                        w = slot(i, CHID)
                        for mt in range(2):
                            c = (w_i * 2 + mt) * KVB * NC
                            for j in range(NJ):
                                m = mm(ps[:, 2, c:c + KVB * NC], w[:, j, mt * P:(mt + 1) * P],
                                       blk[:, w_i, j, :, :].rearrange("p g c -> p (g c)"),
                                       start=(j == 0), stop=(j == NJ - 1))
                        m.then_inc(piece_used, 1)
                    arrived(P_KA)
                    w = slot8(P_KA)
                    for i in range(4):
                        if i == 2:
                            pe.wait_ge(s["kb_act"], 4)
                        m = features(4 + i // 2, (i % 2) * SEQ, w, i * P)
                        if i == 1:
                            m.then_inc(s["ka_out"], 1)
                    m.then_inc(piece_used, 1)
                    arrived(P_QA)
                    w = slot8(P_QA)
                    for i in range(4):
                        if i == 0:
                            pe.wait_ge(s["vs_ready"], 1)
                        if i == 2:
                            pe.wait_ge(s["vw_ready"], 1)
                            pe.wait_ge(s["gate_act"], 1)
                        m = features(6 + i // 2, (i % 2) * SEQ, w, i * P)
                        if i == 1:
                            m.then_inc(s["qa_out"], 1)
                    m.then_inc(piece_used, 1)
                    pe.wait_ge(s["gelu_done"], 1)
                    for mt in range(2):
                        mm(ps[0:HD, 3, 0:KVB * NC], cw2[:, 0, mt, :], hid_g[:, 0, mt, :],
                           start=(mt == 0), stop=(mt == 1))
                    for g in range(KVB):
                        for mt in range(2):
                            m = mm(ps[0:NC, 3, HD + g * HD:2 * HD + g * HD], hid_g[:, 1, mt, g * NC:(g + 1) * NC],
                                   cw2[:, 1, mt, :], start=(mt == 0), stop=(mt == 1))
                    m.then_inc(s["cmp_out"], 1)
                    arrived(P_VA)
                    w = slot8(P_VA)
                    pe.wait_ge(s["qb_dve"], 1)
                    pe.wait_ge(s["qb_act"], 1)
                    tokens(0, 0, w, 0, 512, 0).then_inc(s["va_out"], 1)
                    tokens(1, 0, w, 0, 512, 1).then_inc(piece_used, 1)

                    pe.wait_ge(s["qk_act"], 2)
                    pe.wait_ge(s["qk_dve"], 2)
                    pe.wait_ge(s["kc_ready"], 2)
                    for t in range(TT):
                        for h in range(HB):
                            lo = HD * (h % 2)
                            at = (t * (HB // 2) + h // 2) * CPAD
                            m = mm(ps[:, 6 + h % 2, at:at + NC],
                                   qbT[lo:lo + HD, h // 2, t * P:(t + 1) * P], kcT[lo:lo + HD, h // REP, :],
                                   start=True, stop=True)
                    m.then_inc(s["cscore"], 1)

                    def scores(j):
                        q, k = head_qk(j)
                        if j >= 2:
                            pe.wait_ge(s["costed"], 2 * (j - 1))
                        b = 4 + j % 2
                        mm(ps[:, b, 0:P], q[:, 0:P], k[:, 0:P], start=True, stop=True)
                        mm(ps[:, b, P:3 * P], q[:, P:SEQ], k[:, :], start=True, stop=True).then_inc(s["score"], 1)

                    def turn_weights(j):
                        pe.wait_ge(s["expd"], 2 * (j + 1))
                        if j == 0:
                            pe.wait_ge(s["gelu_x"], 1)
                        if j == 1:
                            pe.wait_ge(s["vc_ready"], 8)
                        if j >= 2:
                            pe.wait_ge(s["prT_act" if j % 2 else "prT_dve"], j // 2)
                        for _, _, c in TRI:
                            m = nc.tensor.transpose(ps[:, 2 + j % 2, c:c + P], pr[:, j % 3, c:c + P], ident)
                        m.then_inc(s["turnedP"], 1)

                    def weigh(j):
                        pe.wait_ge(s["prT_act" if j % 2 else "prT_dve"], j // 2 + 1)
                        if j == 0:
                            pe.wait_ge(s["va_act"], 1)
                            pe.wait_ge(s["va_dve"], 1)
                        if j >= 8 and j % 4 == 0:
                            pe.wait_ge(s["out_even"], j // 4 - 1)
                        b = (j // 4) % 2
                        c = (j % 4) * TT * HD
                        mm(ps[:, b, c:c + HD], prT[:, j % 3, 0:P], head_v(j, 0), start=True, stop=True)
                        mm(ps[:, b, c + HD:c + 2 * HD], prT[:, j % 3, P:2 * P], head_v(j, 0), start=True, stop=False)
                        mm(ps[:, b, c + HD:c + 2 * HD], prT[:, j % 3, 2 * P:3 * P], head_v(j, 1),
                           start=False, stop=True).then_inc(s["summed"], 1)

                    for step in range(NHD + 2):
                        if step < NHD:
                            scores(step)
                        if 1 <= step <= NHD:
                            turn_weights(step - 1)
                        if step >= 2:
                            weigh(step - 2)
                        if step == 5:
                            pe.wait_ge(s["cprob"], 1)
                            for n in range(TT * KVB):
                                m = nc.tensor.transpose(ps[:, 7, n * P:(n + 1) * P],
                                                        pc[:, n // KVB, (n % KVB) * REP:(n % KVB + 1) * REP, :]
                                                        .rearrange("p h c -> p (h c)"), ident)
                            m.then_inc(s["cturn"], 1)
                        if step == 8:
                            pe.wait_ge(s["cturned"], 1)
                            for t in range(TT):
                                for g in range(KVB):
                                    m = mm(ps[:, 6 + t, g * REP * HD:(g + 1) * REP * HD], pcT[:, t * KVB + g, :],
                                           vbd[:, g, :], start=True, stop=True)
                            m.then_inc(s["cout"], 1)

                    pe.wait_ge(s["out_even"], NHD // 4)
                    pe.wait_ge(s["part_added"], 4)
                    turn(HEADS_TURN, xn)
                    turned_in(HEADS_TURN)
                    for half in range(2):
                        arrived(P_WO0 + half)
                        for t in range(TT):
                            tokens(4 + 2 * half + t, 0, slot8(P_WO0 + half), 0, 512, t
                                   ).then_inc(piece_used if t else s["wo_out"], 1)

                    turn(2, xn)
                    turned_in(2)
                    pe.wait_ge(s["x_added"], 4)
                    for t in range(TT):
                        for k in range(KT):
                            mm(ps[:, 4, t * NR:(t + 1) * NR], hT[:, k, t * P:(t + 1) * P], rout[:, k, :],
                               start=(k == 0), stop=False)
                        m = mm(ps[:, 4, t * NR:(t + 1) * NR], tab[0:1, C_ONE:C_ONE + P],
                               small[0:1, SM_RB:SM_RB + NR], start=False, stop=True)
                    m.then_inc(s["routed"], 1)
                    pe.wait_ge(s["rank_in"], 1)
                    lt = tab[:, C_LT:C_LT + P]
                    mm(ps[:, 5, 0:NE], lt, member[:, 0, :], start=True, stop=True)
                    mm(ps[:, 5, NE:2 * NE], ones, member[:, 0, :], start=True, stop=False)
                    mm(ps[:, 5, NE:2 * NE], lt, member[:, 1, :], start=False, stop=True)
                    mm(ps[:, 5, 2 * NE:3 * NE], ones, member[:, 0, :], start=True, stop=False)
                    mm(ps[:, 5, 2 * NE:3 * NE], ones, member[:, 1, :], start=False, stop=True).then_inc(s["ranked"], 1)

                    def gather():
                        for k in range(KT):
                            for t in range(TT):
                                m = mm(ps[:, 2 + k // 4, (k % 4) * P:(k % 4 + 1) * P], xn[:, t, k * P:(k + 1) * P],
                                       pick[:, t, :], start=(t == 0), stop=(t == 1))
                            if k % 4 == 3:
                                m.then_inc(s["gathered"], 1)

                    SCATTER_BANKS = (7, 2, 3, 4)

                    def scatter(n):
                        t, half = n % 2, n // 2
                        mm(ps[:, SCATTER_BANKS[n], :], pickT[:, t, :], y[:, half * 512:(half + 1) * 512],
                           start=True, stop=True).then_inc(s["scattered"], 1)

                    pe.wait_ge(s["picked"], 1)
                    gather()
                    with pe.Fori(0, PAIRS) as j:
                        def got(k):
                            i = ATT_PIECES + k
                            pe.wait_ge(slot_in[i % RING], 16 * ROUNDS * l + 16 * j + 16 * (i // RING + 1))
                            return slot(i, D if k >= E_DOWN else DE)

                        pe.wait_ge(s["xg_ready"], 2 * j + 2)
                        pe.wait_ge(s["pickT_ready"], j + 1)
                        for b, piece in ((0, E_GATE), (1, E_UP)):
                            w2 = [got(piece), got(piece + 1)]
                            for k in range(KT):
                                for a in range(2):
                                    m = mm(ps[a * CAP:(a + 1) * CAP, b, :], xg[:, k, a * CAP:(a + 1) * CAP],
                                           w2[a][:, k, :], start=(k == 0), stop=(k == KT - 1))
                                    if k == KT - 1:
                                        m.then_inc(piece_used, 1)
                        pe.wait_ge(s["picked"], j + 2)
                        pe.wait_ge(s["added"], 4 * j + 1)
                        gather()
                        pe.wait_ge(s["act_ready"], j + 1)
                        for f in range(FT):
                            m = nc.tensor.transpose(ps[:, 4, f * P:(f + 1) * P], act_in[:, f * P:(f + 1) * P], ident)
                        m.then_inc(s["act_turned"], 1)
                        pe.wait_ge(s["y_act"], j + 1)
                        pe.wait_ge(s["y_dve"], j + 1)
                        for n in range(4):
                            if n == 1:
                                pe.wait_ge(s["xg_ready"], 2 * j + 3)
                            if n == 2:
                                pe.wait_ge(s["xg_ready"], 2 * j + 4)
                            if n == 3:
                                pe.wait_ge(s["actT_ready"], j + 1)
                            scatter(n)
                        pe.wait_ge(s["pickw_ready"], j + 1)
                        for t in range(TT):
                            m = nc.tensor.transpose(ps[:, 0, t * P:(t + 1) * P], pickw[:, t, :], ident)
                        m.then_inc(s["pick_turned"], 1)
                        w2 = [got(E_DOWN), got(E_DOWN + 1)]
                        for f in range(FT):
                            for half in range(2):
                                for a in range(2):
                                    m = mm(ps[a * CAP:(a + 1) * CAP, 5 + half, :], actT[:, f, a * CAP:(a + 1) * CAP],
                                           w2[a][:, f, half * 512:(half + 1) * 512],
                                           start=(f == 0), stop=(f == FT - 1))
                                    if f == FT - 1 and half == 1:
                                        m.then_inc(piece_used, 1)
                    pe.wait_ge(s["pickT_ready"], PAIRS + 1)
                    pe.wait_ge(s["y_act"], PAIRS + 1)
                    pe.wait_ge(s["y_dve"], PAIRS + 1)
                    pe.wait_ge(s["added"], 4 * PAIRS + 1)
                    for n in range(4):
                        scatter(n)

                    pe.wait_ge(s["route_done"], 1)
                    with pe.If(pe.value_load(most_i[0:1, 0:1], min_val=0, max_val=SEQ) > CAP):
                        with pe.Fori(0, NG * EPG) as e:
                            for f in range(FT):
                                pe.wait_ge(s["over_ld"], 48 * FT * e + 48 * (f + 1))
                                for b, w in ((0, ow_gate), (1, ow_up)):
                                    features(b, 0, w, 0).then_inc(s["over_g"], 1)
                                pe.wait_ge(s["over_a"], FT * e + f + 1)
                                for t in range(TT):
                                    for half in range(2):
                                        m = mm(ps[:, 2 + 2 * t + half, :], o_a2[:, t * P:(t + 1) * P],
                                               ow_down[:, half * 512:(half + 1) * 512], start=True, stop=True)
                                m.then_inc(s["over_y"], 1)
                        pe.wait_ge(s["over_x"], NG * EPG * FT + 1)
                    pe.wait_ge(s["ple_in"], 16)
                    pe.wait_ge(s["added"], 4 * PAIRS + 5)
                    for half in range(2):
                        for t in range(TT):
                            for k in range(2):
                                m = mm(ps[:, 4 + 2 * half + t, :], pT[:, k, t * P:(t + 1) * P],
                                       ple_w[:, k, half * 512:(half + 1) * 512], start=(k == 0), stop=(k == 1))
                            m.then_inc(s["ple_q"], 1)
                    turn(3, xn)
                    turned_in(3)
                    for half in range(2):
                        arrived(P_PG + half)
                        for t in range(TT):
                            tokens(2 * half + t, 0, slot8(P_PG + half), 0, 512, t
                                   ).then_inc(piece_used if t else s["ple_z"], 1)

                @block.scalar
                def _(act):
                    A = nc.scalar.activation

                    act.wait_ge(small_sem, 16 * l + 16)

                    def norm(n):
                        A(xn[:, 1, :], x[:, 1, :], ACT.Square, accum_out=sq[:, 1:2]).then_inc(s["sq_act"], 1)
                        act.wait_ge(s["rstd_ready"], n + 1)
                        A(xn[:, 1, :], x[:, 1, :], ACT.Copy, scale=rstd[:, 1:2]).then_inc(s["xn_act"], 1)

                    def evac_turned(event, g):
                        for b in (0, 2):
                            act.wait_ge(s["turned"], 4 * event + b + 1)
                            for k in (2 * b, 2 * b + 1):
                                A(hT[:, k, :], ps[:, b, (k % 2) * SEQ:(k % 2 + 1) * SEQ], ACT.Copy,
                                  scale=1.0 if g is None else gain(g, k)).then_inc(s["hT_act"], 1)

                    norm(0)
                    evac_turned(0, 0)
                    used(act, P_KCV)
                    A(vb[:, 0, :, :], ps[:, 6, 0:SEQ].rearrange("p (t n) -> p t n", t=TT), ACT.Copy
                      ).then_inc(s["vs_ready"], 1)
                    used(act, P_QB)
                    A(qbT[:, 2:4, :], ps[:, 1, :].rearrange("p (i n) -> p i n", i=2), ACT.Copy,
                      scale=-(HD ** -0.5)).then_inc(s["qb_act"], 1)
                    act.wait_ge(s["kb_out"], 1)
                    for g in range(KVB):
                        for lo in (0, HD):
                            A(kbT[lo:lo + HD, g, :, :],
                              ps[g * HD:(g + 1) * HD, 5, :].rearrange("p (w n) -> p w n", w=2),
                              ACT.Copy).then_inc(s["kb_act"], 1)
                    used(act, P_KVW)
                    NV = P + 3 * HB
                    A(gate[:], ps[:, 7, 0:2 * NV].rearrange("p (t n) -> p t n", t=TT)[:, :, P:NV], ACT.Tanh,
                      scale=0.5).then_inc(s["gate_act"], 1)
                    act.wait_ge(s["gelu_t"], 1)
                    A(hid_u, hid_u, ACT.Tanh, scale=GELU_C).then_inc(s["gelu_t"], 1)
                    act.wait_ge(s["ka_out"], 1)
                    A(kaT[:, 0:2, :], ps[:, 4, :].rearrange("p (i n) -> p i n", i=2), ACT.Copy
                      ).then_inc(s["qk_act"], 1)
                    act.wait_ge(s["qa_out"], 1)
                    A(qaT[:, 0:2, :], ps[:, 6, :].rearrange("p (i n) -> p i n", i=2), ACT.Copy,
                      scale=-(HD ** -0.5)).then_inc(s["qk_act"], 1)
                    act.wait_ge(s["cmp_out"], 1)
                    for lo in (0, HD):
                        A(kcT[lo:lo + HD, :, :], ps[0:HD, 3, 0:KVB * NC].rearrange("p (g c) -> p g c", g=KVB),
                          ACT.Copy).then_inc(s["kc_ready"], 1)
                    act.wait_ge(s["va_out"], 1)
                    A(va[:, 0, :], ps[:, 0, :], ACT.Copy).then_inc(s["va_act"], 1)

                    def weights(j):
                        for t in range(TT):
                            act.wait_ge(s["costed"], 2 * j + t + 1)
                            if j >= 3 and t == 0:
                                act.wait_ge(s["turnedP"], j - 2)
                            c, n = (0, P) if t == 0 else (P, SEQ)
                            A(pr[:, j % 3, c:c + n], cost[:, j % 2, c:c + n], ACT.Exp, scale=-1.0,
                              bias=low[:, j, t:t + 1], accum_out=den[:, j, t:t + 1]).then_inc(s["expd"], 1)

                    def evac_weights(j):
                        act.wait_ge(s["turnedP"], j + 1)
                        if j >= 3:
                            act.wait_ge(s["summed"], j - 2)
                        A(prT[:, j % 3, :], ps[:, 2 + j % 2, 0:3 * P], ACT.Copy).then_inc(s["prT_act"], 1)

                    for step in range(NHD + 1):
                        if step >= 1 and (step - 1) % 2 == 1:
                            evac_weights(step - 1)
                        if step < NHD:
                            weights(step)
                        if step == 2:
                            act.wait_ge(s["cexp_in"], 1)
                            A(cs[:], cs[:], ACT.Exp, scale=-1.0).then_inc(s["cexp"], 1)
                        if step == 6:
                            act.wait_ge(s["cturn"], 1)
                            A(pcT[:], ps[:, 7, :].rearrange("p (n q) -> p n q", q=P), ACT.Copy
                              ).then_inc(s["cturned"], 1)
                    evac_turned(HEADS_TURN, None)
                    act.wait_ge(s["wo_out"], 1)
                    act.dma_start(ple_w[:], w_pp[l].rearrange("(k p) n -> p k n", p=P)).then_inc(s["ple_in"], 16)

                    act.wait_ge(s["x_added"], 4)
                    norm(1)
                    evac_turned(2, 1)
                    act.wait_ge(s["gexp_in"], 1)
                    A(r_x[:], r_x[:], ACT.Exp).then_inc(s["gexp"], 1)
                    act.wait_ge(s["eexp_in"], 1)
                    A(ex[:], ex[:], ACT.Exp).then_inc(s["eexp"], 1)

                    with act.Fori(0, PAIRS) as j:
                        used(act, ATT_PIECES + E_GATE + 1, j)
                        A(th, ps[:, 0, :], ACT.Tanh, scale=0.5).then_inc(s["th_ready"], 1)
                        act.wait_ge(s["act_turned"], j + 1)
                        A(actT[:], ps[:, 4, :].rearrange("p (f n) -> p f n", f=FT), ACT.Copy
                          ).then_inc(s["actT_ready"], 1)
                        act.wait_ge(s["pick_turned"], j + 1)
                        A(pickT[:], ps[:, 0, 0:TT * P].rearrange("p (t n) -> p t n", t=TT), ACT.Copy
                          ).then_inc(s["pickT_ready"], 1)
                        used(act, ATT_PIECES + E_DOWN + 1, j)
                        A(y[:, 0:512], ps[:, 5, :], ACT.Copy).then_inc(s["y_act"], 1)

                    act.wait_ge(s["route_done"], 1)
                    with act.If(act.value_load(most_i[0:1, 0:1], min_val=0, max_val=SEQ) > CAP):
                        with act.Fori(0, NG * EPG) as e:
                            for f in range(FT):
                                act.wait_ge(s["over_x"], FT * e + f + 1)
                                for dst, w in ((ow_gate, w_eg), (ow_up, w_eu)):
                                    act.dma_start(dst, w[l, e, :, f * P:(f + 1) * P].rearrange("(k p) n -> p k n", p=P)
                                                  ).then_inc(s["over_ld"], 16)
                                act.dma_start(ow_down, w_ed[l, e, f * P:(f + 1) * P, :]).then_inc(s["over_ld"], 16)
                                act.wait_ge(s["over_g"], 2 * FT * e + 2 * f + 1)
                                A(o_th, ps[:, 0, 0:SEQ], ACT.Tanh, scale=0.5).then_inc(s["over_t"], 1)
                        act.wait_ge(s["over_x"], NG * EPG * FT + 1)
                    act.wait_ge(s["added"], 4 * PAIRS + 5)
                    norm(2)
                    evac_turned(3, 2)
                    for n in range(4):
                        if n % 2:
                            used(act, P_PG + n // 2)
                        else:
                            act.wait_ge(s["ple_z"], n // 2 + 1)
                        if n >= 2:
                            act.wait_ge(s["ple_x"], n - 1)
                        A(pth[:, n % 2, :], ps[:, n, :], ACT.Tanh, scale=0.5).then_inc(s["ple_th"], 1)

                @block.gpsimd
                def _(pool):
                    def inverse_rms(n):
                        pool.wait_ge(s["ms_ready"], n + 1)
                        nc.gpsimd.tensor_tensor(rstd[:], sq[:], tab[:, C_POW:C_POW + TT], ALU.pow
                                                ).then_inc(s["rstd_ready"], 1)

                    inverse_rms(0)
                    for m in range(4):
                        pool.wait_ge(s["out_even"], m + 3)
                        if m == 0:
                            pool.wait_ge(s["ocmp"], 2)
                        if m >= 1:
                            pool.wait_ge(s["part_added"], m)
                        o = xn[:, :, 512 + (m % 2) * 256:768 + (m % 2) * 256]
                        nc.gpsimd.tensor_tensor(
                            o, o, part[:, m % 2, :].rearrange("p (t n) -> p t n", t=TT), ALU.add
                        ).then_inc(s["part_added"], 1)
                    pool.wait_ge(s["wo_out"], 1)
                    nc.gpsimd.memset(y[:, 0:512], 0.0).then_inc(s["y_act"], 1)
                    nc.gpsimd.memset(y[:, 512:1024], 0.0).then_inc(s["y_dve"], 1)
                    nc.gpsimd.memset(pickT[:], 0.0).then_inc(s["pickT_ready"], 1)
                    inverse_rms(1)
                    inverse_rms(2)

                @block.vector
                def _(dve):
                    V = nc.vector
                    c = Chain(dve, s["chain_dve"])

                    def norm(n):
                        V.tensor_tensor_reduce(xn[:, 0, :], x[:, 0, :], x[:, 0, :], 1.0, 0.0, ALU.mult, ALU.add,
                                               sq[:, 0:1]).then_inc(s["sq_dve"], 1)
                        dve.wait_ge(s["sq_dve"], n + 1)
                        dve.wait_ge(s["sq_act"], n + 1)
                        V.tensor_scalar(sq[:], sq[:], 1.0 / D, EPS, ALU.mult, ALU.add).then_inc(s["ms_ready"], 1)
                        dve.wait_ge(s["rstd_ready"], n + 1)
                        V.tensor_scalar(xn[:, 0, :], x[:, 0, :], rstd[:, 0:1], None, ALU.mult).then_inc(s["xn_dve"], 1)

                    def evac_turned(event, g):
                        for b in (1, 3):
                            dve.wait_ge(s["turned"], 4 * event + b + 1)
                            for k in (2 * b, 2 * b + 1):
                                src = ps[:, b, (k % 2) * SEQ:(k % 2 + 1) * SEQ]
                                ins = (V.tensor_copy(hT[:, k, :], src) if g is None else
                                       V.tensor_scalar(hT[:, k, :], src, gain(g, k), None, ALU.mult))
                                ins.then_inc(s["hT_dve"], 1)

                    dve.wait_ge(small_sem, 16 * l + 16)
                    norm(0)
                    evac_turned(0, 0)
                    dve.wait_ge(s["kcv_out"], 1)
                    for g in range(KVB):
                        for half in range(2):
                            lo = half * HD
                            kv = ps[g * HD:(g + 1) * HD, 4, :].rearrange("p (w n) -> p w n", w=2)
                            for w_i in range(2):
                                src = bass.AP(kv.tensor, kv.offset + w_i * SEQ + half,
                                              [list(kv.ap[0]), [2, NJ], [CSTR, NC]])
                                add = pos2[lo:lo + HD, w_i, :].unsqueeze(2).to_broadcast([HD, NJ, NC])
                                ins = V.tensor_tensor(blk[lo:lo + HD, w_i, :, g, :], src, add, ALU.add)
                            ins.then_inc(s["blk_ready"], 1)
                    dve.wait_ge(s["qb_out"], 1)
                    V.tensor_scalar(qbT[:, 0:2, :], ps[:, 0, :].rearrange("p (i n) -> p i n", i=2), -(HD ** -0.5),
                                    None, ALU.mult).then_inc(s["qb_dve"], 1)
                    used(dve, P_KVW)
                    NV = P + 3 * HB
                    dve.wait_ge(s["gate_act"], 1)
                    V.tensor_copy(vb[:, 1, :, :], ps[:, 7, 0:2 * NV].rearrange("p (t n) -> p t n", t=TT)[:, :, 0:P]
                                  ).then_inc(s["vw_ready"], 1)
                    V.tensor_scalar(gate[:], gate[:], 0.5, 0.5, ALU.mult, ALU.add).then_inc(s["gate_dve"], 1)
                    used(dve, P_CV1)
                    V.tensor_copy(hid, ps[:, 2, 0:NH]).then_inc(s["gelu_x"], 1)
                    dve.wait_ge(s["gelu_x"], 1)
                    c.add(V.tensor_tensor(hid_u, hid, hid, ALU.mult))
                    c.wait()
                    c.add(V.tensor_scalar(hid_u, hid_u, 0.044715, 1.0, ALU.mult, ALU.add))
                    c.wait()
                    V.tensor_tensor(hid_u, hid_u, hid, ALU.mult).then_inc(s["gelu_t"], 1)
                    dve.wait_ge(s["gelu_t"], 2)
                    c.add(V.scalar_tensor_tensor(out=hid_u, in0=hid_u, scalar=1.0, in1=hid, op0=ALU.add, op1=ALU.mult))
                    c.wait()
                    V.tensor_scalar(hid_g.rearrange("p w m n -> p (w m n)"), hid_u, 0.5, None,
                                    ALU.mult).then_inc(s["gelu_done"], 1)
                    used(dve, P_KA)
                    V.tensor_copy(kaT[:, 2:4, :], ps[:, 5, :].rearrange("p (i n) -> p i n", i=2)
                                  ).then_inc(s["qk_dve"], 1)
                    used(dve, P_QA)
                    V.tensor_scalar(qaT[:, 2:4, :], ps[:, 7, :].rearrange("p (i n) -> p i n", i=2), -(HD ** -0.5),
                                    None, ALU.mult).then_inc(s["qk_dve"], 1)
                    dve.wait_ge(s["kc_ready"], 2)
                    for g in range(KVB):
                        for h in range(REP):
                            V.tensor_copy(vbd[h * CPAD:h * CPAD + NC, g, h * HD:(h + 1) * HD],
                                          ps[0:NC, 3, HD + g * HD:2 * HD + g * HD]).then_inc(s["vc_ready"], 1)
                    used(dve, P_VA)
                    V.tensor_copy(va[:, 1, :], ps[:, 1, :]).then_inc(s["va_dve"], 1)

                    def add_cost(j):
                        kind, h = HEADS[j]
                        tb = cost_a if kind == "a" else cost_b
                        dve.wait_ge(s["score"], j + 1)
                        if j >= 2:
                            dve.wait_ge(s["expd"], 2 * (j - 1))
                        for t in range(TT):
                            lo, n = (0, P) if t == 0 else (P, SEQ)
                            V.tensor_tensor_reduce(cost[:, j % 2, lo:lo + n], ps[:, 4 + j % 2, lo:lo + n],
                                                   tb[:, h, SEQ - n:SEQ], 1.0, 3.0e38, ALU.add, ALU.min,
                                                   low[:, j, t:t + 1]).then_inc(s["costed"], 1)

                    def evac_weights(j):
                        dve.wait_ge(s["turnedP"], j + 1)
                        if j >= 3:
                            dve.wait_ge(s["summed"], j - 2)
                        V.tensor_copy(prT[:, j % 3, :], ps[:, 2 + j % 2, 0:3 * P]).then_inc(s["prT_dve"], 1)

                    def finish_heads(m):
                        j0 = 4 * m
                        dve.wait_ge(s["expd"], 2 * (j0 + 4))
                        c.add(V.reciprocal(wgt[:, j0:j0 + 4, :], den[:, j0:j0 + 4, :]))
                        c.wait()
                        kind, h0 = HEADS[j0]
                        if kind != "a":
                            br = 1 if kind == "s" else 2
                            gt = gate[:].rearrange("p t (h b) -> p h b t", b=3)[:, h0:h0 + 4, br, :]
                            c.add(V.tensor_tensor(wgt[:, j0:j0 + 4, :], wgt[:, j0:j0 + 4, :], gt, ALU.mult))
                            c.wait()
                        dve.wait_ge(s["summed"], j0 + 4)
                        if m >= 4:
                            dve.wait_ge(s["part_added"], m - 3)
                        if kind == "a":
                            dst = xn[:, :, h0 * HD:(h0 + 4) * HD].rearrange("p t (i d) -> p i t d", i=4)
                        else:
                            dst = part[:, m % 2, :].rearrange("p (t i d) -> p i t d", t=TT, i=4)
                        V.tensor_tensor(dst, ps[:, m % 2, :].rearrange("p (i t d) -> p i t d", i=4, t=TT),
                                        wgt[:, j0:j0 + 4, :].unsqueeze(3).to_broadcast([P, 4, TT, HD]),
                                        ALU.mult).then_inc(s["out_even"], 1)

                    cost_c = tab[:, C_CC:C_CC + TT * HB * NC].rearrange("p (b n c) -> p b n c", b=2, c=NC)
                    valid_c = tab[:, C_CV:C_CV + TT * NC].rearrange("p (t c) -> p t c", t=TT)
                    for step in range(NHD + 3):
                        if step < NHD:
                            add_cost(step)
                        if 1 <= step <= NHD and (step - 1) % 2 == 0:
                            evac_weights(step - 1)
                        if step >= 3 and (step - 3) % 4 == 3:
                            finish_heads((step - 3) // 4)
                        if step == 1:
                            dve.wait_ge(s["cscore"], 1)
                            c.add(V.tensor_tensor(cz[:].rearrange("p (b n) c -> p b n c", b=2), ps[:, 6:8, 0:TT * REP * CPAD].rearrange("p b (n c) -> p b n c", c=CPAD)[:, :, :, 0:NC],
                                                  cost_c, ALU.add))
                            c.wait()
                            c.add(V.tensor_reduce(clow, cz[:], AX.X, ALU.min))
                            c.wait()
                            V.tensor_tensor(cs[:], cz[:], clow.unsqueeze(2).to_broadcast([P, TT * HB, NC]),
                                            ALU.subtract).then_inc(s["cexp_in"], 1)
                        if step == 3:
                            dve.wait_ge(s["cexp"], 1)
                            c.add(V.tensor_reduce(cden, cs[:], AX.X, ALU.add))
                            for t in range(TT):
                                ins = V.tensor_tensor(pc[:, t, :, 0:NC].rearrange("p (i b) c -> p b i c", b=2),
                                                      cs[:].rearrange("p (b t i) c -> p b t i c", b=2, t=TT)[:, :, t, :, :],
                                                      valid_c[:, t, :].unsqueeze(1).unsqueeze(1)
                                                      .to_broadcast([P, 2, HB // 2, NC]), ALU.mult)
                            ins.then_inc(s["cprob"], 1)
                            c.wait()
                            c.add(V.reciprocal(cw, cden))
                            c.wait()
                            dve.wait_ge(s["gate_dve"], 1)
                            gt = gate[:].rearrange("p t (i q b) -> p q t i b", q=2, b=3)[:, :, :, :, 0]
                            cwv = cw.rearrange("p (q t i) -> p q t i", q=2, t=TT)
                            c.add(V.tensor_tensor(cwv, cwv, gt, ALU.mult))
                        if step == 10:
                            dve.wait_ge(s["cout"], 1)
                            c.wait()
                            for t in range(TT):
                                cwt = cw.rearrange("p (q t i) -> p i q t", q=2, t=TT)[:, :, :, t]
                                V.tensor_tensor(xn[:, t, 512:1024].rearrange("p (i q d) -> p i q d", q=2, d=HD),
                                                ps[:, 6 + t, :].rearrange("p (i q d) -> p i q d", q=2, d=HD),
                                                cwt.unsqueeze(3).to_broadcast([P, HB // 2, 2, HD]),
                                                ALU.mult).then_inc(s["ocmp"], 1)
                    evac_turned(HEADS_TURN, None)
                    for n in range(4):
                        half, t = n // 2, n % 2
                        if t:
                            used(dve, P_WO0 + half)
                        else:
                            dve.wait_ge(s["wo_out"], half + 1)
                        xs = x[:, t, half * 512:(half + 1) * 512]
                        V.tensor_tensor(xs, xs, ps[:, 4 + n, :], ALU.add).then_inc(s["x_added"], 1)

                    dve.wait_ge(s["x_added"], 4)
                    norm(1)
                    evac_turned(2, 1)
                    tie = tab[:, C_TIE:C_TIE + 4].unsqueeze(1).to_broadcast([P, TT, 4])

                    def wide(v):
                        return v.unsqueeze(2).to_broadcast([P, TT, 4])

                    def do(ins):
                        c.add(ins)
                        c.wait()

                    dve.wait_ge(s["routed"], 1)
                    do(V.tensor_copy(lg[:], ps[:, 4, 0:TT * NR].rearrange("p (t n) -> p t n", t=TT)))
                    glog = lg[:, :, 0:NG]
                    do(V.tensor_reduce(r_m, glog, AX.X, ALU.max))
                    V.tensor_tensor(r_x[:], glog, wide(r_m), ALU.subtract).then_inc(s["gexp_in"], 1)
                    do(V.tensor_tensor(r_e[:], glog, wide(r_m), ALU.is_equal))
                    do(V.tensor_tensor(r_w[:], r_e[:], tie, ALU.mult))
                    do(V.tensor_reduce(r_wm, r_w[:], AX.X, ALU.max))
                    do(V.tensor_tensor(onehot[:], r_w[:], wide(r_wm), ALU.is_equal))
                    big = r_big.rearrange("p (t e g) -> p t e g", t=TT, e=EPG)
                    for t in range(TT):
                        ins = V.tensor_tensor(big[:, t, :, :],
                                              lg[:, t, NG:NR].rearrange("p (g e) -> p e g", g=NG),
                                              onehot[:, t, :].unsqueeze(1).to_broadcast([P, EPG, NG]), ALU.mult)
                    do(ins)
                    do(V.tensor_reduce(within[:], big, AX.X, ALU.add))
                    gt = r_gt.rearrange("p (t e g) -> p t e g", t=TT, e=EPG)
                    other = within[:].unsqueeze(2).to_broadcast([P, TT, EPG, EPG])
                    own = within[:].unsqueeze(3).to_broadcast([P, TT, EPG, EPG])
                    tri = (tab[:, C_TRI:C_TRI + 16].rearrange("p (e g) -> p e g", e=EPG).unsqueeze(1)
                           .to_broadcast([P, TT, EPG, EPG]))
                    V.tensor_tensor(gt, other, own, ALU.is_gt)
                    do(V.tensor_tensor(big, other, own, ALU.is_equal))
                    do(V.tensor_tensor(big, big, tri, ALU.mult))
                    do(V.tensor_tensor(big, big, gt, ALU.add))
                    do(V.tensor_reduce(above[:], big, AX.X, ALU.add))
                    do(V.tensor_scalar(chosen[:], above[:], 2.0, None, ALU.is_lt))
                    for t in range(TT):
                        ins = V.tensor_tensor(member[:, t, :].rearrange("p (g e) -> p g e", g=NG),
                                              onehot[:, t, :].unsqueeze(2).to_broadcast([P, NG, EPG]),
                                              chosen[:, t, :].unsqueeze(1).to_broadcast([P, NG, EPG]), ALU.mult)
                    ins.then_inc(s["rank_in"], 1)
                    do(V.tensor_reduce(top, within[:], AX.X, ALU.max))
                    V.tensor_tensor(ex[:], within[:], wide(top), ALU.subtract).then_inc(s["eexp_in"], 1)
                    V.memset(slot_of[:, :, NE:NE + 2], -1.0)
                    V.memset(weight[:, :, NE:NE + 2], 0.0)
                    dve.wait_ge(s["gexp"], 1)
                    do(V.tensor_reduce(gsum, r_x[:], AX.X, ALU.add))
                    do(V.reciprocal(gw, gsum))
                    dve.wait_ge(s["ranked"], 1)
                    do(V.scalar_tensor_tensor(out=slot_of[:, :, 0:NE],
                                              in0=ps[:, 5, 0:2 * NE].rearrange("p (t n) -> p t n", t=TT),
                                              scalar=1.0, in1=member[:], op0=ALU.add, op1=ALU.mult))
                    do(V.tensor_scalar(slot_of[:, :, 0:NE], slot_of[:, :, 0:NE], -1.0, None, ALU.add))

                    iota = tab[:, C_IOTA:C_IOTA + CAP]

                    def column(v, t, j, a):
                        return v[:, t, a:a + 1] if isinstance(j, int) and j == 0 else v[:, t, bass.ds(2 * j + a, 1)]

                    def make_pick(j):
                        for t in range(TT):
                            for a in range(2):
                                ins = V.tensor_scalar(pick[:, t, a * CAP:(a + 1) * CAP], iota,
                                                      column(slot_of, t, j, a), None, ALU.is_equal)
                        ins.then_inc(s["picked"], 1)

                    def make_pickw(j):
                        for t in range(TT):
                            for a in range(2):
                                ins = V.tensor_scalar(pickw[:, t, a * CAP:(a + 1) * CAP], iota,
                                                      column(slot_of, t, j, a), column(weight, t, j, a),
                                                      ALU.is_equal, ALU.mult)
                        ins.then_inc(s["pickw_ready"], 1)

                    def evac_gathered(n):
                        for b in range(2):
                            dve.wait_ge(s["gathered"], n + b)
                            V.tensor_tensor(xg[:, b * 4:b * 4 + 4, :],
                                            ps[:, 2 + b, :].rearrange("p (k n) -> p k n", k=4),
                                            gain(1, b * 4, 4).unsqueeze(2).to_broadcast([P, 4, P]),
                                            ALU.mult).then_inc(s["xg_ready"], 1)

                    def add_scattered(n0):
                        for n in range(4):
                            t, half = n % 2, n // 2
                            dve.wait_ge(s["scattered"], n0 + n)
                            xs = x[:, t, half * 512:(half + 1) * 512]
                            V.tensor_tensor(xs, xs, ps[:, (7, 2, 3, 4)[n], :], ALU.add).then_inc(s["added"], 1)

                    make_pick(0)
                    do(V.tensor_reduce(most, ps[:, 5, 2 * NE:3 * NE], AX.X, ALU.max))
                    V.tensor_copy(most_i[:], most).then_inc(s["route_done"], 1)
                    dve.wait_ge(s["eexp"], 1)
                    do(V.tensor_tensor(ex[:], ex[:], chosen[:], ALU.mult))
                    do(V.tensor_reduce(esum, ex[:], AX.X, ALU.add))
                    do(V.reciprocal(esum, esum))
                    do(V.scalar_tensor_tensor(out=esum, in0=esum, scalar=0.5, in1=gw, op0=ALU.mult, op1=ALU.mult))
                    do(V.tensor_tensor(ex[:], ex[:], wide(esum), ALU.mult))
                    for t in range(TT):
                        ins = V.tensor_tensor(weight[:, t, 0:NE].rearrange("p (g e) -> p g e", g=NG),
                                              onehot[:, t, :].unsqueeze(2).to_broadcast([P, NG, EPG]),
                                              ex[:, t, :].unsqueeze(1).to_broadcast([P, NG, EPG]), ALU.mult)
                    ins.then_inc(s["added"], 1)
                    dve.wait_ge(s["added"], 1)
                    make_pickw(0)
                    evac_gathered(1)
                    base = c.n
                    with dve.Fori(0, PAIRS) as j:
                        cj = Chain(dve, s["chain_dve"], 0, base + j)
                        make_pick(j + 1)
                        dve.wait_ge(s["th_ready"], j + 1)
                        cj.add(V.scalar_tensor_tensor(out=a1, in0=th, scalar=1.0, in1=ps[:, 0, :],
                                                      op0=ALU.add, op1=ALU.mult))
                        used(dve, ATT_PIECES + E_UP + 1, j)
                        cj.wait()
                        V.tensor_tensor(act_in, a1, ps[:, 1, :], ALU.mult).then_inc(s["act_ready"], 1)
                        evac_gathered(2 * j + 3)
                        add_scattered(4 * j + 1)
                        used(dve, ATT_PIECES + E_DOWN + 1, j)
                        V.tensor_copy(y[:, 512:1024], ps[:, 6, :]).then_inc(s["y_dve"], 1)
                        make_pickw(j + 1)
                    c.n += PAIRS
                    add_scattered(4 * PAIRS + 1)

                    dve.wait_ge(s["added"], 4 * PAIRS + 5)
                    with dve.If(dve.value_load(most_i[0:1, 0:1], min_val=0, max_val=SEQ) > CAP):
                        co = Chain(dve, s["over_l"])
                        co.add(V.tensor_scalar(over_w[:], slot_of[:, :, 0:NE], float(CAP), None, ALU.is_ge))
                        co.wait()
                        V.tensor_tensor(over_w[:], over_w[:], weight[:, :, 0:NE], ALU.mult).then_inc(s["over_x"], 1)
                        dve.wait_ge(s["over_x"], 1)
                        with dve.Fori(0, NG * EPG) as e:
                            ce = Chain(dve, s["over_l"], 0, co.n + FT * e)
                            for f in range(FT):
                                dve.wait_ge(s["over_t"], FT * e + f + 1)
                                ce.add(V.scalar_tensor_tensor(out=o_a1, in0=o_th, scalar=1.0, in1=ps[:, 0, 0:SEQ],
                                                              op0=ALU.add, op1=ALU.mult))
                                ce.wait()
                                dve.wait_ge(s["over_g"], 2 * FT * e + 2 * f + 2)
                                V.tensor_tensor(o_a2, o_a1, ps[:, 1, 0:SEQ], ALU.mult).then_inc(s["over_a"], 1)
                                dve.wait_ge(s["over_y"], FT * e + f + 1)
                                for t in range(TT):
                                    for half in range(2):
                                        xs = x[:, t, half * 512:(half + 1) * 512]
                                        ins = V.scalar_tensor_tensor(
                                            out=xs, in0=ps[:, 2 + 2 * t + half, :],
                                            scalar=over_w[:, t, bass.ds(e, 1)], in1=xs, op0=ALU.mult, op1=ALU.add)
                                ins.then_inc(s["over_x"], 1)
                        dve.wait_ge(s["over_x"], NG * EPG * FT + 1)
                    norm(2)
                    evac_turned(3, 2)
                    for n in range(4):
                        half, t = n // 2, n % 2
                        dve.wait_ge(s["ple_th"], n + 1)
                        dve.wait_ge(s["ple_q"], 4)
                        do(V.scalar_tensor_tensor(out=pv[:, n % 2, :], in0=pth[:, n % 2, :], scalar=1.0,
                                                  in1=ps[:, 4 + n, :], op0=ALU.add, op1=ALU.mult))
                        xs = x[:, t, half * 512:(half + 1) * 512]
                        V.scalar_tensor_tensor(out=xs, in0=pv[:, n % 2, :], scalar=0.5, in1=xs, op0=ALU.mult,
                                               op1=ALU.add).then_inc(s["ple_x"], 1)

            nc.sync.sem_clear(range(nums[0], nums[-1] + 1))
            nc.all_engine_barrier()

        with nc.Block() as block:
            @block.gpsimd
            def _(pool):
                pool.wait_ge(s["ms_ready"], 1)
                nc.gpsimd.tensor_tensor(rstd[:], sq[:], tab[:, C_POW:C_POW + TT], ALU.pow
                                        ).then_inc(s["rstd_ready"], 1)

            @block.scalar
            def _(act):
                nc.scalar.activation(xn[:, 1, :], x[:, 1, :], ACT.Square, accum_out=sq[:, 1:2]
                                     ).then_inc(s["sq_act"], 1)

            @block.vector
            def _(dve):
                V = nc.vector
                dve.wait_ge(fgain_sem, 16)
                c = Chain(dve, s["chain_dve"])
                c.add(V.tensor_tensor_reduce(xn[:, 0, :], x[:, 0, :], x[:, 0, :], 1.0, 0.0, ALU.mult, ALU.add,
                                             sq[:, 0:1]))
                c.wait()
                dve.wait_ge(s["sq_act"], 1)
                V.tensor_scalar(sq[:], sq[:], 1.0 / D, EPS, ALU.mult, ALU.add).then_inc(s["ms_ready"], 1)
                dve.wait_ge(s["rstd_ready"], 1)
                for t in range(TT):
                    V.scalar_tensor_tensor(out=xn[:, t, :], in0=x[:, t, :], scalar=rstd[:, t:t + 1], in1=fgain[:],
                                           op0=ALU.mult, op1=ALU.mult).then_inc(s["xn_dve"], 1)

            @block.sync
            def _(sp):
                o = out.rearrange("(t p) d -> p t d", p=P)
                for t in range(TT):
                    sp.wait_ge(s["xn_dve"], t + 1)
                    sp.dma_start(o[:, t, :], xn[:, t, :]).then_inc(out_sem, 16)
                sp.wait_ge(out_sem, 16 * TT)


def kernel(x, p, attn_norm, w_in, w_out, w_cmp_k1, w_cmp_k2, w_cmp_v1, w_cmp_v2, cmp_pos,
           ffn_norm, w_route_group, b_route_group, w_route_expert, b_route_expert,
           w_expert_gate, w_expert_up, w_expert_down, ple_norm, w_ple_gate, w_ple_proj, final_norm):
    import numpy as _np
    import concourse.bacc as _bacc
    from concourse import mybir as _mybir
    from concourse.bass_utils import run_bass_kernel_spmd as _run

    A = _np.asarray

    def columns(a):
        a = A(a)
        d, r, n = a.shape
        return a.reshape(d, r // P, P, n).transpose(0, 2, 1, 3).reshape(d, P, -1)

    bias = _np.zeros((DEPTH, P, NR), _np.float32)
    bias[:, 0, :NG] = A(b_route_group)
    bias[:, 0, NG:] = A(b_route_expert)
    pos = A(cmp_pos).reshape(DEPTH, 2, CBLK // 2, 2, HD).transpose(0, 3, 4, 1, 2).reshape(DEPTH, P, -1)
    router = _np.concatenate([A(w_route_group), A(w_route_expert)], axis=2)
    small = _np.concatenate(
        [columns(A(g)[:, :, None]) for g in (attn_norm, ffn_norm, ple_norm)]
        + [pos, columns(w_cmp_k2), columns(w_cmp_v2), columns(router), bias,
           columns(A(p)[:, 0].transpose(0, 2, 1))], axis=2)
    arrays = {
        "x_rows": A(x)[0], "small": small, "tables": tables(),
        "final_rows": _np.broadcast_to(A(final_norm)[None, :], (P, D)),
        "w_in": A(w_in), "w_out": A(w_out), "w_cmp_k1": A(w_cmp_k1), "w_cmp_v1": A(w_cmp_v1),
        "w_expert_gate": A(w_expert_gate), "w_expert_up": A(w_expert_up), "w_expert_down": A(w_expert_down),
        "w_ple_gate": A(w_ple_gate), "w_ple_proj": A(w_ple_proj),
    }
    arrays = {k: _np.ascontiguousarray(v) for k, v in arrays.items()}
    nc = _bacc.Bacc("TRN2", target_bir_lowering=False, num_devices=1)
    args = [nc.dram_tensor(k + "_dram", v.shape, _mybir.dt.from_np(v.dtype), kind="ExternalInput").ap()
            for k, v in arrays.items()]
    args.append(nc.dram_tensor("out_dram", (SEQ, D), _mybir.dt.float32, kind="ExternalOutput").ap())
    build_trunk(nc, *args)
    r = _run(nc, [{k + "_dram": v for k, v in arrays.items()}], core_ids=[0])
    return r.results[0]["out_dram"].reshape(1, SEQ, D)
```

```python
import math
from contextlib import ExitStack

import numpy as np

import concourse.bass as bass
from concourse import mybir

F32 = mybir.dt.float32
I32 = mybir.dt.int32
ALU = mybir.AluOpType
ACT = mybir.ActivationFunctionType
AX = mybir.AxisListType

P = 128
DEPTH, SEQ, D = 2, 256, 1024
TT = SEQ // P
KT = D // P
HD = 64
HA, HB, KVB = 8, 8, 2
REP = HB // KVB
PLE = 256
NG, EPG, DE = 4, 4, 512
FT = DE // P
NR = NG + NG * EPG
CBLK, CSTR, CHID = 32, 16, 256
NC = (SEQ - CBLK) // CSTR + 1
CPAD = 32
CG = 16
CAP = 64
NE = NG * EPG
PAIRS = NE // 2
EPS = 1e-6
HUGE = 1e30
GELU_C = math.sqrt(2.0 / math.pi)

QA, KA, VA, QB = 0, 512, 1024, 1536
KC = 2048
KW = KC + 512
N_IN = KW + 2 * P + 3 * HB

RING = 6
SLOT = 4096
ATT_PIECES = 10
PAIR_PIECES = 6
PIECES = ATT_PIECES + PAIRS * PAIR_PIECES + 2
IN_RING = PIECES - 2
EARLY = PIECES - IN_RING
assert PIECES % RING == 0 and PAIR_PIECES % RING == 0
P_KCV, P_QB, P_KVW, P_CK1, P_CV1, P_KA, P_QA, P_VA, P_WO0, P_WO1 = range(ATT_PIECES)
E_GATE, E_UP, E_DOWN = 0, 2, 4
P_PG = PIECES - 2

SM_GAIN = 0
SM_POS = SM_GAIN + 3 * KT
SM_W2 = SM_POS + 2 * (CBLK // 2)
SM_ROUT = SM_W2 + 2 * 2 * HD
SM_RB = SM_ROUT + KT * 32
SM_PT = SM_RB + TT * NR
SM = SM_PT + 2 * SEQ
C_DIST = 0
C_MA = C_DIST + SEQ
C_MB = C_MA + SEQ
CS = C_MB + SEQ
C_CC = 0
C_CV = C_CC + TT * HB * NC
C_ID = C_CV + TT * NC
C_LT = C_ID + P
C_ONE = C_LT + P
C_IOTA = C_ONE + P
C_SUM4 = C_IOTA + CAP
C_TIE = C_SUM4 + NR
C_POW = C_TIE + 4
C_TRI = C_POW + TT
CN = C_TRI + 16


def slopes():
    n = HA + HB
    s = [2.0 ** (-8.0 * (i + 1) / n) for i in range(n)]
    return s[0::2], s[1::2]


def cost_parts():
    c = np.zeros((P, CS), np.float64)
    q = np.arange(P)[:, None]
    dist = P + q - np.arange(SEQ)[None, :]
    past = dist >= 0
    count = ((dist <= 128).astype(int) + (dist % 4 == 0) + (dist % 16 == 0)) * past
    c[:, C_DIST:C_DIST + SEQ] = np.where(past, dist, 0)
    c[:, C_MA:C_MA + SEQ] = np.where(count > 0, -np.log(np.maximum(count, 1)), HUGE)
    c[:, C_MB:C_MB + SEQ] = np.where(past, 0.0, HUGE)
    return c.astype(np.float32)


def tables():
    c = np.zeros((P, CN), np.float64)
    q = np.arange(P)[:, None]
    end = np.arange(NC) * CSTR + CBLK - 1
    _, mb = slopes()
    for t in range(TT):
        dc = (t * P + q) - end[None, :]
        for h in range(HB):
            at = C_CC + (t * HB + h) * NC
            c[:, at:at + NC] = np.where(dc >= 0, mb[h] * dc, HUGE)
        c[:, C_CV + t * NC:C_CV + (t + 1) * NC] = dc >= 0
    c[:, C_ID:C_ID + P] = np.eye(P)
    c[:, C_LT:C_LT + P] = q < np.arange(P)[None, :]
    c[:, C_ONE:C_ONE + P] = 1.0
    c[:, C_IOTA:C_IOTA + CAP] = np.arange(CAP) + 1
    c[:, C_SUM4:C_SUM4 + NR] = (q % 32) == np.arange(NR)[None, :]
    c[:, C_TIE:C_TIE + 4] = [4, 3, 2, 1]
    c[:, C_POW:C_POW + TT] = -0.5
    c[:, C_TRI:C_TRI + 16] = np.tril(np.ones((4, 4)), -1).ravel()
    return c.astype(np.float32)


class Chain:

    def __init__(self, eng, sem, n=0, base=0):
        self.eng, self.sem, self.n, self.base = eng, sem, n, base

    def add(self, ins):
        self.n += 1
        ins.then_inc(self.sem, 1)

    def wait(self):
        self.eng.wait_ge(self.sem, self.base + self.n)


def build_trunk(nc, x_in, small_in, parts_in, table_in, fgain_in, w_in, w_out, w_ck1, w_cv1,
                w_eg, w_eu, w_ed, w_pg, w_pp, out):
    ctx = ExitStack()
    with ctx:
        def sb(name, shape, dt=F32):
            return ctx.enter_context(nc.sbuf_tensor(name, shape, dt))

        ring = sb("ring", [P, RING, SLOT])
        x = sb("x", [P, TT, D])
        xn = sb("xn", [P, TT, D])
        hT = sb("hT", [P, KT, SEQ])
        tab = sb("tab", [P, CN])
        small = sb("small", [P, SM])
        cost_a = sb("cost_a", [P, HA, SEQ])
        cost_b = sb("cost_b", [P, HB, SEQ])
        pc = sb("pc", [P, TT, HB, CPAD])
        vbd = sb("vbd", [P, KVB, REP * HD])
        kcbd = sb("kcbd", [P, KVB, 2 * CPAD])
        sq = sb("sq", [P, TT])
        xn_flat = xn[:].rearrange("p t d -> p (t d)")
        rstd = sb("rstd", [P, TT])
        work = sb("work", [P, 15312])

        ps = ctx.enter_context(nc.psum_tensor("ps", [P, 8, 512], F32))

        fgain = ring[:, RING - 2, 0:D]

        BUF_S = 3
        BUF_W = 4
        cut = [0]

        def take(n):
            cut[0] += n
            assert cut[0] <= 15312, cut[0]
            return work[:, cut[0] - n:cut[0]]

        qbT = take(4 * SEQ).rearrange("p (i n) -> p i n", i=4)
        qaT = take(4 * SEQ).rearrange("p (i n) -> p i n", i=4)
        kaz = take(HA * SEQ).rearrange("p (i q n) -> p i q n", i=4, q=2)
        kbz = take(KVB * 4 * SEQ).rearrange("p (g w q n) -> p g w q n", g=KVB, w=2, q=2)
        va = take(TT * 512).rearrange("p (t n) -> p t n", t=TT)
        vb = take(TT * 2 * P).rearrange("p (w t n) -> p w t n", w=2, t=TT)
        gate = take(TT * 3 * HB).rearrange("p (t n) -> p t n", t=TT)
        cost = take(BUF_S * 3 * P).rearrange("p (b n) -> p b n", b=BUF_S)
        pr_at = cut[0]
        pr = take(BUF_W * 3 * P).rearrange("p (b n) -> p b n", b=BUF_W)
        prT = take(4 * 3 * P).rearrange("p (b n) -> p b n", b=4)
        low = take(24 * TT).rearrange("p (j t) -> p j t", t=TT)
        den = take(24 * TT).rearrange("p (j t) -> p j t", t=TT)
        wgt = take(24 * TT).rearrange("p (j t) -> p j t", t=TT)
        NJ = CBLK // 2
        assert (4 + BUF_W) * 3 * P >= 2 * NJ * KVB * CG + 3 * CHID + 2 * HD
        c0 = pr_at
        blk = work[:, c0:c0 + 2 * NJ * KVB * CG].rearrange("p (w j g c) -> p w j g c", w=2, j=NJ, g=KVB)
        c0 += 2 * NJ * KVB * CG
        NH = 2 * KVB * CG
        hid, hid_u, hid_g = (work[0:NH, c0 + i * CHID:c0 + (i + 1) * CHID] for i in range(3))
        c0 += 3 * CHID
        hidT = work[:, c0:c0 + 2 * NH].rearrange("p (m n) -> p m n", m=2)
        cs = take(TT * HB * NC).rearrange("p (n c) -> p n c", c=NC)
        cz = take(TT * HB * NC).rearrange("p (n c) -> p n c", c=NC)
        clow = take(TT * HB)
        cden = take(TT * HB)
        cw = take(TT * HB)
        pcT = take(TT * KVB * P).rearrange("p (g n) -> p g n", g=KVB)
        parts = take(CS)

        cut[0] = 0
        r_m = take(TT)
        r_e = take(TT * 4).rearrange("p (t n) -> p t n", t=TT)
        r_w = take(TT * 4).rearrange("p (t n) -> p t n", t=TT)
        r_wm = take(TT)
        onehot = take(TT * NG).rearrange("p (t n) -> p t n", t=TT)
        r_x = take(TT * 4).rearrange("p (t n) -> p t n", t=TT)
        gsum = take(TT)
        gw = take(TT)
        r_big = take(TT * NE)
        r_before = take(2 * TT * NE)
        within = take(TT * EPG).rearrange("p (t n) -> p t n", t=TT)
        above = take(TT * EPG).rearrange("p (t n) -> p t n", t=TT)
        chosen = take(TT * EPG).rearrange("p (t n) -> p t n", t=TT)
        top = take(TT)
        ex = take(TT * EPG).rearrange("p (t n) -> p t n", t=TT)
        esum = take(TT)
        member = take(TT * NE).rearrange("p (t n) -> p t n", t=TT)
        weight = take(TT * NE).rearrange("p (t n) -> p t n", t=TT)
        slot_of = take(TT * NE).rearrange("p (t n) -> p t n", t=TT)
        most = take(1)
        over_w = take(TT * NE).rearrange("p (t n) -> p t n", t=TT)
        pick = take(TT * P).rearrange("p (t n) -> p t n", t=TT)
        pickw = take(TT * P).rearrange("p (t n) -> p t n", t=TT)
        pickT = take(TT * P).rearrange("p (t n) -> p t n", t=TT)
        over_from = cut[0]
        xg = take(KT * P).rearrange("p (k n) -> p k n", k=KT)
        th = take(DE)
        a1 = take(DE)
        act_in = a1
        lgT = th[:, 0:SEQ]
        actT = take(FT * P).rearrange("p (f n) -> p f n", f=FT)
        y = take(D)
        ow_gate = work[:, over_from:over_from + KT * P].rearrange("p (k n) -> p k n", k=KT)
        ow_up = work[:, over_from + KT * P:over_from + 2 * KT * P].rearrange("p (k n) -> p k n", k=KT)
        ow_down = work[:, over_from + 2 * KT * P:over_from + 2 * KT * P + D]
        o_th, o_a1, o_a2 = (xn_flat[:, i * SEQ:(i + 1) * SEQ] for i in range(3))
        assert cut[0] >= over_from + 3 * D
        ple_w = take(2 * D).rearrange("p (k n) -> p k n", k=2)
        last_gate = take(2 * SLOT).rearrange("p (a k n) -> p a k n", a=2, k=KT)
        pth = work[:, over_from:over_from + 2 * 512].rearrange("p (b n) -> p b n", b=2)
        pv = work[:, over_from + 2 * 512:over_from + 4 * 512].rearrange("p (b n) -> p b n", b=2)
        most_i = sb("most_i", [P, 1], I32)

        ident = tab[:, C_ID:C_ID + P]
        ones = tab[:, C_ONE:C_ONE + P]

        def gain(s, k0, n=1):
            return small[:, SM_GAIN + s * KT + k0:SM_GAIN + s * KT + k0 + n]

        pos2 = small[:, SM_POS:SM_POS + 2 * NJ].rearrange("p (w j) -> p w j", w=2)
        cw2 = small[:, SM_W2:SM_W2 + 4 * HD].rearrange("p (w m n) -> p w m n", w=2, m=2)
        rout = small[:, SM_ROUT:SM_ROUT + KT * 32].rearrange("p (k n) -> p k n", k=KT)
        pT = small[:, SM_PT:SM_PT + 2 * SEQ].rearrange("p (k n) -> p k n", k=2)

        def sem(name):
            return ctx.enter_context(nc.semaphore(name))

        slot_in = [sem(f"slot_in{i}") for i in range(RING)]
        piece_used = sem("piece_used")
        parts_sem = sem("cost_parts")
        x_in_sem, table_sem, fgain_sem, out_sem = sem("x_in"), sem("table"), sem("fgain"), sem("out_s")
        small_sem = sem("small_in")
        names = """ple_in last_gate_in sq_act sq_dve ms_ready rstd_ready chain_dve xn_dve xn_act turned hT_act hT_dve kcv_out qb_out kb_out qa_out ka_out cmp_out va_out
            blk_ready kb_act vs_ready vw_ready gate_act gate_dve qb_dve qb_act gelu_x gelu_t gelu_done
            qk_act qk_dve kc_ready vc_ready va_act va_dve cscore cexp_in cexp cprob cturn cturned
            score costed expd scaled turnedP prT_ready summed oT_dve oT_act wo_out
            cost_made blk_zero zeroed hid_turned hidT_ready x_added
            logitsT logitsT_ready routed rank_in ranked counted gexp_in gexp eexp_in eexp route_done picked pickw_ready gathered
            xg_ready th_ready act_ready act_turned actT_ready pick_turned pickT_ready y_act y_dve
            scattered added
            ple_q ple_z ple_th ple_x over_ld over_g over_t over_a over_y over_x over_l""".split()
        s = {n: sem("l_" + n) for n in names}
        nums = [v.num for v in s.values()]
        assert nums == list(range(nums[0], nums[0] + len(nums)))

        def piece_src(l, i):
            cols = {P_KCV: (KC, 512), P_QB: (QB, 512), P_KVW: (KW, N_IN - KW), P_QA: (QA, 512),
                    P_KA: (KA, 512), P_VA: (VA, 512)}
            if i in cols:
                c, n = cols[i]
                return w_in[l, :, c:c + n].rearrange("(k p) n -> p k n", p=P), n
            if i in (P_CK1, P_CV1):
                return (w_ck1 if i == P_CK1 else w_cv1)[l].rearrange("(k p) n -> p k n", p=P), CHID
            assert i in (P_WO0, P_WO1)
            h = i - P_WO0
            return w_out[l, :, h * 512:(h + 1) * 512].rearrange("(k p) n -> p k n", p=P), 512

        def rounds(i):
            return len(range(i % RING, IN_RING, RING))

        def slot(i, n):
            k = SLOT // n
            return ring[:, i % RING, 0:k * n].rearrange("p (k n) -> p k n", n=n)

        def slot8(i, n=512):
            return ring[:, i % RING, 0:KT * n].rearrange("p (k n) -> p k n", n=n)

        def load_piece(sp, l, i):
            src, n = piece_src(l, i)
            dst = ring[:, i % RING, 0:src.shape[1] * n].rearrange("p (k n) -> p k n", n=n)
            sp.dma_start(dst, src).then_inc(slot_in[i % RING], 16)

        sa, sbb = slopes()

        with nc.Block() as block:
            @block.sync
            def _(sp):
                sp.dma_start(x[:], x_in.rearrange("(t p) d -> p t d", p=P)).then_inc(x_in_sem, 16)
                sp.dma_start(tab[:], table_in).then_inc(table_sem, 16)
                sp.dma_start(small[:], small_in[0]).then_inc(small_sem, 16)
                for i in range(RING):
                    load_piece(sp, 0, i)
                    if i == 0:
                        sp.dma_start(parts, parts_in).then_inc(parts_sem, 16)

            @block.vector
            def _(dve):
                nc.vector.memset(pc[:], 0.0)
                nc.vector.memset(vbd[:], 0.0)
                nc.vector.memset(kcbd[:], 0.0)
                dve.wait_ge(table_sem, 16)
                dve.wait_ge(x_in_sem, 16)

        PAIRS_H = ([("a", i) for i in range(HA // 2)]
                   + [(br, i) for i in range(HB // 2) for br in ("s", "w")])
        HEADS = [(kind, 2 * i + q) for kind, i in PAIRS_H for q in range(2)]
        NHD = len(HEADS)
        LAG = 3

        def pair_tile(n):
            kind, i = PAIRS_H[n]
            return i if kind == "a" else HA // 2 + i

        WHOLE = [2, 4, 8, 12]

        def head_qk(j):
            kind, h = HEADS[j]
            if kind == "a":
                return qaT[:, h // 2, :], kaz[:, h // 2, h % 2, :]
            return qbT[:, h // 2, :], kbz[:, h // REP, 0 if kind == "s" else 1, h % 2, :]

        def head_v(j, t):
            kind, h = HEADS[j]
            if kind == "a":
                return va[:, t, h * HD:(h + 1) * HD]
            return vb[:, 0 if kind == "s" else 1, t, (h // REP) * HD:(h // REP + 1) * HD]

        with nc.Fori(0, DEPTH) as l:
            with nc.Block() as block:

                def used(eng, i, j=0):
                    eng.wait_ge(piece_used, PIECES * l + PAIR_PIECES * j + i + 1)

                @block.sync
                def _(sp):
                    def room(n):
                        sp.wait_ge(piece_used, PIECES * l + n + 1 - RING)

                    for i in range(RING, ATT_PIECES):
                        room(i)
                        load_piece(sp, l, i)

                    def load_expert_piece(j, k, early=0):
                        i = ATT_PIECES + k - early
                        sp.wait_ge(piece_used, PIECES * l + PAIR_PIECES * j + i + 1 - RING)
                        w = (w_eg, w_eu, w_ed)[k // 2]
                        sp.dma_start(slot(i, D if k >= E_DOWN else DE),
                                     w[l, 2 * j + k % 2].rearrange("(k p) n -> p k n", p=P)
                                     ).then_inc(slot_in[i % RING], 16)

                    with sp.Fori(0, PAIRS - 1) as j:
                        for k in range(PAIR_PIECES):
                            load_expert_piece(j, k)
                    for k in range(E_UP, PAIR_PIECES):
                        load_expert_piece(PAIRS - 1, k, EARLY)
                    for h in range(2):
                        i = P_PG + h - EARLY
                        room(i)
                        sp.dma_start(slot8(i), w_pg[l, :, h * 512:(h + 1) * 512].rearrange("(k p) n -> p k n", p=P)
                                     ).then_inc(slot_in[i % RING], 16)
                    with sp.If(l < DEPTH - 1):
                        for i in (*range(IN_RING % RING, RING), *range(IN_RING % RING)):
                            if i == (P_PG - EARLY) % RING:
                                sp.wait_ge(s["hT_act"], 3 * KT // 2)
                                sp.wait_ge(s["hT_dve"], 3 * KT // 2)
                                sp.wait_ge(s["ple_q"], 4)
                                sp.dma_start(small[:], small_in[(l + 1) % DEPTH]).then_inc(small_sem, 16)
                            sp.wait_ge(piece_used, PIECES * l + RING * (rounds(i) - 1) + i + EARLY + 1)
                            load_piece(sp, (l + 1) % DEPTH, i)
                    with sp.If(l > DEPTH - 2):
                        sp.wait_ge(piece_used, PIECES * l + RING * (rounds(RING - 2) - 1) + RING - 2 + EARLY + 1)
                        sp.dma_start(fgain, fgain_in).then_inc(fgain_sem, 16)

                @block.tensor
                def _(pe):
                    mm = nc.tensor.matmul

                    def arrived(i):
                        pe.wait_ge(slot_in[i % RING], 16 * rounds(i) * l + 16 * (i // RING + 1))

                    def turn(event, src):
                        for t in range(TT):
                            pe.wait_ge(s["xn_act" if t else "xn_dve"], event + 1)
                            for k in range(KT):
                                at = (k % 2) * SEQ + t * P
                                m = nc.tensor.transpose(ps[:, k // 2, at:at + P], src[:, t, k * P:(k + 1) * P], ident)
                                if t == TT - 1 and k % 2 == 1:
                                    m.then_inc(s["turned"], 1)

                    def turned_in(event):
                        pe.wait_ge(s["hT_act"], KT // 2 * (event + 1))
                        pe.wait_ge(s["hT_dve"], KT // 2 * (event + 1))

                    pe.wait_ge(small_sem, 16 * l + 16)
                    turn(0, xn)
                    turned_in(0)

                    def features(bank, c, w, col):
                        for k in range(KT):
                            m = mm(ps[:, bank, c:c + SEQ], w[:, k, col:col + P], hT[:, k, :],
                                   start=(k == 0), stop=(k == KT - 1))
                        return m

                    def tokens(bank, c, w, col, n, t):
                        for k in range(KT):
                            m = mm(ps[:, bank, c:c + n], hT[:, k, t * P:(t + 1) * P], w[:, k, col:col + n],
                                   start=(k == 0), stop=(k == KT - 1))
                        return m

                    arrived(P_KCV)
                    w = slot8(P_KCV)
                    features(4, 0, w, 0)
                    features(4, SEQ, w, P).then_inc(s["kcv_out"], 1)
                    features(5, 0, w, 2 * P)
                    tokens(6, 0, w, 3 * P, P, 0)
                    tokens(6, P, w, 3 * P, P, 1).then_inc(piece_used, 1)
                    arrived(P_QB)
                    w = slot8(P_QB)
                    for i in range(4):
                        m = features(i // 2, (i % 2) * SEQ, w, i * P)
                        if i == 1:
                            m.then_inc(s["qb_out"], 1)
                    m.then_inc(piece_used, 1)
                    arrived(P_KVW)
                    w = slot8(P_KVW, N_IN - KW)
                    features(5, SEQ, w, 0).then_inc(s["kb_out"], 1)
                    NV = P + 3 * HB
                    tokens(7, 0, w, P, NV, 0)
                    tokens(7, NV, w, P, NV, 1).then_inc(piece_used, 1)
                    pe.wait_ge(s["blk_ready"], 4)
                    arrived(P_CK1)
                    arrived(P_CV1)
                    for j in range(NJ // 2):
                        for w_i, i in ((0, P_CK1), (1, P_CV1)):
                            for late in range(2):
                                c = late * 64 + w_i * 32
                                m = mm(ps[c:c + 32, 2, 0:CHID],
                                       blk[:, w_i, late * NJ // 2 + j, :, :].rearrange("p g c -> p (g c)"),
                                       slot(i, CHID)[:, late * NJ // 2 + j, :], start=(j == 0),
                                       stop=(j == NJ // 2 - 1))
                            if j == NJ // 2 - 1:
                                m.then_inc(piece_used, 1)
                    arrived(P_KA)
                    w = slot8(P_KA)
                    for i in range(4):
                        if i == 2:
                            pe.wait_ge(s["kb_act"], 4)
                        m = features(4 + i // 2, (i % 2) * SEQ, w, i * P)
                        if i == 1:
                            m.then_inc(s["ka_out"], 1)
                    m.then_inc(piece_used, 1)
                    arrived(P_QA)
                    w = slot8(P_QA)
                    for i in range(4):
                        if i == 0:
                            pe.wait_ge(s["vs_ready"], 1)
                        if i == 2:
                            pe.wait_ge(s["vw_ready"], 1)
                            pe.wait_ge(s["gate_act"], 1)
                        m = features(6 + i // 2, (i % 2) * SEQ, w, i * P)
                        if i == 1:
                            m.then_inc(s["qa_out"], 1)
                    m.then_inc(piece_used, 1)
                    pe.wait_ge(s["gelu_done"], 1)
                    for mt in range(2):
                        m = nc.tensor.transpose(ps[:, 2, mt * NH:(mt + 1) * NH], hid_g[:, mt * P:(mt + 1) * P],
                                                ident[0:NH, 0:NH])
                    m.then_inc(s["hid_turned"], 1)
                    pe.wait_ge(s["hidT_ready"], 1)
                    for mt in range(2):
                        mm(ps[0:HD, 3, 0:KVB * CG], cw2[:, 0, mt, :], hidT[:, mt, 0:KVB * CG],
                           start=(mt == 0), stop=(mt == 1))
                    for g in range(KVB):
                        for mt in range(2):
                            m = mm(ps[0:CG, 3, HD + g * HD:2 * HD + g * HD],
                                   hidT[:, mt, (KVB + g) * CG:(KVB + g + 1) * CG],
                                   cw2[:, 1, mt, :], start=(mt == 0), stop=(mt == 1))
                    m.then_inc(s["cmp_out"], 1)
                    arrived(P_VA)
                    w = slot8(P_VA)
                    pe.wait_ge(s["qb_dve"], 1)
                    pe.wait_ge(s["qb_act"], 1)
                    tokens(0, 0, w, 0, 512, 0).then_inc(s["va_out"], 1)
                    tokens(1, 0, w, 0, 512, 1).then_inc(piece_used, 1)

                    pe.wait_ge(s["qk_act"], 3)
                    pe.wait_ge(s["qk_dve"], 3)
                    pe.wait_ge(s["kc_ready"], 2)
                    for t in range(TT):
                        for i in range(HB // 2):
                            at = (t * (HB // 2) + i) * 2 * CPAD
                            m = mm(ps[:, 7, at:at + 2 * CPAD], qbT[:, i, t * P:(t + 1) * P],
                                   kcbd[:, 2 * i // REP, :], start=True, stop=True)
                    m.then_inc(s["cscore"], 1)

                    def scores(j):
                        q, k = head_qk(j)
                        if j >= BUF_S:
                            pe.wait_ge(s["costed"], 2 * (j - BUF_S + 1))
                        b = 4 + j % BUF_S
                        mm(ps[:, b, 0:P], q[:, 0:P], k[:, 0:P], start=True, stop=True)
                        mm(ps[:, b, P:3 * P], q[:, P:SEQ], k[:, :], start=True, stop=True).then_inc(s["score"], 1)

                    def turn_weights(j):
                        pe.wait_ge(s["scaled"], j + 1)
                        if j == 1:
                            pe.wait_ge(s["vc_ready"], 8)
                        if j >= 2:
                            pe.wait_ge(s["prT_ready"], j - 1)
                        for c in range(0, 3 * P, P):
                            m = nc.tensor.transpose(ps[:, 2 + j % 2, c:c + P], pr[:, j % BUF_W, c:c + P], ident)
                        m.then_inc(s["turnedP"], 1)

                    def weigh(n):
                        kind, i = PAIRS_H[n]
                        pe.wait_ge(s["prT_ready"], 2 * n + 2)
                        if n == 0:
                            pe.wait_ge(s["va_act"], 1)
                            pe.wait_ge(s["va_dve"], 1)
                        tile = pair_tile(n)
                        if kind == "s" and i == 0:
                            pe.wait_ge(s["cturned"], 1)
                            pe.wait_ge(s["oT_dve"], 1)
                        if kind == "s" and i == 2:
                            pe.wait_ge(s["oT_act"], 1)
                        b = (tile // 2) % 2
                        c = (tile % 2) * SEQ
                        out = [ps[q * HD:(q + 1) * HD, b, c:c + SEQ] for q in range(2)]
                        if kind == "s":
                            for q in range(2):
                                h = 2 * i + q
                                mm(out[q], vbd[:, h // REP, (h % REP) * HD:(h % REP + 1) * HD],
                                   pcT[:, h // REP, :], start=True, stop=False)
                        for q in range(2):
                            mm(out[q], head_v(2 * n + q, 0), prT[:, (2 * n + q) % 4, 0:SEQ],
                               start=(kind == "a"), stop=False)
                        for q in range(2):
                            m = mm(out[q][:, P:SEQ], head_v(2 * n + q, 1), prT[:, (2 * n + q) % 4, SEQ:3 * P],
                                   start=False, stop=(kind != "s"))
                        m.then_inc(s["summed"], 1)

                    for step in range(NHD + LAG + 2):
                        if step < NHD:
                            scores(step)
                        if LAG <= step < NHD + LAG:
                            turn_weights(step - LAG)
                        if step == 6:
                            pe.wait_ge(s["cprob"], 1)
                            for g in range(KVB):
                                for t in range(TT):
                                    at = g * SEQ + t * P
                                    m = nc.tensor.transpose(ps[:, 7, at:at + P],
                                                            pc[:, t, g * REP:(g + 1) * REP, :]
                                                            .rearrange("p h c -> p (h c)"), ident)
                            m.then_inc(s["cturn"], 1)
                        if step >= LAG + 2 and (step - LAG) % 2 == 0:
                            weigh((step - LAG) // 2 - 1)

                    pe.wait_ge(s["oT_act"], 2)
                    pe.wait_ge(s["oT_dve"], 2)
                    for half in range(2):
                        arrived(P_WO0 + half)
                        for t in range(TT):
                            tokens(4 + 2 * half + t, 0, slot8(P_WO0 + half), 0, 512, t
                                   ).then_inc(piece_used if t else s["wo_out"], 1)

                    turn(1, xn)
                    turned_in(1)
                    pe.wait_ge(s["x_added"], 4)
                    for k in range(KT):
                        c = k % 4 * 32
                        m = mm(ps[c:c + 32, 4, 0:SEQ], rout[:, k, :], hT[:, k, :], start=(k < 4), stop=(k >= 4))
                    m.then_inc(s["logitsT"], 1)
                    mm(ps[:, 6, 0:TT * NR], tab[0:1, C_ONE:C_ONE + P], small[0:1, SM_RB:SM_RB + TT * NR],
                       start=True, stop=False)
                    pe.wait_ge(s["logitsT_ready"], 1)
                    for t in range(TT):
                        m = mm(ps[:, 6, t * NR:(t + 1) * NR], lgT[:, t * P:(t + 1) * P],
                               tab[:, C_SUM4:C_SUM4 + NR], start=False, stop=(t == TT - 1))
                    m.then_inc(s["routed"], 1)
                    pe.wait_ge(s["rank_in"], 1)
                    lt = tab[:, C_LT:C_LT + P]
                    mm(ps[:, 5, 0:TT * NE], lt, member[:].rearrange("p t n -> p (t n)"), start=True, stop=False)
                    mm(ps[:, 5, NE:2 * NE], ones, member[:, 0, :], start=False, stop=True).then_inc(s["ranked"], 1)
                    for t in range(TT):
                        m = mm(ps[:, 6, 0:NE], ones, member[:, t, :], start=(t == 0), stop=(t == TT - 1))
                    m.then_inc(s["counted"], 1)

                    def gather():
                        for k in range(KT):
                            for t in range(TT):
                                m = mm(ps[:, 2 + k // 4, (k % 4) * P:(k % 4 + 1) * P], xn[:, t, k * P:(k + 1) * P],
                                       pick[:, t, :], start=(t == 0), stop=(t == 1))
                            if k % 4 == 3:
                                m.then_inc(s["gathered"], 1)

                    SCATTER_BANKS = (7, 2, 3, 4)

                    def scatter(n):
                        t, half = n % 2, n // 2
                        mm(ps[:, SCATTER_BANKS[n], :], pickT[:, t, :], y[:, half * 512:(half + 1) * 512],
                           start=True, stop=True).then_inc(s["scattered"], 1)

                    pe.wait_ge(s["picked"], 1)
                    gather()

                    def turn_activation():
                        for f in range(FT):
                            m = nc.tensor.transpose(ps[:, 4, f * P:(f + 1) * P], act_in[:, f * P:(f + 1) * P], ident)
                        m.then_inc(s["act_turned"], 1)

                    def pair(j, last=False):
                        def got(k):
                            if last and k < E_UP:
                                pe.wait_ge(s["last_gate_in"], 32)
                                return last_gate[:, k, :, :]
                            i = ATT_PIECES + k - (EARLY if last else 0)
                            pe.wait_ge(slot_in[i % RING], 16 * rounds(i) * l + 16 * j + 16 * (i // RING + 1))
                            return slot(i, D if k >= E_DOWN else DE)

                        pe.wait_ge(s["xg_ready"], 2 * j + 2)
                        pe.wait_ge(s["pickT_ready"], j + 1)
                        for b, piece in ((0, E_GATE), (1, E_UP)):
                            w2 = [got(piece), got(piece + 1)]
                            for k in range(KT):
                                for a in range(2):
                                    m = mm(ps[a * CAP:(a + 1) * CAP, b, :], xg[:, k, a * CAP:(a + 1) * CAP],
                                           w2[a][:, k, :], start=(k == 0), stop=(k == KT - 1))
                                    if k == KT - 1:
                                        m.then_inc(piece_used, 1)
                        pe.wait_ge(s["added"], 4 * j + 1)
                        if not last:
                            pe.wait_ge(s["picked"], j + 2)
                            gather()
                            pe.wait_ge(s["act_ready"], j + 1)
                            turn_activation()
                        pe.wait_ge(s["y_act"], j + 1)
                        pe.wait_ge(s["y_dve"], j + 1)
                        for n in range(4):
                            if n == 1 and not last:
                                pe.wait_ge(s["xg_ready"], 2 * j + 3)
                            if n == 2 and not last:
                                pe.wait_ge(s["xg_ready"], 2 * j + 4)
                            if n == 3:
                                if last:
                                    pe.wait_ge(s["act_ready"], j + 1)
                                    turn_activation()
                                pe.wait_ge(s["actT_ready"], j + 1)
                            scatter(n)
                        pe.wait_ge(s["pickw_ready"], j + 1)
                        for t in range(TT):
                            m = nc.tensor.transpose(ps[:, 0, t * P:(t + 1) * P], pickw[:, t, :], ident)
                        m.then_inc(s["pick_turned"], 1)
                        w2 = [got(E_DOWN), got(E_DOWN + 1)]
                        for f in range(FT):
                            for half in range(2):
                                for a in range(2):
                                    m = mm(ps[a * CAP:(a + 1) * CAP, 5 + half, :], actT[:, f, a * CAP:(a + 1) * CAP],
                                           w2[a][:, f, half * 512:(half + 1) * 512],
                                           start=(f == 0), stop=(f == FT - 1))
                                    if f == FT - 1 and half == 1:
                                        m.then_inc(piece_used, 1)

                    with pe.Fori(0, PAIRS - 1) as j:
                        pair(j)
                    pair(PAIRS - 1, last=True)

                    pe.wait_ge(s["pickT_ready"], PAIRS + 1)
                    pe.wait_ge(s["y_act"], PAIRS + 1)
                    pe.wait_ge(s["y_dve"], PAIRS + 1)
                    pe.wait_ge(s["added"], 4 * PAIRS + 1)
                    for n in range(4):
                        scatter(n)

                    pe.wait_ge(s["route_done"], 1)
                    with pe.If(pe.value_load(most_i[0:1, 0:1], min_val=0, max_val=SEQ) > CAP):
                        with pe.Fori(0, NG * EPG) as e:
                            for f in range(FT):
                                pe.wait_ge(s["over_ld"], 48 * FT * e + 48 * (f + 1))
                                for b, w in ((0, ow_gate), (1, ow_up)):
                                    features(b, 0, w, 0).then_inc(s["over_g"], 1)
                                pe.wait_ge(s["over_a"], FT * e + f + 1)
                                for t in range(TT):
                                    for half in range(2):
                                        m = mm(ps[:, 2 + 2 * t + half, :], o_a2[:, t * P:(t + 1) * P],
                                               ow_down[:, half * 512:(half + 1) * 512], start=True, stop=True)
                                m.then_inc(s["over_y"], 1)
                        pe.wait_ge(s["over_x"], NG * EPG * FT + 1)
                    pe.wait_ge(s["ple_in"], 16)
                    pe.wait_ge(s["added"], 4 * PAIRS + 5)
                    for half in range(2):
                        for t in range(TT):
                            for k in range(2):
                                m = mm(ps[:, 4 + 2 * half + t, :], pT[:, k, t * P:(t + 1) * P],
                                       ple_w[:, k, half * 512:(half + 1) * 512], start=(k == 0), stop=(k == 1))
                            m.then_inc(s["ple_q"], 1)
                    turn(2, xn)
                    turned_in(2)
                    for half in range(2):
                        arrived(P_PG - EARLY + half)
                        for t in range(TT):
                            tokens(2 * half + t, 0, slot8(P_PG - EARLY + half), 0, 512, t
                                   ).then_inc(piece_used if t else s["ple_z"], 1)

                @block.scalar
                def _(act):
                    A = nc.scalar.activation

                    act.wait_ge(small_sem, 16 * l + 16)

                    def norm(n):
                        A(xn[:, 1, :], x[:, 1, :], ACT.Square, accum_out=sq[:, 1:2]).then_inc(s["sq_act"], 1)
                        act.wait_ge(s["rstd_ready"], n + 1)
                        A(xn[:, 1, :], x[:, 1, :], ACT.Copy, scale=rstd[:, 1:2]).then_inc(s["xn_act"], 1)

                    def evac_turned(event, g):
                        for b in (0, 2):
                            act.wait_ge(s["turned"], 4 * event + b + 1)
                            for k in (2 * b, 2 * b + 1):
                                A(hT[:, k, :], ps[:, b, (k % 2) * SEQ:(k % 2 + 1) * SEQ], ACT.Copy,
                                  scale=gain(g, k)).then_inc(s["hT_act"], 1)

                    norm(0)
                    evac_turned(0, 0)
                    used(act, P_KCV)
                    A(vb[:, 0, :, :], ps[:, 6, 0:SEQ].rearrange("p (t n) -> p t n", t=TT), ACT.Copy
                      ).then_inc(s["vs_ready"], 1)
                    used(act, P_QB)
                    A(qbT[:, 2:4, :], ps[:, 1, :].rearrange("p (i n) -> p i n", i=2), ACT.Copy,
                      scale=-(HD ** -0.5)).then_inc(s["qb_act"], 1)
                    act.wait_ge(s["kb_out"], 1)
                    for g in range(KVB):
                        for lo in (0, HD):
                            if g == 0 and lo == 0:
                                act.wait_ge(s["zeroed"], 4)
                            A(kbz[lo:lo + HD, g, :, lo // HD, :],
                              ps[g * HD:(g + 1) * HD, 5, :].rearrange("p (w n) -> p w n", w=2),
                              ACT.Copy).then_inc(s["kb_act"], 1)
                    used(act, P_KVW)
                    NV = P + 3 * HB
                    A(gate[:], ps[:, 7, 0:2 * NV].rearrange("p (t n) -> p t n", t=TT)[:, :, P:NV], ACT.Tanh,
                      scale=0.5).then_inc(s["gate_act"], 1)
                    act.wait_ge(s["gelu_t"], 1)
                    A(hid_u, hid_u, ACT.Tanh, scale=GELU_C).then_inc(s["gelu_t"], 1)
                    act.wait_ge(s["ka_out"], 1)
                    for q in range(2):
                        A(kaz[q * HD:(q + 1) * HD, 0:2, q, :],
                          ps[q * HD:(q + 1) * HD, 4, :].rearrange("p (i n) -> p i n", i=2), ACT.Copy
                          ).then_inc(s["qk_act"], 1)
                    act.wait_ge(s["qa_out"], 1)
                    A(qaT[:, 0:2, :], ps[:, 6, :].rearrange("p (i n) -> p i n", i=2), ACT.Copy,
                      scale=-(HD ** -0.5)).then_inc(s["qk_act"], 1)
                    act.wait_ge(s["cmp_out"], 1)
                    for lo in (0, HD):
                        at = lo // HD * CPAD
                        A(kcbd[lo:lo + HD, :, at:at + NC],
                          ps[0:HD, 3, 0:KVB * CG].rearrange("p (g c) -> p g c", g=KVB)[:, :, 0:NC],
                          ACT.Copy).then_inc(s["kc_ready"], 1)
                    act.wait_ge(s["va_out"], 1)
                    A(va[:, 0, :], ps[:, 0, :], ACT.Copy).then_inc(s["va_act"], 1)

                    def weights(j):
                        for t in range(TT):
                            act.wait_ge(s["costed"], 2 * j + t + 1)
                            if j >= BUF_W and t == 0:
                                act.wait_ge(s["turnedP"], j - BUF_W + 1)
                            c, n = (0, P) if t == 0 else (P, SEQ)
                            A(pr[:, j % BUF_W, c:c + n], cost[:, j % BUF_S, c:c + n], ACT.Exp, scale=-1.0,
                              bias=low[:, j, t:t + 1], accum_out=den[:, j, t:t + 1]).then_inc(s["expd"], 1)

                    def evac_weights(j):
                        act.wait_ge(s["turnedP"], j + 1)
                        if j >= 4:
                            act.wait_ge(s["summed"], j // 2 - 1)
                        A(prT[:, j % 4, :], ps[:, 2 + j % 2, 0:3 * P], ACT.Copy).then_inc(s["prT_ready"], 1)

                    def evac_out(m):
                        act.wait_ge(s["summed"], WHOLE[m])
                        A(hT[:, 2 * m:2 * m + 2, :], ps[:, m % 2, :].rearrange("p (i n) -> p i n", i=2), ACT.Copy
                          ).then_inc(s["oT_act"], 1)

                    for step in range(NHD + LAG):
                        if step >= LAG:
                            evac_weights(step - LAG)
                        if step < NHD:
                            weights(step)
                        if step == 2:
                            act.wait_ge(s["cexp_in"], 1)
                            A(cs[:], cs[:], ACT.Exp, scale=-1.0).then_inc(s["cexp"], 1)
                        if step == 7:
                            act.wait_ge(s["cturn"], 1)
                            A(pcT[:], ps[:, 7, :].rearrange("p (g n) -> p g n", g=KVB), ACT.Copy
                              ).then_inc(s["cturned"], 1)
                        if step == 2 * WHOLE[1] + LAG + 1:
                            evac_out(1)
                    evac_out(3)
                    act.wait_ge(s["summed"], len(PAIRS_H))
                    for a in range(2):
                        act.dma_start(last_gate[:, a, :, :], w_eg[l, NE - 2 + a].rearrange("(k p) n -> p k n", p=P)
                                      ).then_inc(s["last_gate_in"], 16)
                    act.dma_start(ple_w[:], w_pp[l].rearrange("(k p) n -> p k n", p=P)).then_inc(s["ple_in"], 16)

                    act.wait_ge(s["x_added"], 4)
                    norm(1)
                    evac_turned(1, 1)
                    act.wait_ge(s["gexp_in"], 1)
                    A(r_x[:], r_x[:], ACT.Exp).then_inc(s["gexp"], 1)
                    act.wait_ge(s["eexp_in"], 1)
                    A(ex[:], ex[:], ACT.Exp).then_inc(s["eexp"], 1)

                    with act.Fori(0, PAIRS) as j:
                        used(act, ATT_PIECES + E_GATE + 1, j)
                        A(th, ps[:, 0, :], ACT.Tanh, scale=0.5).then_inc(s["th_ready"], 1)
                        act.wait_ge(s["act_turned"], j + 1)
                        A(actT[:], ps[:, 4, :].rearrange("p (f n) -> p f n", f=FT), ACT.Copy
                          ).then_inc(s["actT_ready"], 1)
                        act.wait_ge(s["pick_turned"], j + 1)
                        A(pickT[:], ps[:, 0, 0:TT * P].rearrange("p (t n) -> p t n", t=TT), ACT.Copy
                          ).then_inc(s["pickT_ready"], 1)
                        used(act, ATT_PIECES + E_DOWN + 1, j)
                        A(y[:, 0:512], ps[:, 5, :], ACT.Copy).then_inc(s["y_act"], 1)

                    act.wait_ge(s["route_done"], 1)
                    with act.If(act.value_load(most_i[0:1, 0:1], min_val=0, max_val=SEQ) > CAP):
                        with act.Fori(0, NG * EPG) as e:
                            for f in range(FT):
                                act.wait_ge(s["over_x"], FT * e + f + 1)
                                for dst, w in ((ow_gate, w_eg), (ow_up, w_eu)):
                                    act.dma_start(dst, w[l, e, :, f * P:(f + 1) * P].rearrange("(k p) n -> p k n", p=P)
                                                  ).then_inc(s["over_ld"], 16)
                                act.dma_start(ow_down, w_ed[l, e, f * P:(f + 1) * P, :]).then_inc(s["over_ld"], 16)
                                act.wait_ge(s["over_g"], 2 * FT * e + 2 * f + 1)
                                A(o_th, ps[:, 0, 0:SEQ], ACT.Tanh, scale=0.5).then_inc(s["over_t"], 1)
                        act.wait_ge(s["over_x"], NG * EPG * FT + 1)
                    act.wait_ge(s["added"], 4 * PAIRS + 5)
                    norm(2)
                    evac_turned(2, 2)
                    for n in range(4):
                        if n % 2:
                            used(act, P_PG + n // 2)
                        else:
                            act.wait_ge(s["ple_z"], n // 2 + 1)
                        if n >= 2:
                            act.wait_ge(s["ple_x"], n - 1)
                        A(pth[:, n % 2, :], ps[:, n, :], ACT.Tanh, scale=0.5).then_inc(s["ple_th"], 1)

                @block.gpsimd
                def _(pool):
                    def inverse_rms(n):
                        pool.wait_ge(s["ms_ready"], n + 1)
                        nc.gpsimd.tensor_tensor(rstd[:], sq[:], tab[:, C_POW:C_POW + TT], ALU.pow
                                                ).then_inc(s["rstd_ready"], 1)

                    nc.gpsimd.memset(blk[:], 0.0).then_inc(s["blk_zero"], 1)
                    pool.wait_ge(s["blk_zero"], 1)
                    inverse_rms(0)
                    pool.wait_ge(s["rstd_ready"], 1)
                    for q in range(2):
                        lo = HD - q * HD
                        if q:
                            pool.wait_ge(s["zeroed"], 2)
                        nc.gpsimd.memset(kbz[lo:lo + HD, :, :, q, :], 0.0).then_inc(s["zeroed"], 1)
                        pool.wait_ge(s["zeroed"], 2 * q + 1)
                        nc.gpsimd.memset(kaz[lo:lo + HD, :, q, :], 0.0).then_inc(s["zeroed"], 1)
                    pool.wait_ge(s["wo_out"], 1)
                    nc.gpsimd.memset(y[:, 0:512], 0.0).then_inc(s["y_act"], 1)
                    nc.gpsimd.memset(y[:, 512:1024], 0.0).then_inc(s["y_dve"], 1)
                    nc.gpsimd.memset(pickT[:], 0.0).then_inc(s["pickT_ready"], 1)
                    inverse_rms(1)
                    inverse_rms(2)

                @block.vector
                def _(dve):
                    V = nc.vector
                    c = Chain(dve, s["chain_dve"])

                    def norm(n):
                        V.tensor_tensor_reduce(xn[:, 0, :], x[:, 0, :], x[:, 0, :], 1.0, 0.0, ALU.mult, ALU.add,
                                               sq[:, 0:1]).then_inc(s["sq_dve"], 1)
                        dve.wait_ge(s["sq_dve"], n + 1)
                        dve.wait_ge(s["sq_act"], n + 1)
                        V.tensor_scalar(sq[:], sq[:], 1.0 / D, EPS, ALU.mult, ALU.add).then_inc(s["ms_ready"], 1)
                        dve.wait_ge(s["rstd_ready"], n + 1)
                        V.tensor_scalar(xn[:, 0, :], x[:, 0, :], rstd[:, 0:1], None, ALU.mult).then_inc(s["xn_dve"], 1)

                    def evac_turned(event, g):
                        for b in (1, 3):
                            dve.wait_ge(s["turned"], 4 * event + b + 1)
                            for k in (2 * b, 2 * b + 1):
                                src = ps[:, b, (k % 2) * SEQ:(k % 2 + 1) * SEQ]
                                V.tensor_scalar(hT[:, k, :], src, gain(g, k), None, ALU.mult
                                                ).then_inc(s["hT_dve"], 1)

                    dve.wait_ge(small_sem, 16 * l + 16)
                    norm(0)
                    evac_turned(0, 0)
                    dve.wait_ge(s["kcv_out"], 1)
                    dve.wait_ge(s["blk_zero"], 1)
                    for g in range(KVB):
                        for half in range(2):
                            lo = half * HD
                            kv = ps[g * HD:(g + 1) * HD, 4, :].rearrange("p (w n) -> p w n", w=2)
                            for w_i in range(2):
                                src = bass.AP(kv.tensor, kv.offset + w_i * SEQ + half,
                                              [list(kv.ap[0]), [2, NJ], [CSTR, NC]])
                                add = pos2[lo:lo + HD, w_i, :].unsqueeze(2).to_broadcast([HD, NJ, NC])
                                ins = V.tensor_tensor(blk[lo:lo + HD, w_i, :, g, 0:NC], src, add, ALU.add)
                            ins.then_inc(s["blk_ready"], 1)
                    with dve.If(l < 1):
                        dve.wait_ge(parts_sem, 16)
                        for tb, slope, c_mask in ((cost_a, sa, C_MA), (cost_b, sbb, C_MB)):
                            for h in range(len(slope)):
                                V.scalar_tensor_tensor(out=tb[:, h, :], in0=parts[:, C_DIST:C_DIST + SEQ],
                                                       scalar=slope[h], in1=parts[:, c_mask:c_mask + SEQ],
                                                       op0=ALU.mult, op1=ALU.add).then_inc(s["cost_made"], 1)
                        dve.wait_ge(s["cost_made"], HA + HB)
                    dve.wait_ge(s["qb_out"], 1)
                    V.tensor_scalar(qbT[:, 0:2, :], ps[:, 0, :].rearrange("p (i n) -> p i n", i=2), -(HD ** -0.5),
                                    None, ALU.mult).then_inc(s["qb_dve"], 1)
                    used(dve, P_KVW)
                    NV = P + 3 * HB
                    dve.wait_ge(s["gate_act"], 1)
                    V.tensor_copy(vb[:, 1, :, :], ps[:, 7, 0:2 * NV].rearrange("p (t n) -> p t n", t=TT)[:, :, 0:P]
                                  ).then_inc(s["vw_ready"], 1)
                    V.tensor_scalar(gate[:], gate[:], 0.5, 0.5, ALU.mult, ALU.add).then_inc(s["gate_dve"], 1)
                    used(dve, P_CV1)
                    c.add(V.tensor_copy(hid, ps[0:NH, 2, 0:CHID]))
                    c.wait()
                    V.tensor_tensor(hid, hid, ps[NH:2 * NH, 2, 0:CHID], ALU.add).then_inc(s["gelu_x"], 1)
                    dve.wait_ge(s["gelu_x"], 1)
                    c.add(V.tensor_tensor(hid_u, hid, hid, ALU.mult))
                    c.wait()
                    c.add(V.tensor_scalar(hid_u, hid_u, 0.044715, 1.0, ALU.mult, ALU.add))
                    c.wait()
                    V.tensor_tensor(hid_u, hid_u, hid, ALU.mult).then_inc(s["gelu_t"], 1)
                    dve.wait_ge(s["gelu_t"], 2)
                    c.add(V.scalar_tensor_tensor(out=hid_u, in0=hid_u, scalar=1.0, in1=hid, op0=ALU.add, op1=ALU.mult))
                    c.wait()
                    V.tensor_scalar(hid_g, hid_u, 0.5, None, ALU.mult).then_inc(s["gelu_done"], 1)
                    used(dve, P_KA)
                    for q in range(2):
                        V.tensor_copy(kaz[q * HD:(q + 1) * HD, 2:4, q, :],
                                      ps[q * HD:(q + 1) * HD, 5, :].rearrange("p (i n) -> p i n", i=2)
                                      ).then_inc(s["qk_dve"], 1)
                    used(dve, P_QA)
                    V.tensor_scalar(qaT[:, 2:4, :], ps[:, 7, :].rearrange("p (i n) -> p i n", i=2), -(HD ** -0.5),
                                    None, ALU.mult).then_inc(s["qk_dve"], 1)
                    dve.wait_ge(s["hid_turned"], 1)
                    V.tensor_copy(hidT[:], ps[:, 2, 0:2 * NH].rearrange("p (m n) -> p m n", m=2)
                                  ).then_inc(s["hidT_ready"], 1)
                    dve.wait_ge(s["kc_ready"], 2)
                    for g in range(KVB):
                        for h in range(REP):
                            V.tensor_copy(vbd[h * CPAD:h * CPAD + NC, g, h * HD:(h + 1) * HD],
                                          ps[0:NC, 3, HD + g * HD:2 * HD + g * HD]).then_inc(s["vc_ready"], 1)
                    used(dve, P_VA)
                    V.tensor_copy(va[:, 1, :], ps[:, 1, :]).then_inc(s["va_dve"], 1)

                    def add_cost(j):
                        kind, h = HEADS[j]
                        tb = cost_a if kind == "a" else cost_b
                        dve.wait_ge(s["score"], j + 1)
                        if j >= BUF_S:
                            dve.wait_ge(s["expd"], 2 * (j - BUF_S + 1))
                        for t in range(TT):
                            lo, n = (0, P) if t == 0 else (P, SEQ)
                            V.tensor_tensor_reduce(cost[:, j % BUF_S, lo:lo + n], ps[:, 4 + j % BUF_S, lo:lo + n],
                                                   tb[:, h, SEQ - n:SEQ], 1.0, 3.0e38, ALU.add, ALU.min,
                                                   low[:, j, t:t + 1]).then_inc(s["costed"], 1)

                    def scale_weights(j):
                        kind, h = HEADS[j]
                        dve.wait_ge(s["expd"], 2 * (j + 1))
                        c.add(V.reciprocal(wgt[:, j, :], den[:, j, :]))
                        c.wait()
                        for t in range(TT):
                            lo, n = (0, P) if t == 0 else (P, SEQ)
                            br = 3 * h + (1 if kind == "s" else 2)
                            two = (None,) if kind == "a" else (gate[:, t, br:br + 1],)
                            ins = V.tensor_scalar(pr[:, j % BUF_W, lo:lo + n], pr[:, j % BUF_W, lo:lo + n], wgt[:, j, t:t + 1],
                                                  *two, *((ALU.mult,) if kind == "a" else (ALU.mult, ALU.mult)))
                        ins.then_inc(s["scaled"], 1)

                    def evac_out(m):
                        dve.wait_ge(s["summed"], WHOLE[m])
                        V.tensor_copy(hT[:, 2 * m:2 * m + 2, :], ps[:, m % 2, :].rearrange("p (i n) -> p i n", i=2)
                                      ).then_inc(s["oT_dve"], 1)

                    cost_c = tab[:, C_CC:C_CC + TT * HB * NC].rearrange("p (n c) -> p n c", c=NC)
                    valid_c = tab[:, C_CV:C_CV + TT * NC].rearrange("p (t c) -> p t c", t=TT)
                    for step in range(NHD + 1):
                        if step < NHD:
                            add_cost(step)
                        if step >= 1:
                            scale_weights(step - 1)
                        if step == 1:
                            dve.wait_ge(s["cscore"], 1)
                            c.add(V.tensor_tensor(cz[:], ps[:, 7, :].rearrange("p (n c) -> p n c", c=CPAD)[:, :, 0:NC],
                                                  cost_c, ALU.add))
                            c.wait()
                            c.add(V.tensor_reduce(clow, cz[:], AX.X, ALU.min))
                            c.wait()
                            V.tensor_tensor(cs[:], cz[:], clow.unsqueeze(2).to_broadcast([P, TT * HB, NC]),
                                            ALU.subtract).then_inc(s["cexp_in"], 1)
                        if step == 3:
                            dve.wait_ge(s["cexp"], 1)
                            c.add(V.tensor_reduce(cden, cs[:], AX.X, ALU.add))
                            for t in range(TT):
                                c.add(V.tensor_tensor(cz[:, t * HB:(t + 1) * HB, :], cs[:, t * HB:(t + 1) * HB, :],
                                                      valid_c[:, t, :].unsqueeze(1).to_broadcast([P, HB, NC]),
                                                      ALU.mult))
                            c.wait()
                            c.add(V.reciprocal(cw, cden))
                            c.wait()
                            dve.wait_ge(s["gate_dve"], 1)
                            gt = gate[:].rearrange("p t (h b) -> p t h b", b=3)[:, :, :, 0]
                            cwv = cw.rearrange("p (t h) -> p t h", t=TT)
                            c.add(V.tensor_tensor(cwv, cwv, gt, ALU.mult))
                            c.wait()
                            V.tensor_tensor(pc[:, :, :, 0:NC].rearrange("p t h c -> p (t h) c"), cz[:],
                                            cw.unsqueeze(2).to_broadcast([P, TT * HB, NC]), ALU.mult
                                            ).then_inc(s["cprob"], 1)
                        if step == 2 * WHOLE[0] + LAG + 1:
                            evac_out(0)
                        if step == 2 * WHOLE[2] + LAG + 1:
                            evac_out(2)
                    for n in range(4):
                        half, t = n // 2, n % 2
                        if t:
                            used(dve, P_WO0 + half)
                        else:
                            dve.wait_ge(s["wo_out"], half + 1)
                        xs = x[:, t, half * 512:(half + 1) * 512]
                        V.tensor_tensor(xs, xs, ps[:, 4 + n, :], ALU.add).then_inc(s["x_added"], 1)

                    dve.wait_ge(s["x_added"], 4)
                    norm(1)
                    evac_turned(1, 1)

                    def wide(v):
                        return v.unsqueeze(2).to_broadcast([P, TT, 4])

                    def do(ins):
                        c.add(ins)
                        c.wait()

                    dve.wait_ge(s["logitsT"], 1)
                    V.tensor_copy(lgT, ps[:, 4, 0:SEQ]).then_inc(s["logitsT_ready"], 1)
                    dve.wait_ge(s["routed"], 1)
                    lg = ps[:, 6, 0:TT * NR].rearrange("p (t n) -> p t n", t=TT)
                    glog = lg[:, :, 0:NG]
                    do(V.tensor_reduce(r_m, glog, AX.X, ALU.max))
                    do(V.tensor_tensor(r_e[:], glog, wide(r_m), ALU.is_equal))
                    V.tensor_tensor(r_x[:], glog, wide(r_m), ALU.subtract).then_inc(s["gexp_in"], 1)
                    for t in range(TT):
                        ins = V.tensor_tensor_reduce(r_w[:, t, :], r_e[:, t, :], tab[:, C_TIE:C_TIE + NG], 1.0, 0.0,
                                                     ALU.mult, ALU.max, r_wm[:, t:t + 1])
                    do(ins)
                    do(V.tensor_tensor(onehot[:], r_w[:], wide(r_wm), ALU.is_equal))
                    big = r_big.rearrange("p (t e g) -> p t e g", t=TT, e=EPG)
                    for t in range(TT):
                        ins = V.tensor_tensor(big[:, t, :, :],
                                              lg[:, t, NG:NR].rearrange("p (g e) -> p e g", g=NG),
                                              onehot[:, t, :].unsqueeze(1).to_broadcast([P, EPG, NG]), ALU.mult)
                    do(ins)
                    do(V.tensor_reduce(within[:], big, AX.X, ALU.add))
                    before = r_before.rearrange("p (t e g) -> p t e g", t=TT, e=EPG)
                    other = within[:].unsqueeze(2).to_broadcast([P, TT, EPG, EPG])
                    own = within[:].unsqueeze(3).to_broadcast([P, TT, EPG, EPG])
                    tri = (tab[:, C_TRI:C_TRI + 16].rearrange("p (e g) -> p e g", e=EPG).unsqueeze(1)
                           .to_broadcast([P, TT, EPG, EPG]))
                    do(V.tensor_tensor(big, other, own, ALU.is_equal))
                    V.tensor_tensor(before[:, :, :, EPG:2 * EPG], other, own, ALU.is_gt)
                    do(V.tensor_tensor(before[:, :, :, 0:EPG], big, tri, ALU.mult))
                    do(V.tensor_reduce(above[:], before, AX.X, ALU.add))
                    for t in range(TT):
                        ins = V.scalar_tensor_tensor(out=member[:, t, :].rearrange("p (g e) -> p g e", g=NG),
                                                     in0=above[:, t, :].unsqueeze(1).to_broadcast([P, NG, EPG]),
                                                     scalar=2.0,
                                                     in1=onehot[:, t, :].unsqueeze(2).to_broadcast([P, NG, EPG]),
                                                     op0=ALU.is_lt, op1=ALU.mult)
                    ins.then_inc(s["rank_in"], 1)
                    do(V.tensor_scalar(chosen[:], above[:], 2.0, None, ALU.is_lt))
                    do(V.tensor_reduce(top, within[:], AX.X, ALU.max))
                    V.tensor_tensor(ex[:], within[:], wide(top), ALU.subtract).then_inc(s["eexp_in"], 1)
                    dve.wait_ge(s["gexp"], 1)
                    do(V.tensor_reduce(gsum, r_x[:], AX.X, ALU.add))
                    do(V.reciprocal(gw, gsum))
                    dve.wait_ge(s["ranked"], 1)
                    do(V.scalar_tensor_tensor(out=slot_of[:],
                                              in0=ps[:, 5, 0:2 * NE].rearrange("p (t n) -> p t n", t=TT),
                                              scalar=1.0, in1=member[:], op0=ALU.add, op1=ALU.mult))

                    iota = tab[:, C_IOTA:C_IOTA + CAP]

                    def column(v, t, j, a):
                        return v[:, t, a:a + 1] if isinstance(j, int) and j == 0 else v[:, t, bass.ds(2 * j + a, 1)]

                    def make_pick(j):
                        for t in range(TT):
                            for a in range(2):
                                ins = V.tensor_scalar(pick[:, t, a * CAP:(a + 1) * CAP], iota,
                                                      column(slot_of, t, j, a), None, ALU.is_equal)
                        ins.then_inc(s["picked"], 1)

                    def make_pickw(j):
                        for t in range(TT):
                            for a in range(2):
                                ins = V.tensor_scalar(pickw[:, t, a * CAP:(a + 1) * CAP], iota,
                                                      column(slot_of, t, j, a), column(weight, t, j, a),
                                                      ALU.is_equal, ALU.mult)
                        ins.then_inc(s["pickw_ready"], 1)

                    def evac_gathered(n):
                        for b in range(2):
                            dve.wait_ge(s["gathered"], n + b)
                            V.tensor_tensor(xg[:, b * 4:b * 4 + 4, :],
                                            ps[:, 2 + b, :].rearrange("p (k n) -> p k n", k=4),
                                            gain(1, b * 4, 4).unsqueeze(2).to_broadcast([P, 4, P]),
                                            ALU.mult).then_inc(s["xg_ready"], 1)

                    def add_scattered(n0):
                        for n in range(4):
                            t, half = n % 2, n // 2
                            dve.wait_ge(s["scattered"], n0 + n)
                            xs = x[:, t, half * 512:(half + 1) * 512]
                            V.tensor_tensor(xs, xs, ps[:, (7, 2, 3, 4)[n], :], ALU.add).then_inc(s["added"], 1)

                    make_pick(0)
                    dve.wait_ge(s["counted"], 1)
                    do(V.tensor_reduce(most, ps[:, 6, 0:NE], AX.X, ALU.max))
                    V.tensor_copy(most_i[:], most).then_inc(s["route_done"], 1)
                    dve.wait_ge(s["eexp"], 1)
                    do(V.tensor_tensor(ex[:], ex[:], chosen[:], ALU.mult))
                    do(V.tensor_reduce(esum, ex[:], AX.X, ALU.add))
                    do(V.reciprocal(esum, esum))
                    do(V.scalar_tensor_tensor(out=esum, in0=esum, scalar=0.5, in1=gw, op0=ALU.mult, op1=ALU.mult))
                    do(V.tensor_tensor(ex[:], ex[:], wide(esum), ALU.mult))
                    for t in range(TT):
                        ins = V.tensor_tensor(weight[:, t, :].rearrange("p (g e) -> p g e", g=NG),
                                              onehot[:, t, :].unsqueeze(2).to_broadcast([P, NG, EPG]),
                                              ex[:, t, :].unsqueeze(1).to_broadcast([P, NG, EPG]), ALU.mult)
                    ins.then_inc(s["added"], 1)
                    dve.wait_ge(s["added"], 1)
                    make_pickw(0)
                    evac_gathered(1)
                    base = c.n

                    def activate_and_add(j, last=False):
                        cj = Chain(dve, s["chain_dve"], 0, base + j)
                        if not last:
                            make_pick(j + 1)
                        dve.wait_ge(s["th_ready"], j + 1)
                        cj.add(V.scalar_tensor_tensor(out=a1, in0=th, scalar=1.0, in1=ps[:, 0, :],
                                                      op0=ALU.add, op1=ALU.mult))
                        used(dve, ATT_PIECES + E_UP + 1, j)
                        cj.wait()
                        V.tensor_tensor(act_in, a1, ps[:, 1, :], ALU.mult).then_inc(s["act_ready"], 1)
                        if not last:
                            evac_gathered(2 * j + 3)
                        add_scattered(4 * j + 1)
                        used(dve, ATT_PIECES + E_DOWN + 1, j)
                        V.tensor_copy(y[:, 512:1024], ps[:, 6, :]).then_inc(s["y_dve"], 1)
                        if not last:
                            make_pickw(j + 1)

                    with dve.Fori(0, PAIRS - 1) as j:
                        activate_and_add(j)
                    activate_and_add(PAIRS - 1, last=True)
                    c.n += PAIRS
                    add_scattered(4 * PAIRS + 1)

                    dve.wait_ge(s["added"], 4 * PAIRS + 5)
                    with dve.If(dve.value_load(most_i[0:1, 0:1], min_val=0, max_val=SEQ) > CAP):
                        co = Chain(dve, s["over_l"])
                        co.add(V.tensor_scalar(over_w[:], slot_of[:], float(CAP), None, ALU.is_gt))
                        co.wait()
                        V.tensor_tensor(over_w[:], over_w[:], weight[:], ALU.mult).then_inc(s["over_x"], 1)
                        dve.wait_ge(s["over_x"], 1)
                        with dve.Fori(0, NG * EPG) as e:
                            ce = Chain(dve, s["over_l"], 0, co.n + FT * e)
                            for f in range(FT):
                                dve.wait_ge(s["over_t"], FT * e + f + 1)
                                ce.add(V.scalar_tensor_tensor(out=o_a1, in0=o_th, scalar=1.0, in1=ps[:, 0, 0:SEQ],
                                                              op0=ALU.add, op1=ALU.mult))
                                ce.wait()
                                dve.wait_ge(s["over_g"], 2 * FT * e + 2 * f + 2)
                                V.tensor_tensor(o_a2, o_a1, ps[:, 1, 0:SEQ], ALU.mult).then_inc(s["over_a"], 1)
                                dve.wait_ge(s["over_y"], FT * e + f + 1)
                                for t in range(TT):
                                    for half in range(2):
                                        xs = x[:, t, half * 512:(half + 1) * 512]
                                        ins = V.scalar_tensor_tensor(
                                            out=xs, in0=ps[:, 2 + 2 * t + half, :],
                                            scalar=over_w[:, t, bass.ds(e, 1)], in1=xs, op0=ALU.mult, op1=ALU.add)
                                ins.then_inc(s["over_x"], 1)
                        dve.wait_ge(s["over_x"], NG * EPG * FT + 1)
                    norm(2)
                    evac_turned(2, 2)
                    for n in range(4):
                        half, t = n // 2, n % 2
                        dve.wait_ge(s["ple_th"], n + 1)
                        dve.wait_ge(s["ple_q"], 4)
                        do(V.scalar_tensor_tensor(out=pv[:, n % 2, :], in0=pth[:, n % 2, :], scalar=1.0,
                                                  in1=ps[:, 4 + n, :], op0=ALU.add, op1=ALU.mult))
                        xs = x[:, t, half * 512:(half + 1) * 512]
                        V.scalar_tensor_tensor(out=xs, in0=pv[:, n % 2, :], scalar=0.5, in1=xs, op0=ALU.mult,
                                               op1=ALU.add).then_inc(s["ple_x"], 1)

            nc.sync.sem_clear(range(nums[0], nums[-1] + 1))
            nc.all_engine_barrier()

        with nc.Block() as block:
            @block.gpsimd
            def _(pool):
                pool.wait_ge(s["ms_ready"], 1)
                nc.gpsimd.tensor_tensor(rstd[:], sq[:], tab[:, C_POW:C_POW + TT], ALU.pow
                                        ).then_inc(s["rstd_ready"], 1)

            @block.scalar
            def _(act):
                nc.scalar.activation(xn[:, 1, :], x[:, 1, :], ACT.Square, accum_out=sq[:, 1:2]
                                     ).then_inc(s["sq_act"], 1)

            @block.vector
            def _(dve):
                V = nc.vector
                dve.wait_ge(fgain_sem, 16)
                c = Chain(dve, s["chain_dve"])
                c.add(V.tensor_tensor_reduce(xn[:, 0, :], x[:, 0, :], x[:, 0, :], 1.0, 0.0, ALU.mult, ALU.add,
                                             sq[:, 0:1]))
                c.wait()
                dve.wait_ge(s["sq_act"], 1)
                V.tensor_scalar(sq[:], sq[:], 1.0 / D, EPS, ALU.mult, ALU.add).then_inc(s["ms_ready"], 1)
                dve.wait_ge(s["rstd_ready"], 1)
                for t in range(TT):
                    V.scalar_tensor_tensor(out=xn[:, t, :], in0=x[:, t, :], scalar=rstd[:, t:t + 1], in1=fgain,
                                           op0=ALU.mult, op1=ALU.mult).then_inc(s["xn_dve"], 1)

            @block.sync
            def _(sp):
                o = out.rearrange("(t p) d -> p t d", p=P)
                for t in range(TT):
                    sp.wait_ge(s["xn_dve"], t + 1)
                    sp.dma_start(o[:, t, :], xn[:, t, :]).then_inc(out_sem, 16)
                sp.wait_ge(out_sem, 16 * TT)


def kernel(x, p, attn_norm, w_in, w_out, w_cmp_k1, w_cmp_k2, w_cmp_v1, w_cmp_v2, cmp_pos,
           ffn_norm, w_route_group, b_route_group, w_route_expert, b_route_expert,
           w_expert_gate, w_expert_up, w_expert_down, ple_norm, w_ple_gate, w_ple_proj, final_norm):
    import numpy as _np
    import concourse.bacc as _bacc
    from concourse import mybir as _mybir
    from concourse.bass_utils import run_bass_kernel_spmd as _run

    A = _np.asarray

    def columns(a):
        a = A(a)
        d, r, n = a.shape
        return a.reshape(d, r // P, P, n).transpose(0, 2, 1, 3).reshape(d, P, -1)

    bias = _np.zeros((DEPTH, P, TT, NR), _np.float32)
    bias[:, 0, :, :NG] = A(b_route_group)[:, None]
    bias[:, 0, :, NG:] = A(b_route_expert)[:, None]
    pos = A(cmp_pos).reshape(DEPTH, 2, CBLK // 2, 2, HD).transpose(0, 3, 4, 1, 2).reshape(DEPTH, P, -1)
    router = _np.zeros((DEPTH, D, 32), _np.float32)
    router[:, :, :NG] = A(w_route_group)
    router[:, :, NG:NR] = A(w_route_expert)
    small = _np.concatenate(
        [columns(A(g)[:, :, None]) for g in (attn_norm, ffn_norm, ple_norm)]
        + [pos, columns(w_cmp_k2), columns(w_cmp_v2), columns(router), bias.reshape(DEPTH, P, -1),
           columns(A(p)[:, 0].transpose(0, 2, 1))], axis=2)
    arrays = {
        "x_rows": A(x)[0], "small": small, "cost_parts": cost_parts(), "tables": tables(),
        "final_rows": _np.broadcast_to(A(final_norm)[None, :], (P, D)),
        "w_in": A(w_in), "w_out": A(w_out), "w_cmp_k1": A(w_cmp_k1), "w_cmp_v1": A(w_cmp_v1),
        "w_expert_gate": A(w_expert_gate), "w_expert_up": A(w_expert_up), "w_expert_down": A(w_expert_down),
        "w_ple_gate": A(w_ple_gate), "w_ple_proj": A(w_ple_proj),
    }
    arrays = {k: _np.ascontiguousarray(v) for k, v in arrays.items()}
    nc = _bacc.Bacc("TRN2", target_bir_lowering=False, num_devices=1)
    args = [nc.dram_tensor(k + "_dram", v.shape, _mybir.dt.from_np(v.dtype), kind="ExternalInput").ap()
            for k, v in arrays.items()]
    args.append(nc.dram_tensor("out_dram", (SEQ, D), _mybir.dt.float32, kind="ExternalOutput").ap())
    build_trunk(nc, *args)
    r = _run(nc, [{k + "_dram": v for k, v in arrays.items()}], core_ids=[0])
    return r.results[0]["out_dram"].reshape(1, SEQ, D)
```
